# Optimizing a Trainium2 kernel written in Bass

```python
import math
import jax, jax.numpy as jnp
from jax import lax
import numpy as np

D_MODEL = 1024
BATCH = 1
SEQ = 1024
DEPTH = 1

N_META = 16
D_MIX = D_MODEL
EPS = 1e-6
N_ATTN_HEADS = 8
ATTN_HEAD_DIM = 64
D_ATTN = N_ATTN_HEADS * ATTN_HEAD_DIM
Q_RANK = 256
KV_RANK = 128
N_IDX_HEADS = 4
IDX_DIM = 64
TOPK_MAX = 256
Q_BLOCK = 128
N_REL_BUCKETS = 32
REL_MAX_DIST = 128
N_GDN_HEADS = 4
GDN_HEAD_DIM = 128
D_GDN = N_GDN_HEADS * GDN_HEAD_DIM
CONV_WIDTH = 4
CHUNK = 64
IN_PROJ_SPLITS = (Q_RANK, KV_RANK, IDX_DIM, N_IDX_HEADS, D_ATTN, D_GDN, D_GDN, D_GDN, D_GDN, N_GDN_HEADS, N_GDN_HEADS)
D_IN_PROJ = Q_RANK + KV_RANK + IDX_DIM + N_IDX_HEADS + D_ATTN + 4 * D_GDN + 2 * N_GDN_HEADS

kernel_name = "hybrid_dsa_gdn_parallel_heads"

def _split_last(a, sizes):
    outs, start = [], 0
    for s in sizes:
        outs.append(a[..., start:start + s])
        start += s
    return outs

def _rms_norm(x, gain):
    xf = x.astype(jnp.float32)
    y = xf * lax.rsqrt(jnp.mean(xf * xf, axis=-1, keepdims=True) + EPS)
    return (y * gain.astype(jnp.float32)).astype(x.dtype)

def _l2_norm(x):
    return x * lax.rsqrt(jnp.sum(x * x, axis=-1, keepdims=True) + EPS)

def _pad_seq(a, before, after):
    widths = [(0, 0)] * a.ndim
    widths[1] = (before, after)
    return jnp.pad(a, widths)

def _t5_bucket(dist):
    n = jnp.maximum(dist, 0)
    max_exact = N_REL_BUCKETS // 2
    nf = jnp.maximum(n, 1).astype(jnp.float32)
    large = max_exact + (jnp.log(nf / max_exact) / math.log(REL_MAX_DIST / max_exact)
                         * (N_REL_BUCKETS - max_exact)).astype(jnp.int32)
    large = jnp.minimum(large, N_REL_BUCKETS - 1)
    return jnp.where(n < max_exact, n, large)

def _dsa_mixer(c_q, c_kv, k_idx, w_idx, g_cq, g_ckv, w_uq, w_ukv, w_q_idx, g_qn, g_kn, rel_table, topk):
    B, T, _ = c_q.shape
    cq = _rms_norm(c_q, g_cq)
    ckv = _rms_norm(c_kv, g_ckv)
    q = _rms_norm((cq @ w_uq).reshape(B, T, N_ATTN_HEADS, ATTN_HEAD_DIM), g_qn)
    k_lin, v = _split_last(ckv @ w_ukv, (D_ATTN, D_ATTN))
    k = _rms_norm(k_lin.reshape(B, T, N_ATTN_HEADS, ATTN_HEAD_DIM), g_kn)
    v = v.reshape(B, T, N_ATTN_HEADS, ATTN_HEAD_DIM)
    q_idx = (cq @ w_q_idx).reshape(B, T, N_IDX_HEADS, IDX_DIM)
    w_idx = w_idx * (N_IDX_HEADS ** -0.5)

    n_blk = -(-T // Q_BLOCK)
    Tp = n_blk * Q_BLOCK
    pad = Tp - T
    q_p, qi_p, wi_p = _pad_seq(q, 0, pad), _pad_seq(q_idx, 0, pad), _pad_seq(w_idx, 0, pad)
    k_p, v_p, ki_p = _pad_seq(k, 0, pad), _pad_seq(v, 0, pad), _pad_seq(k_idx, 0, pad)
    key_pos = jnp.arange(Tp, dtype=jnp.int32)
    scale = ATTN_HEAD_DIM ** -0.5

    def to_blocks(a):
        return jnp.moveaxis(a.reshape((B, n_blk, Q_BLOCK) + a.shape[2:]), 1, 0)

    def one_block(args):
        qb, qib, wb, t0 = args
        q_pos = t0 + jnp.arange(Q_BLOCK, dtype=jnp.int32)
        causal = key_pos[None, :] <= q_pos[:, None]
        idx_logits = jnp.einsum('bqhd,bsd->bqhs', qib, ki_p) * (IDX_DIM ** -0.5)
        idx_score = jnp.einsum('bqh,bqhs->bqs', wb, jax.nn.relu(idx_logits)).astype(jnp.float32)
        idx_score = jnp.where(causal[None], idx_score, -jnp.inf)
        _, sel = lax.top_k(idx_score, topk)
        valid = sel <= q_pos[None, :, None]
        kg = jax.vmap(lambda a, i: a[i])(k_p, sel)
        vg = jax.vmap(lambda a, i: a[i])(v_p, sel)
        bias = rel_table[_t5_bucket(q_pos[None, :, None] - sel)]
        logits = (jnp.einsum('bqhd,bqkhd->bqhk', qb, kg).astype(jnp.float32) * scale
                  + jnp.moveaxis(bias, -1, 2).astype(jnp.float32))
        logits = jnp.where(valid[:, :, None, :], logits, -jnp.inf)
        p = jax.nn.softmax(logits, axis=-1).astype(vg.dtype)
        return jnp.einsum('bqhk,bqkhd->bqhd', p, vg)

    t0s = jnp.arange(n_blk, dtype=jnp.int32) * Q_BLOCK
    out = lax.map(one_block, (to_blocks(q_p), to_blocks(qi_p), to_blocks(wi_p), t0s))
    return jnp.moveaxis(out, 0, 1).reshape(B, Tp, D_ATTN)[:, :T]

def _gdn_mixer(q, k, v, z, b, a, conv_w, a_log, dt_bias, g_out, n_front):
    B, T, _ = q.shape
    f32 = jnp.float32
    H, d = N_GDN_HEADS, GDN_HEAD_DIM
    qkv = jnp.concatenate([q, k, v], axis=-1).astype(f32)
    qkv = lax.conv_general_dilated(qkv, conv_w.astype(f32)[:, None, :], window_strides=(1,),
                                   padding=[(CONV_WIDTH - 1, 0)], dimension_numbers=('NWC', 'WIO', 'NWC'),
                                   feature_group_count=3 * D_GDN)
    qkv = jax.nn.silu(qkv)
    qc, kc, vc = _split_last(qkv, (D_GDN, D_GDN, D_GDN))
    qc = _l2_norm(qc.reshape(B, T, H, d)) * (d ** -0.5)
    kc = _l2_norm(kc.reshape(B, T, H, d))
    vc = vc.reshape(B, T, H, d)
    beta = jax.nn.sigmoid(b.astype(f32))
    g = -jnp.exp(a_log.astype(f32)) * jax.nn.softplus(a.astype(f32) + dt_bias.astype(f32))

    qc, kc, vc, beta, g = (_pad_seq(t, n_front, 0) for t in (qc, kc, vc, beta, g))
    Tc = T + n_front
    N = Tc // CHUNK

    def chunks4(t):
        return t.reshape(B, N, CHUNK, H, d).transpose(0, 3, 1, 2, 4)

    def chunks3(t):
        return t.reshape(B, N, CHUNK, H).transpose(0, 3, 1, 2)

    qc, kc, vc = chunks4(qc), chunks4(kc), chunks4(vc)
    beta, g = chunks3(beta), chunks3(g)
    decay = jnp.cumsum(g, axis=-1)
    tri = jnp.tril(jnp.ones((CHUNK, CHUNK), dtype=bool))
    strict = jnp.tril(jnp.ones((CHUNK, CHUNK), dtype=bool), -1)
    gamma = jnp.exp(jnp.where(tri, decay[..., :, None] - decay[..., None, :], -jnp.inf))
    kb = kc * beta[..., None]
    amat = jnp.eye(CHUNK, dtype=f32) + jnp.where(strict, jnp.einsum('bhncd,bhnsd->bhncs', kb, kc) * gamma, 0.0)
    u = lax.linalg.triangular_solve(amat, vc * beta[..., None], left_side=True, lower=True, unit_diagonal=True)
    w = lax.linalg.triangular_solve(amat, kb * jnp.exp(decay)[..., None], left_side=True, lower=True,
                                    unit_diagonal=True)
    aqk = jnp.where(tri, jnp.einsum('bhncd,bhnsd->bhncs', qc, kc) * gamma, 0.0)
    q_dec = qc * jnp.exp(decay)[..., None]
    k_dec = kc * jnp.exp(decay[..., -1:] - decay)[..., None]
    chunk_decay = jnp.exp(decay[..., -1])

    def step(S, xs):
        u_i, w_i, qd_i, kd_i, aqk_i, cd_i = xs
        v_new = u_i - jnp.einsum('bhcd,bhde->bhce', w_i, S)
        o = jnp.einsum('bhcd,bhde->bhce', qd_i, S) + jnp.einsum('bhcs,bhse->bhce', aqk_i, v_new)
        S = S * cd_i[..., None, None] + jnp.einsum('bhcd,bhce->bhde', kd_i, v_new)
        return S, o

    xs = tuple(jnp.moveaxis(t, 2, 0) for t in (u, w, q_dec, k_dec, aqk, chunk_decay))
    S0 = jnp.zeros((B, H, d, d), f32)
    _, o = lax.scan(step, S0, xs)
    o = o.transpose(1, 0, 3, 2, 4).reshape(B, Tc, H, d)[:, n_front:]
    o = _rms_norm(o, g_out) * jax.nn.silu(z.astype(f32).reshape(B, T, H, d))
    return o.reshape(B, T, D_GDN)

def _hybrid_layer(h, norm_gain, w_in, cq_norm_gain, ckv_norm_gain, w_uq, w_ukv, w_q_idx, q_norm_gain,
                  k_norm_gain, conv_w, a_log, dt_bias, gdn_norm_gain, w_out, rel_table, topk):
    hn = _rms_norm(h, norm_gain)
    proj = hn @ w_in
    (c_q, c_kv, k_idx, w_idx, z_attn, q_g, k_g, v_g, z_g, b_g, a_g) = _split_last(proj, IN_PROJ_SPLITS)
    o_attn = _dsa_mixer(c_q, c_kv, k_idx, w_idx, cq_norm_gain, ckv_norm_gain, w_uq, w_ukv, w_q_idx,
                        q_norm_gain, k_norm_gain, rel_table, topk) * jax.nn.silu(z_attn)
    o_gdn = _gdn_mixer(q_g, k_g, v_g, z_g, b_g, a_g, conv_w, a_log, dt_bias, gdn_norm_gain,
                       (-N_META) % CHUNK).astype(h.dtype)
    y = jnp.concatenate([o_attn.astype(h.dtype), o_gdn], axis=-1) @ w_out
    return h + y

def setup_inputs(seed: int = 0) -> dict:
    key = jax.random.key(seed)
    ks = jax.random.split(key, 20)
    nrm = jax.random.normal
    x = nrm(ks[0], (BATCH, SEQ, D_MODEL), jnp.float32)
    meta_tokens = nrm(ks[1], (N_META, D_MODEL), jnp.float32)
    rel_bias_table = 0.5 * nrm(ks[2], (N_REL_BUCKETS, N_ATTN_HEADS), jnp.float32)
    norm_gain = 1.0 + 0.02 * nrm(ks[3], (DEPTH, D_MODEL), jnp.float32)
    w_in = nrm(ks[4], (DEPTH, D_MODEL, D_IN_PROJ), jnp.float32) * D_MODEL ** -0.5
    cq_norm_gain = 1.0 + 0.02 * nrm(ks[5], (DEPTH, Q_RANK), jnp.float32)
    ckv_norm_gain = 1.0 + 0.02 * nrm(ks[6], (DEPTH, KV_RANK), jnp.float32)
    w_uq = nrm(ks[7], (DEPTH, Q_RANK, D_ATTN), jnp.float32) * Q_RANK ** -0.5
    w_ukv = nrm(ks[8], (DEPTH, KV_RANK, 2 * D_ATTN), jnp.float32) * KV_RANK ** -0.5
    w_q_idx = nrm(ks[9], (DEPTH, Q_RANK, N_IDX_HEADS * IDX_DIM), jnp.float32) * Q_RANK ** -0.5
    q_norm_gain = 1.0 + 0.02 * nrm(ks[10], (DEPTH, ATTN_HEAD_DIM), jnp.float32)
    k_norm_gain = 1.0 + 0.02 * nrm(ks[11], (DEPTH, ATTN_HEAD_DIM), jnp.float32)
    conv_w = nrm(ks[12], (DEPTH, CONV_WIDTH, 3 * D_GDN), jnp.float32) * CONV_WIDTH ** -0.5
    a_log = jnp.log(jax.random.uniform(ks[13], (DEPTH, N_GDN_HEADS), jnp.float32, minval=1.0, maxval=16.0))
    dt = jnp.exp(jax.random.uniform(ks[14], (DEPTH, N_GDN_HEADS), jnp.float32,
                                    minval=math.log(1e-3), maxval=math.log(1e-1)))
    dt_bias = dt + jnp.log(-jnp.expm1(-dt))
    gdn_norm_gain = 1.0 + 0.02 * nrm(ks[15], (DEPTH, GDN_HEAD_DIM), jnp.float32)
    w_out = nrm(ks[16], (DEPTH, D_MIX, D_MODEL), jnp.float32) * D_MIX ** -0.5
    return {"x": x, "meta_tokens": meta_tokens, "rel_bias_table": rel_bias_table, "norm_gain": norm_gain,
            "w_in": w_in, "cq_norm_gain": cq_norm_gain, "ckv_norm_gain": ckv_norm_gain, "w_uq": w_uq,
            "w_ukv": w_ukv, "w_q_idx": w_q_idx, "q_norm_gain": q_norm_gain, "k_norm_gain": k_norm_gain,
            "conv_w": conv_w, "a_log": a_log, "dt_bias": dt_bias, "gdn_norm_gain": gdn_norm_gain,
            "w_out": w_out}

def reference(x, meta_tokens, rel_bias_table, norm_gain, w_in, cq_norm_gain, ckv_norm_gain, w_uq, w_ukv,
              w_q_idx, q_norm_gain, k_norm_gain, conv_w, a_log, dt_bias, gdn_norm_gain, w_out):
    B, S, _ = x.shape
    topk = min(TOPK_MAX, S // 4)
    meta = jnp.broadcast_to(meta_tokens[None].astype(x.dtype), (B, N_META, D_MODEL))
    h = jnp.concatenate([meta, x], axis=1)
    for l in range(DEPTH):
        h = _hybrid_layer(h, norm_gain[l], w_in[l], cq_norm_gain[l], ckv_norm_gain[l], w_uq[l], w_ukv[l],
                          w_q_idx[l], q_norm_gain[l], k_norm_gain[l], conv_w[l], a_log[l], dt_bias[l],
                          gdn_norm_gain[l], w_out[l], rel_bias_table, topk)
    return h[:, N_META:]


_drawn_inputs = setup_inputs


def setup_inputs(seed=0):
    import zlib

    import numpy as np

    out = dict(_drawn_inputs(seed))
    spreads = {}
    factors = {'rel_bias_table': 3.254,
     'norm_gain': 4.288,
     'cq_norm_gain': 8.0,
     'ckv_norm_gain': 8.0,
     'q_norm_gain': 8.0,
     'k_norm_gain': 8.0,
     'gdn_norm_gain': 7.46}
    for name, (base, spread) in spreads.items():
        noise = np.random.default_rng([zlib.crc32(name.encode()), seed]).standard_normal(out[name].shape)
        drawn = base * np.exp(spread * noise) if base else spread * noise
        out[name] = __import__('jax').numpy.asarray(drawn.astype(out[name].dtype))
    for name, factor in factors.items():
        out[name] = (out[name] * factor).astype(out[name].dtype)
    return out
```

```python
import math
from contextlib import ExitStack

import concourse.bass as bass
import numpy as np
from concourse import mybir

F32 = mybir.dt.float32
BF16 = mybir.dt.bfloat16
I32 = mybir.dt.int32
ALU = mybir.AluOpType
ACT = mybir.ActivationFunctionType
AX = mybir.AxisListType

D, SEQ, META, EPS = 1024, 1024, 16, 1e-6
T = META + SEQ
HA, DA = 8, 64
HG, DG = 4, 128
HI = 4
TOPK = 256
CONV = 4
NB = SEQ // 128
NT = NB + 1
ROWS = [META] + [128] * NB
OFF = [0] + [META + 128 * i for i in range(NB)]
KEYS = [META + 128 * (i + 1) for i in range(NB)]
SC0 = [sum(KEYS[:i]) for i in range(NB + 1)]
KD = D // 128
NA = 460
CHUNKS = [(0, 272), (272, 656), (656, 1040)]
FILL = -1.0e30
LOWEST = -3.0e38
TOPBITS = 32
N_REL = 32
SKEW = 383


def rel_onehot():
    dist = np.arange(SKEW, dtype=np.int32)[::-1] - 127
    n = np.maximum(dist, 0)
    nf = np.maximum(n, 1).astype(np.float32)
    large = 16 + (np.log(nf / 16) / math.log(128 / 16) * 16).astype(np.int32)
    bucket = np.where(n < 16, n, np.minimum(large, 31))
    out = np.zeros((N_REL, SKEW), np.float32)
    out[bucket, np.arange(SKEW)] += 1.0
    out[N_REL - 1, :] -= 1.0
    return out


COMPACT = [2, 4, 8, 16]
FULL = [32, 64]


def gdn_levels(t):
    return ([2, 4, 8], []) if t == 0 else (COMPACT, FULL)


def pe_steps(t):
    comp, full = gdn_levels(t)
    s = ["kn", "vn", "kk", "rb"]
    for l in comp:
        s += [f"x{l}", f"y{l}"]
    for l in full:
        s += [f"x{l}", f"y{l}"]
    s += ["w", "v"]
    if t:
        s += ["o"]
    s += ["s"]
    if t:
        s += ["yt", "out"]
    return s


def dve_steps(t):
    comp, full = gdn_levels(t)
    s = ["kbe", "kdec", "bv", "ga", "gq", "at", "aq", "t0", "t1", "t2", "t3"]
    for l in [1] + comp:
        s += [f"tc{l}", f"ttc{l}"]
        if l == 16:
            s += ["tf16"]
        s += [f"ttf{l}"]
    for l in full:
        if l == 32:
            s += ["tf32"]
        s += [f"ttf{l}"]
    s += ["vnew"]
    s += ["s"] if t == 0 else ["s0", "s1", "s2", "s"]
    if t:
        s += ["y0", "y1", "y2", "y", "yt", "out"]
    return s


def act_steps(t):
    comp, full = gdn_levels(t)
    s = ["ga0", "ga1", "ga2", "ga3", "gq0", "gq1", "gq2", "gq3"]
    if t:
        s += ["eq"]
    s += [f"x{l}" for l in comp + full] + ["w"]
    if t:
        s += ["so0", "so1", "so2", "so3", "ln", "ro", "yt"]
    return s


def pool_steps(t):
    comp, full = gdn_levels(t)
    s = [f"m{l}" for l in comp + full]
    if t:
        s += ["qd", "zg"]
    return s


class Steps:

    def __init__(self, lists):
        self.value = {}
        for t, names in enumerate(lists):
            for name in names:
                self.value[t, name] = len(self.value) + 1

    def __call__(self, t, name):
        return self.value[t, name]


def hybrid(nc, x, meta, rel, norm_gain, w_in, g_cq, g_ckv, w_uq, w_ukv, w_qi, g_qn, g_kn, conv_w, a_log,
           dt_bias, g_gdn, w_out, onehot, out):
    ctx = ExitStack()
    with ctx:
        def sb(name, shape, dt=F32):
            return ctx.enter_context(nc.sbuf_tensor(name, shape, dt))

        def sem(name):
            return ctx.enter_context(nc.semaphore(name))

        areaH = sb("areaH", [128, KD * T])
        areaW = sb("areaW", [128, 2 * KD * 512])
        areaC = sb("areaC", [128, 12876])
        areaQ = sb("areaQ", [128, 4 * SEQ + 4 * T + NT * 512])
        scores = sb("scores", [128, SC0[NB]])
        tmp = sb("tmp", [128, 2 * T])
        zst = sb("zst", [128, 2, 512])
        junk = sb("junk", [128, T], BF16)

        class Area:
            def __init__(self, ap):
                self.ap, self.at = ap, 0

            def take(self, *shape):
                n = int(np.prod(shape))
                v = self.ap[:, self.at:self.at + n]
                self.at += n
                assert self.at <= self.ap.shape[1], (self.at, self.ap.shape)
                if len(shape) == 2:
                    v = v.rearrange("p (a b) -> p a b", a=shape[0])
                if len(shape) == 3:
                    v = v.rearrange("p (a b c) -> p a b c", a=shape[0], b=shape[1])
                return v

        hT = areaH[:, :].rearrange("p (k t) -> p k t", k=KD)
        wslot = areaW[:, :].rearrange("p (s k n) -> p s k n", s=2, k=KD)

        c = Area(areaC)
        xin = c.take(2, D)
        cn = c.take(2, 512)
        qkn = c.take(2, 1024)
        cT = c.take(3, T)
        kiT = c.take(T)
        wuq = c.take(2, 512)
        wukv = c.take(1024)
        wqi = c.take(2, 256)
        qiT = c.ap[:, 0:2 * SEQ].rearrange("p (m t) -> p m t", m=2)
        PADT = CONV - 1 + T
        conv = areaC[:, 0:12 * PADT].rearrange("p (m t) -> p m t", m=12)
        conv4 = areaC[:, 0:12 * PADT].rearrange("p (g h t) -> p g h t", g=3, h=4)

        a = Area(areaQ)
        qT, kT, vN = a.take(4, SEQ), a.take(4, T), a.take(NT, 512)

        a = Area(areaH)
        L = a.take(2, T)
        pT = a.take(2, NT, 128)
        bias = a.take(HA, 256)
        mbn = a.take(2, 256)
        zA = a.take(2, 512)
        oA = zst[:, 0, :]

        a = Area(areaQ)
        kbe, kdec, bv = a.take(HG, 128), a.take(HG, 128), a.take(HG, 128)
        ga, gq = a.take(HG, 128), a.take(HG, 128)
        AT, aq = a.take(HG, 128), a.take(HG, 128)
        ATm = {l: a.take(HG, 128) for l in COMPACT + FULL}
        TTf, Tf, Xf = a.take(HG, 128), a.take(HG, 128), a.take(HG, 128)
        TTc, Tc, Xc = a.take(HG, 32), a.take(HG, 32), a.take(HG, 32)
        wT, qd, vnew, S = a.take(HG, 128), a.take(HG, 128), a.take(HG, 128), a.take(HG, 128)
        lnb, gg, dec, tot = a.take(NT, 4), a.take(NT, 4), a.take(NT, 4), a.take(NT, 4)
        t1, t2 = a.take(NT, 8), a.take(NT, 8)
        rv1, rv2, cb = a.take(NT, 4), a.take(NT, 4), a.take(NT, 4)
        skbe, skd, beta, cd = a.take(NT, 4), a.take(NT, 4), a.take(NT, 4), a.take(NT, 4)
        so, ro = a.take(4), a.take(4)
        a = Area(areaH)
        zG = a.take(2, 512)
        ycat = a.take(2, D)
        yT = a.take(8, 128)
        xres = a.take(2, D)
        sqk = a.take(2, 8 * 128)
        a = Area(tmp)
        R = a.take(2, T)
        cum = tmp[:, 0:T]
        eqb = tmp[:, T:2 * T].bitcast(BF16)
        eq, drop = eqb[:, 0:T], eqb[:, T:2 * T]

        small = sb("small", [128, 1500])
        s = Area(small)
        ident, triu, ones = s.take(128), s.take(128), s.take(128)
        maskS, maskI = s.take(128), s.take(128)
        ic, negc1 = s.take(32), s.take(32)
        gain = s.take(KD)
        gc = s.take(3)
        gq8, gk = s.take(1), s.take(1)
        epst = s.take(1)
        epsn = s.take(1)
        cw = s.take(CONV, 12)
        alog, dtb = s.take(HG), s.take(HG)
        ggd = s.take(128)
        ss, rx = s.take(NT), s.take(NT)
        st, rc = s.take(2, 2), s.take(2, 2)
        ssk, rk = s.take(2, 16), s.take(2, 16)
        widx = s.take(NT, 4)
        ba = s.take(NT, 8)
        cnt, need = s.take(8), s.take(8)
        mx, nm = s.take(HA * NB, 2), s.take(HA * NB)
        rs = s.take(HA * NB)
        rinv = s.take(8)
        ssq = s.take(NT, 8)
        masks = sb("masks", [128, 7, 128], BF16)
        iw = sb("iw", [128, 6, 8], I32)
        bits, cand, flip, pat, hit = (iw[:, j, :] for j in range(5))
        patf = pat.bitcast(F32)
        relt = sb("relt", [N_REL, HA])
        oneh = zst[:, 0, 0:SKEW]
        rowst = zst[:, 1, 0:SKEW]

        ps = ctx.enter_context(nc.psum_tensor("ps", [128, 8, 512], F32))
        pf = ps[:, :, :].rearrange("p b n -> p (b n)")

        skew_d = nc.dram_tensor("skew_scratch", [HA, 128 * SKEW], F32).ap()
        za_d = nc.dram_tensor("gate_a_scratch", [SEQ, 512], F32).ap()
        zg_d = nc.dram_tensor("gate_g_scratch", [SEQ, 512], F32).ap()
        oa_d = nc.dram_tensor("attn_scratch", [SEQ, 512], F32).ap()

        s_par, s_small, s_const, s_dconst = sem("params_in"), sem("lat_weights_in"), sem("consts"), sem("dve_consts")
        s_w = [sem("w_in0"), sem("w_in1")]
        s_x = [sem("x_in0"), sem("x_in1")]
        s_rx, s_xn, s_xT, s_hn = sem("x_rstd"), sem("x_scaled"), sem("x_turned"), sem("hT_ready")
        s_al = sem("act_own")
        s_pA, s_rc, s_c1, s_cn, s_cT, s_ceD, s_ceA = (sem(n) for n in (
            "projA_done", "c_rstd", "c_copied", "c_scaled", "c_turned", "cT_ready", "kiT_ready"))
        s_kq, s_sq, s_ssk, s_rk, s_kqn, s_kqT, s_kTe, s_qTe, s_v = (sem(n) for n in (
            "kq_done", "kq_squared", "kq_sumsq", "kq_rstd", "kq_scaled", "kq_turned", "kT_ready", "qT_ready", "v_ready"))
        s_qi, s_qie, s_iq, s_relu, s_acc, s_caus = (sem(n) for n in (
            "qi_done", "qiT_ready", "index_dots", "index_relu", "index_scores", "scores_causal"))
        s_tk, s_tl, s_pen, s_mb = sem("topk_steps"), sem("topk_own"), sem("penalty"), sem("penalty_causal")
        s_rb, s_rbe, s_sk, s_skr, s_bias = (sem(n) for n in (
            "bias_rows", "bias_rows_out", "skew_written", "skew_last", "bias_in"))
        s_z, s_ze, s_zo = sem("z_done"), sem("z_ready"), [sem("z_out0"), sem("z_out1")]
        s_ch, s_che, s_pad, s_cv, s_cve, s_cvl = (sem(n) for n in (
            "chan_done", "chan_ready", "pads_zero", "conv_sum", "conv_ready", "conv_own"))
        s_grp = sem("group_done")
        s_S, s_red, s_far, s_nm, s_P, s_mbn, s_PT, s_PTe, s_o, s_on, s_or = (sem(n) for n in (
            "logits", "row_max", "row_max_far", "neg_max", "probs", "bias_mask", "probs_turned", "probsT_ready",
            "attn_out", "attn_gated", "attn_scaled"))
        s_meta = sem("meta_logits_read")
        s_PTa = sem("probsT_ready_act")
        s_za, s_oo = [sem("za_in0"), sem("za_in1")], sem("attn_stored")
        s_sqk, s_ssq, s_gd, s_ga, s_gp = (sem(n) for n in (
            "k_squared", "sumsq_dots", "gates_dve", "gates_act", "gates_pe"))
        g_pe, g_dve, g_act, g_pool = sem("gdn_pe"), sem("gdn_dve"), sem("gdn_act"), sem("gdn_pool")
        s_zg, s_yc, s_xr, s_out = ([sem(f"{n}{i}") for i in range(2)] for n in ("zg_in", "oa_in", "xres_in", "y_out"))
        s_outT = sem("final")
        PE, DV, AC, PO = (Steps([f(t) for t in range(NT)]) for f in (pe_steps, dve_steps, act_steps, pool_steps))
        N_CONST, N_DCONST, N_PAR = 22, 6, 16 * 15

        def tok(t):
            return slice(OFF[t], OFF[t] + ROWS[t])

        def per_head(ap, n, width=128, heads=HG):
            return ap.unsqueeze(2).broadcast_to([n, heads, width])

        def all_heads(ap, n, width=128, heads=HG):
            return ap.unsqueeze(1).broadcast_to([n, heads, width])

        def pieces(n):
            return [(j, min(j + 512, n)) for j in range(0, n, 512)]

        def split(i):
            return META if KEYS[i] > 1024 else 0

        def rounds(i):
            tiles = list(range(i + 2))
            return [tiles[j:j + 4] for j in range(0, len(tiles), 4)]

        sq2 = areaC[:, 12876 - 1024:12876]

        def copy_round(copy, n, rr, tiles):
            src = ps[:, 6 + rr % 2, :].rearrange("p (k t) -> p k t", k=4)
            if tiles[0] == 0:
                copy(pT[0:META, n % 2, 0, :], src[0:META, 0, :])
                return copy(pT[:, n % 2, 1:len(tiles), :], src[:, 1:len(tiles), :])
            return copy(pT[:, n % 2, tiles[0]:tiles[-1] + 1, :], src[:, 0:len(tiles), :])

        ROUND0 = [0]
        for i in range(NB):
            for h in range(HA):
                ROUND0.append(ROUND0[-1] + len(rounds(i)))

        def turned(r):
            return ((s_PTe, r // 2 + 1) if r % 2 == 0 else (s_PTa, r // 2 + 1))

        zc = 452
        GROUPS = [None, zc, zc + 2048, zc + 512, zc + 1024, zc + 1536, None, None]

        ctx.enter_context(nc.allow_non_contiguous_dma(reason="gains and conv taps, a few KB, go one to a partition"))
        block = ctx.enter_context(nc.Block())

        @block.sync
        def _(sp):
            x2 = x.rearrange("a s d -> (a s) d")

            def load_x(t):
                if t >= 2:
                    sp.wait_ge(s_xT, 2 * (t - 1))
                src = meta if t == 0 else x2[128 * (t - 1):128 * t, :]
                sp.dma_start(xin[0:ROWS[t], t % 2, :], src).then_inc(s_x[t % 2], 16)

            load_x(0)
            load_x(1)
            wv = w_in[0].rearrange("(k p) n -> p k n", p=128)
            for k in range(KD):
                sp.dma_start(wslot[:, 0, k, 0:452], wv[:, k, 0:452]).then_inc(s_w[0], 16)
                sp.dma_start(wslot[:, 0, k, 452:460], wv[:, k, 3012:3020]).then_inc(s_w[0], 16)
            for t in range(2, NT):
                load_x(t)
            sp.dma_start(wuq, w_uq[0].rearrange("(k p) n -> p k n", p=128)).then_inc(s_small, 16)
            sp.dma_start(wukv, w_ukv[0]).then_inc(s_small, 16)
            sp.dma_start(wqi, w_qi[0].rearrange("(k p) n -> p k n", p=128)).then_inc(s_small, 16)

            def load_group(g):
                if g >= 2:
                    sp.wait_ge(s_grp, g - 1)
                if g < 6:
                    src = wv[:, :, GROUPS[g]:GROUPS[g] + 512]
                else:
                    src = w_out[0].rearrange("(k p) n -> p k n", p=128)[:, :, 512 * (g - 6):512 * (g - 5)]
                sp.dma_start(wslot[:, g % 2, :, :], src).then_inc(s_w[g % 2], 16)

            load_group(1)
            sp.dma_start(oneh[0:N_REL], onehot).then_inc(s_skr, 16)
            for h in range(HA):
                sp.wait_ge(s_rbe, h + 1)
                sp.dma_start(skew_d[h].rearrange("(p m) -> p m", p=128), rowst).then_inc(s_sk, 16)
            load_group(2)

            def store_z(g, u):
                n = (g - 1) * NB + u
                sp.wait_ge(s_ze, n + 1)
                dst = (za_d if g == 1 else zg_d)[128 * u:128 * u + 128, :]
                sp.dma_start(dst, zst[:, n % 2, :]).then_inc(s_zo[n % 2], 16)

            for u in range(NB):
                store_z(1, u)
            load_group(3)
            for u in range(NB):
                store_z(2, u)
            for g in range(4, 8):
                load_group(g)
            sp.wait_ge(s_sk, 16 * HA)
            sp.wait_ge(s_grp, 6)
            for h in range(HA):
                src = skew_d[h, 127:127 + 128 * (SKEW - 1)].rearrange("(p m) -> p m", p=128)[:, 0:256]
                sp.dma_start(bias[:, h, :], src).then_inc(s_bias, 16)
            sp.wait_ge(s_zo[0], 16 * NB)
            sp.wait_ge(s_zo[1], 16 * NB)
            for i in range(NB):
                if i >= 2:
                    sp.wait_ge(s_on, i - 1)
                sp.dma_start(zA[:, i % 2, :], za_d[128 * i:128 * i + 128, :]).then_inc(s_za[i % 2], 16)
                if i:
                    sp.wait_ge(s_or, i)
                    sp.dma_start(oa_d[128 * (i - 1):128 * i, :], oA).then_inc(s_oo, 16)
            sp.wait_ge(s_or, NB)
            sp.dma_start(oa_d[128 * (NB - 1):128 * NB, :], oA).then_inc(s_oo, 16)
            sp.wait_ge(s_oo, 16 * NB)
            for t in range(1, NT):
                u = t - 1
                if u >= 2:
                    sp.wait_ge(g_pe, PE(t - 2, "yt"))
                    sp.wait_ge(g_dve, DV(t - 2, "out"))
                sp.dma_start(zG[:, u % 2, :], zg_d[128 * u:128 * u + 128, :]).then_inc(s_zg[u % 2], 16)
                sp.dma_start(ycat[:, u % 2, 0:512], oa_d[128 * u:128 * u + 128, :]).then_inc(s_yc[u % 2], 16)
                sp.dma_start(xres[:, u % 2, :], x2[128 * u:128 * u + 128, :]).then_inc(s_xr[u % 2], 16)
                if u:
                    sp.wait_ge(g_dve, DV(t - 1, "out"))
                    sp.dma_start(out[0, 128 * (u - 1):128 * u, :], xres[:, (u - 1) % 2, :]).then_inc(s_out[(u - 1) % 2], 16)
                    sp.wait_ge(s_out[(u - 1) % 2], 16 * ((u - 1) // 2 + 1))
            sp.wait_ge(g_dve, DV(NB, "out"))
            sp.dma_start(out[0, 128 * (NB - 1):, :], xres[:, (NB - 1) % 2, :]).then_inc(s_out[(NB - 1) % 2], 16)
            for q in s_out:
                sp.wait_ge(q, 16 * (NB // 2))

        @block.gpsimd
        def _(pool):
            par = [
                (gain, norm_gain[0].rearrange("(k p) -> p k", p=128)),
                (gc[:, 0:2], g_cq[0].rearrange("(k p) -> p k", p=128)),
                (gc[:, 2:3], g_ckv[0].rearrange("(k p) -> p k", p=128)),
                (gq8[0:64], g_qn[0].rearrange("(k p) -> p k", p=64)),
                (gq8[64:128], g_qn[0].rearrange("(k p) -> p k", p=64)),
                (gk[0:64], g_kn[0].rearrange("(k p) -> p k", p=64)),
                (gk[64:128], g_kn[0].rearrange("(k p) -> p k", p=64)),
                (alog, a_log[0].partition_broadcast(128)),
                (dtb, dt_bias[0].partition_broadcast(128)),
                (ggd, g_gdn[0].partition_broadcast(128)),
                (relt[:, :], rel),
            ] + [(cw[:, j, :], conv_w[0, j].rearrange("(m p) -> p m", p=128)) for j in range(CONV)]
            for dst, src in par[0:3]:
                pool.dma_start(dst, src).then_inc(s_par, 16)
            done = [0]

            def link(ins):
                done[0] += 1
                ins.then_inc(s_const, 1)
                pool.wait_ge(s_const, done[0])

            link(nc.gpsimd.memset(ones, 1.0))
            sel = nc.gpsimd.affine_select
            link(nc.gpsimd.memset(ident, 0.0))
            link(sel(out=ident, in_=ident, compare_op=ALU.not_equal, fill=1.0, base=0, pattern=[[-1, 128]],
                     channel_multiplier=1))
            for dst, src in par[3:]:
                pool.dma_start(dst, src).then_inc(s_par, 16)
            link(sel(out=triu, in_=ones, compare_op=ALU.is_ge, fill=0.0, base=0, pattern=[[1, 128]],
                     channel_multiplier=-1))
            link(nc.gpsimd.memset(maskS, 0.0))
            link(sel(out=maskI, in_=maskS, compare_op=ALU.is_ge, fill=FILL, base=0, pattern=[[1, 128]],
                     channel_multiplier=-1))
            link(sel(out=maskS, in_=maskS, compare_op=ALU.is_gt, fill=FILL, base=0, pattern=[[1, 128]],
                     channel_multiplier=-1))
            for n, l in enumerate(COMPACT + FULL):
                m = masks[:, n, :].rearrange("p (b f) -> p b f", f=2 * l)
                link(sel(out=m, in_=ones.rearrange("p (b f) -> p b f", f=2 * l), compare_op=ALU.is_ge, fill=0.0,
                         base=0, pattern=[[-2 * l, 128 // (2 * l)], [0, 2 * l]], channel_multiplier=1))
                link(sel(out=m, in_=m, compare_op=ALU.is_ge, fill=0.0, base=l - 1,
                         pattern=[[2 * l, 128 // (2 * l)], [0, 2 * l]], channel_multiplier=-1))
            m = masks[:, 6, :].rearrange("p (b f) -> p b f", f=32)
            link(sel(out=m, in_=ones.rearrange("p (b f) -> p b f", f=32), compare_op=ALU.is_ge, fill=0.0, base=0,
                     pattern=[[-32, 4], [0, 32]], channel_multiplier=1))
            link(sel(out=m, in_=m, compare_op=ALU.is_ge, fill=0.0, base=31, pattern=[[32, 4], [0, 32]],
                     channel_multiplier=-1))
            link(nc.gpsimd.memset(ssq, 1.0))
            assert done[0] == N_CONST, done
            for i in range(1, NB):
                sc = scores[:, SC0[i + 1] - 128:SC0[i + 1]]
                pool.wait_ge(s_acc, HI * i)
                sel(out=sc, in_=sc, compare_op=ALU.is_ge, fill=LOWEST, base=0, pattern=[[-1, 128]],
                    channel_multiplier=1).then_inc(s_caus, 1)
            for i in range(NB):
                sc = scores[:, SC0[i + 1] - 128:SC0[i + 1]]
                pool.wait_ge(s_pen, i + 1)
                sel(out=sc, in_=sc, compare_op=ALU.is_ge, fill=FILL, base=0, pattern=[[-1, 128]],
                    channel_multiplier=1).then_inc(s_mb, 1)
            pool.wait_ge(s_mb, NB)
            pool.wait_ge(s_bias, 16 * HA)
            for i in range(NB):
                near = 144 if i == 0 else 256
                for h in range(HA):
                    n = HA * i + h
                    if n >= 2:
                        pool.wait_ge(s_red, n - 1)
                    nc.gpsimd.tensor_tensor(mbn[:, n % 2, 0:near], scores[:, SC0[i + 1] - near:SC0[i + 1]],
                                            bias[:, h, 256 - near:256], ALU.add).then_inc(s_mbn, 1)
            pool.wait_ge(s_cve, 12)
            pool.wait_ge(s_or, NB)
            pool.wait_ge(s_oo, 16 * NB)
            for t in range(NT):
                n = ROWS[t]
                if t >= 2:
                    pool.wait_ge(s_ssq, t - 1)
                v = conv[:, 0:8, 3 + OFF[t]:3 + OFF[t] + n]
                o = sqk[:, t % 2, :].rearrange("p (m t) -> p m t", m=8)[:, :, 0:n]
                nc.gpsimd.tensor_tensor(o, v, v, ALU.mult).then_inc(s_sqk, 1)
            for t in range(NT):
                comp, full = gdn_levels(t)
                pool.wait_ge(g_dve, DV(t, "at"))
                for l in comp + full:
                    if t:
                        last = max(j for j in gdn_levels(t - 1)[0] + gdn_levels(t - 1)[1] if j <= l)
                        pool.wait_ge(g_pe, PE(t - 1, f"x{last}"))
                    nc.gpsimd.tensor_tensor(ATm[l], AT, all_heads(masks[:, (COMPACT + FULL).index(l), :], 128),
                                            ALU.mult).then_inc(g_pool, 1)
                if t:
                    u = t - 1
                    pool.wait_ge(g_act, AC(t, "eq"))
                    nc.gpsimd.tensor_tensor(qd, qd, conv[:, 0:4, 3 + OFF[t]:3 + OFF[t] + 128],
                                            ALU.mult).then_inc(g_pool, 1)
                    pool.wait_ge(s_zg[u % 2], 16 * (u // 2 + 1))
                    z4 = zG[:, u % 2, :].rearrange("p (h d) -> p h d", h=HG)
                    nc.gpsimd.tensor_tensor(z4, z4, all_heads(ggd, 128), ALU.mult).then_inc(g_pool, 1)

        @block.scalar
        def _(act):
            A = nc.scalar.activation
            own = [0]

            def link(ins):
                own[0] += 1
                ins.then_inc(s_al, 1)
                act.wait_ge(s_al, own[0])

            act.wait_ge(s_dconst, N_DCONST)
            def x_rstd(t):
                n = ROWS[t]
                act.wait_ge(s_x[t % 2], 16 * (t // 2 + 1))
                link(A(junk[0:n, 0:D], xin[0:n, t % 2, :], ACT.Square, accum_out=ss[0:n, t:t + 1]))
                link(A(rx[0:n, t:t + 1], ss[0:n, t:t + 1], ACT.Ln, scale=1.0 / D, bias=epst[0:n]))
                A(rx[0:n, t:t + 1], rx[0:n, t:t + 1], ACT.Exp, scale=-0.5).then_inc(s_rx, 1)

            def latents(t):
                n, b = ROWS[t], 4 + t % 2
                act.wait_ge(s_pA, t + 1)
                if t >= 2:
                    act.wait_ge(s_cT, t - 1)
                    act.wait_ge(s_cn, t - 1)
                A(junk[0:n, 0:256], ps[0:n, b, 0:256], ACT.Square, scale=1 / 16,
                  accum_out=st[0:n, t % 2, 0:1])
                link(A(junk[0:n, 256:384], ps[0:n, b, 256:384], ACT.Square, scale=128 ** -0.5,
                       accum_out=st[0:n, t % 2, 1:2]))
                nc.scalar.copy(cn[0:n, t % 2, 384:448], ps[0:n, b, 384:448])
                nc.scalar.copy(cn[0:n, t % 2, 448:512], ps[0:n, b, 384:448])
                nc.scalar.mul(widx[0:n, t, :], ps[0:n, b, 448:452], (HI * DA) ** -0.5)
                nc.scalar.copy(ba[0:n, t, :], ps[0:n, b, 452:460]).then_inc(s_c1, 1)
                link(A(rc[0:n, t % 2, :], st[0:n, t % 2, :], ACT.Ln, bias=epst[0:n]))
                A(rc[0:n, t % 2, :], rc[0:n, t % 2, :], ACT.Exp, scale=-0.5).then_inc(s_rc, 1)

            for t in range(NT + 3):
                if t < NT:
                    x_rstd(t)
                if 2 <= t < NT + 2:
                    latents(t - 2)
                if t >= 3:
                    act.wait_ge(s_cT, t - 2)
                    nc.scalar.copy(kiT[:, tok(t - 3)], ps[:, 6 + (t - 3) % 2, 384:384 + ROWS[t - 3]]).then_inc(s_ceA, 1)
            for t in range(NT):
                n, b = ROWS[t], 2 * (t % 2)
                kq = pf[0:n, 512 * b:512 * b + 1024]
                act.wait_ge(s_kq, t + 1)
                A(sq2[0:n], kq, ACT.Square, scale=1 / 8).then_inc(s_sq, 1)
                nc.scalar.copy(vN[0:n, t, :], ps[0:n, 4 + t % 2, :]).then_inc(s_v, 1)
                act.wait_ge(s_ssk, t + 1)
                link(A(rk[0:n, t % 2, :], ssk[0:n, t % 2, :], ACT.Ln, bias=epst[0:n]))
                A(rk[0:n, t % 2, :], rk[0:n, t % 2, :], ACT.Exp, scale=-0.5).then_inc(s_rk, 1)
                act.wait_ge(s_kqT, t + 1)
                A(kT[:, :, tok(t)], ps[:, 6, :].rearrange("p (h t) -> p h t", h=4)[:, :, 0:n], ACT.Copy,
                  scale=gk).then_inc(s_kTe, 1)
            for n in range(4):
                act.wait_ge(s_qi, n + 1)
                nc.scalar.copy(qiT[:, n // 2, 512 * (n % 2):512 * (n % 2) + 512], ps[:, 6 + n % 2, :]).then_inc(s_qie, 1)
            for n in range(HI * (NB - 1)):
                i = 1 + n // HI
                act.wait_ge(s_iq, n + 1)
                if n >= 2:
                    act.wait_ge(s_acc, n - 1)
                A(R[:, n % 2, 0:KEYS[i]], pf[:, 1536 * (n % 2):1536 * (n % 2) + KEYS[i]], ACT.Relu).then_inc(s_relu, 1)
            for h in range(HA):
                act.wait_ge(s_rb, h + 1)
                if h:
                    act.wait_ge(s_sk, 16 * h)
                nc.scalar.copy(rowst, ps[:, 6 + h % 2, 0:SKEW]).then_inc(s_rbe, 1)
            act.wait_ge(s_sk, 16 * HA)
            for n in range(2 * NB):
                act.wait_ge(s_z, n + 1)
                if n >= 2:
                    act.wait_ge(s_zo[n % 2], 16 * (n // 2))
                A(zst[:, n % 2, :], ps[:, n % 4, :], ACT.Silu).then_inc(s_ze, 1)
            for n in range(36):
                m, (lo, hi) = n // 3, CHUNKS[n % 3]
                act.wait_ge(s_ch, n + 1)
                nc.scalar.copy(conv[:, m, 3 + lo:3 + hi], ps[:, n % 4, 0:hi - lo]).then_inc(s_che, 1)
            for m in range(12):
                act.wait_ge(s_cv, CONV * (m + 1))
                A(conv[:, m, 3:], tmp[:, T * (m % 2):T * (m % 2) + T], ACT.Silu).then_inc(s_cve, 1)
            for m in range(HA * NB + 1):
                if m < HA * NB:
                    nk = KEYS[m // HA]
                    act.wait_ge(s_nm, m + 1)
                    A(L[:, m % 2, 0:nk], L[:, m % 2, 0:nk], ACT.Exp, bias=nm[:, m:m + 1],
                      accum_out=rs[:, m:m + 1]).then_inc(s_P, 1)
                if m:
                    n = m - 1
                    for r, tiles in enumerate(rounds(n // HA)):
                        rr = ROUND0[n] + r
                        if rr % 2:
                            act.wait_ge(s_PT, rr + 1)
                            if n >= 2:
                                act.wait_ge(s_o, n - 1)
                            copy_round(nc.scalar.copy, n, rr, tiles).then_inc(s_PTa, 1)
            g = [0]

            def glink(ins):
                g[0] += 1
                ins.then_inc(s_ga, 1)
                act.wait_ge(s_ga, g[0])

            act.wait_ge(s_gd, 5)
            glink(A(t1, t1, ACT.Exp, scale=-1.0))
            glink(A(t1, t1, ACT.Ln, bias=1.0))
            glink(A(alog, alog, ACT.Exp))
            act.wait_ge(s_gd, 9)
            glink(A(ssq, ssq, ACT.Ln, bias=epst))
            act.wait_ge(s_gd, 15)
            glink(A(skbe, rv1, ACT.Exp))
            glink(A(skd, t2[:, :, 0:4], ACT.Exp))
            glink(A(beta, lnb, ACT.Exp))
            glink(A(cd, tot, ACT.Exp))
            for t in range(NT):
                n = ROWS[t]
                comp, full = gdn_levels(t)
                for nm_, buf in (("ga", ga), ("gq", gq)):
                    act.wait_ge(g_dve, DV(t, nm_))
                    for h in range(HG):
                        A(buf[0:n, h, 0:n], buf[0:n, h, 0:n], ACT.Exp, bias=cb[0:n, t, h:h + 1]).then_inc(g_act, 1)
                if t:
                    act.wait_ge(g_pe, PE(t - 1, "o") if t > 1 else PE(t, "rb"))
                    act.wait_ge(g_pe, PE(t, "rb"))
                    A(qd, ps[:, 5, :].rearrange("p (h t) -> p h t", h=HG), ACT.Exp).then_inc(g_act, 1)
                for l in comp:
                    act.wait_ge(g_pe, PE(t, f"x{l}"))
                    nc.scalar.copy(Xc, ps[:, 0, 0:128].rearrange("p (h t) -> p h t", h=HG)).then_inc(g_act, 1)
                for l in full:
                    act.wait_ge(g_pe, PE(t, f"x{l}"))
                    nc.scalar.copy(Xf, ps[:, 0, :].rearrange("p (h t) -> p h t", h=HG)).then_inc(g_act, 1)
                act.wait_ge(g_pe, PE(t, "w"))
                nc.scalar.copy(wT[:, :, 0:n], ps[:, 3, :].rearrange("p (h t) -> p h t", h=HG)[:, :, 0:n]).then_inc(g_act, 1)
                if t:
                    act.wait_ge(g_pe, PE(t, "o"))
                    if t > 1:
                        act.wait_ge(g_dve, DV(t - 1, "y"))
                    for h in range(HG):
                        A(junk[:, 128 * h:128 * h + 128], ps[:, 7, 128 * h:128 * h + 128], ACT.Square, scale=DG ** -0.5,
                          accum_out=so[:, h:h + 1]).then_inc(g_act, 1)
                    act.wait_ge(g_act, AC(t, "so3"))
                    A(ro, so, ACT.Ln, bias=epst).then_inc(g_act, 1)
                    act.wait_ge(g_act, AC(t, "ln"))
                    A(ro, ro, ACT.Exp, scale=-0.5).then_inc(g_act, 1)
                    act.wait_ge(g_pe, PE(t, "yt"))
                    if t > 1:
                        act.wait_ge(g_pe, PE(t - 1, "out"))
                    nc.scalar.copy(yT[:, 0:4, :], ps[:, 4, :].rearrange("p (h t) -> p h t", h=4)).then_inc(g_act, 1)

        @block.vector
        def _(dve):
            V = nc.vector
            d = [0]

            def dlink(ins):
                d[0] += 1
                ins.then_inc(s_dconst, 1)
                dve.wait_ge(s_dconst, d[0])

            dlink(V.memset(epst, EPS))
            dlink(V.memset(epsn, EPS))
            dlink(V.memset(ba, 0.0))
            dlink(V.memset(junk[:, :], 0.0))
            dlink(V.memset(bits, 0))
            dlink(V.memset(cand, 0))
            def scale_x(t):
                n = ROWS[t]
                dve.wait_ge(s_rx, t + 1)
                V.tensor_scalar(xin[0:n, t % 2, :], xin[0:n, t % 2, :], rx[0:n, t:t + 1], None, ALU.mult).then_inc(s_xn, 1)

            def h_turned(t):
                n = ROWS[t]
                for b in range(2):
                    dve.wait_ge(s_xT, 2 * t + b + 1)
                    bank = ps[:, 2 * (t % 2) + b, :].rearrange("p (k t) -> p k t", k=4)[:, :, 0:n]
                    V.tensor_tensor(hT[:, 4 * b:4 * b + 4, tok(t)], bank, per_head(gain[:, 4 * b:4 * b + 4], 128, n, 4),
                                    ALU.mult).then_inc(s_hn, 1)

            def scale_c(t):
                n, b = ROWS[t], 4 + t % 2
                dve.wait_ge(s_rc, t + 1)
                if t >= 2:
                    dve.wait_ge(s_cT, t - 1)
                V.tensor_scalar(cn[0:n, t % 2, 0:256], ps[0:n, b, 0:256], rc[0:n, t % 2, 0:1], None, ALU.mult)
                V.tensor_scalar(cn[0:n, t % 2, 256:384], ps[0:n, b, 256:384], rc[0:n, t % 2, 1:2], None,
                                ALU.mult).then_inc(s_cn, 1)

            def c_turned(t):
                n = ROWS[t]
                dve.wait_ge(s_cT, t + 1)
                dve.wait_ge(s_ceA, t + 1)
                src = ps[:, 6 + t % 2, 0:384].rearrange("p (k t) -> p k t", k=3)[:, :, 0:n]
                V.tensor_tensor(cT[:, :, tok(t)], src, per_head(gc, 128, n, 3), ALU.mult).then_inc(s_ceD, 1)

            for t in range(NT + 3):
                if t < NT:
                    scale_x(t)
                if t == 1:
                    dve.wait_ge(s_par, N_PAR)
                if 1 <= t <= NT:
                    h_turned(t - 1)
                if 2 <= t < NT + 2:
                    scale_c(t - 2)
                if t >= 3:
                    c_turned(t - 3)
            V.tensor_scalar(gq8, gq8, DA ** -0.5, None, ALU.mult).then_inc(s_tl, 1)
            dve.wait_ge(s_tl, 1)
            for t in range(NT):
                n, b = ROWS[t], 2 * (t % 2)
                dve.wait_ge(s_sq, t + 1)
                if t >= 2:
                    dve.wait_ge(s_rk, t - 1)
                V.tensor_reduce(ssk[0:n, t % 2, :], sq2[0:n].rearrange("p (h d) -> p h d", h=16), AX.X,
                                ALU.add).then_inc(s_ssk, 1)
                dve.wait_ge(s_rk, t + 1)
                if t >= 2:
                    dve.wait_ge(s_kqT, t - 1)
                V.tensor_tensor(qkn[0:n, t % 2, :].rearrange("p (h d) -> p h d", h=16),
                                pf[0:n, 512 * b:512 * b + 1024].rearrange("p (h d) -> p h d", h=16),
                                per_head(rk[0:n, t % 2, :], n, DA, 16), ALU.mult).then_inc(s_kqn, 1)
                if t:
                    dve.wait_ge(s_kqT, t + 1)
                    V.tensor_scalar(qT[:, :, 128 * (t - 1):128 * t], ps[:, 7, :].rearrange("p (h t) -> p h t", h=4),
                                    gq8, None, ALU.mult).then_inc(s_qTe, 1)
            for n in range(HI * (NB - 1)):
                i, h = 1 + n // HI, n % HI
                sc = scores[:, SC0[i]:SC0[i] + KEYS[i]]
                dve.wait_ge(s_relu, n + 1)
                if h == 0:
                    V.tensor_scalar(sc, R[:, n % 2, 0:KEYS[i]], widx[:, i + 1, h:h + 1], None,
                                    ALU.mult).then_inc(s_acc, 1)
                else:
                    dve.wait_ge(s_acc, n)
                    V.scalar_tensor_tensor(sc, R[:, n % 2, 0:KEYS[i]], widx[:, i + 1, h:h + 1], sc, ALU.mult,
                                           ALU.add).then_inc(s_acc, 1)
            NI = NB - 1
            dve.wait_ge(s_caus, NI)
            base = 1
            U, B = iw[:, 5, 0:NI], bits[:, 0:NI]
            V.memset(U, 0).then_inc(s_tl, 1)
            V.memset(B, -2 ** 31).then_inc(s_tl, 1)
            dve.wait_ge(s_tl, base + 2)
            PER = 6 + NI
            with dve.Fori(0, TOPBITS) as it:
                cd_, fl, pt, ht = (v[:, 0:NI] for v in (cand, flip, pat, hit))
                V.tensor_tensor(cd_, U, B, ALU.bitwise_or).then_inc(s_tk, 1)
                dve.wait_ge(s_tk, it * PER + 1)
                V.tensor_scalar(fl, cd_, 31, -1, ALU.arith_shift_right, ALU.bitwise_xor).then_inc(s_tk, 1)
                dve.wait_ge(s_tk, it * PER + 2)
                V.scalar_tensor_tensor(pt, fl, -2 ** 31, cd_, ALU.bitwise_or, ALU.bitwise_xor).then_inc(s_tk, 1)
                dve.wait_ge(s_tk, it * PER + 3)
                for i in range(1, NB):
                    V.tensor_scalar(junk[:, 0:KEYS[i]], scores[:, SC0[i]:SC0[i] + KEYS[i]],
                                    patf[:, i - 1:i], 0.0, ALU.is_ge, ALU.add,
                                    accum_out=cnt[:, i - 1:i]).then_inc(s_tk, 1)
                    dve.wait_ge(s_tk, it * PER + 3 + i)
                V.tensor_scalar(ht, cnt[:, 0:NI], float(TOPK), -1.0, ALU.is_ge, ALU.mult).then_inc(s_tk, 1)
                V.tensor_scalar(B, B, 1, None, ALU.logical_shift_right)
                dve.wait_ge(s_tk, it * PER + 4 + NI)
                V.tensor_tensor(ht, ht, cd_, ALU.bitwise_and).then_inc(s_tk, 1)
                dve.wait_ge(s_tk, it * PER + 5 + NI)
                V.tensor_tensor(U, U, ht, ALU.bitwise_or).then_inc(s_tk, 1)
                dve.wait_ge(s_tk, it * PER + 6 + NI)
            V.tensor_scalar(flip[:, 0:NI], U, 31, -1, ALU.arith_shift_right, ALU.bitwise_xor).then_inc(s_tl, 1)
            dve.wait_ge(s_tl, base + 3)
            V.scalar_tensor_tensor(pat[:, 0:NI], flip[:, 0:NI], -2 ** 31, U, ALU.bitwise_or,
                                   ALU.bitwise_xor).then_inc(s_tl, 1)
            dve.wait_ge(s_tl, base + 4)
            for i in range(1, NB):
                V.tensor_scalar(junk[:, 0:KEYS[i]], scores[:, SC0[i]:SC0[i] + KEYS[i]], patf[:, i - 1:i], 0.0,
                                ALU.is_gt, ALU.add, accum_out=cnt[:, i - 1:i]).then_inc(s_tl, 1)
                dve.wait_ge(s_tl, base + 4 + i)
            base += NI - 1
            V.tensor_scalar(need[:, 0:NI], cnt[:, 0:NI], -1.0, float(TOPK), ALU.mult, ALU.add).then_inc(s_tl, 1)
            V.memset(scores[:, 0:KEYS[0]], 0.0).then_inc(s_pen, 1)
            dve.wait_ge(s_tl, base + 6)
            k = base + 6
            for i in range(1, NB):
                sc, thr, nk = scores[:, SC0[i]:SC0[i] + KEYS[i]], patf[:, i - 1:i], KEYS[i]
                V.tensor_scalar(eq[:, 0:nk], sc, thr, None, ALU.is_equal).then_inc(s_tl, 1)
                dve.wait_ge(s_tl, k + 1)
                V.tensor_tensor_scan(cum[:, 0:nk], eq[:, 0:nk], junk[:, 0:nk], 0.0, ALU.add,
                                     ALU.bypass).then_inc(s_tl, 1)
                dve.wait_ge(s_tl, k + 2)
                V.scalar_tensor_tensor(drop[:, 0:nk], cum[:, 0:nk], need[:, i - 1:i], eq[:, 0:nk], ALU.is_gt,
                                       ALU.mult).then_inc(s_tl, 1)
                dve.wait_ge(s_tl, k + 3)
                V.scalar_tensor_tensor(sc, sc, thr, drop[:, 0:nk], ALU.is_ge, ALU.subtract).then_inc(s_tl, 1)
                dve.wait_ge(s_tl, k + 4)
                k += 4
                V.tensor_scalar(sc, sc, -1.0, -FILL, ALU.add, ALU.mult).then_inc(s_pen, 1)
            dve.wait_ge(s_qie, 4)
            dve.wait_ge(s_che, 1)
            V.memset(conv[:, :, 0:3], 0.0).then_inc(s_pad, 1)
            dve.wait_ge(s_pad, 1)
            for m in range(12):
                dve.wait_ge(s_che, 3 * (m + 1))
                acc = tmp[:, T * (m % 2):T * (m % 2) + T]
                if m >= 2:
                    dve.wait_ge(s_cve, m - 1)
                for j in range(CONV):
                    if j == 0:
                        V.tensor_scalar(acc, conv[:, m, 0:T], cw[:, 0, m:m + 1], None, ALU.mult).then_inc(s_cv, 1)
                    else:
                        dve.wait_ge(s_cv, CONV * m + j)
                        V.scalar_tensor_tensor(acc, conv[:, m, j:j + T], cw[:, j, m:m + 1], acc, ALU.mult,
                                               ALU.add).then_inc(s_cv, 1)
            dve.wait_ge(s_grp, 6)
            dve.wait_ge(s_mb, NB)
            def logits(n):
                i, h = n // HA, n % HA
                near = 144 if i == 0 else 256
                far = KEYS[i] - near
                lg = pf[:, 1536 * (n % 2):1536 * (n % 2) + KEYS[i]]
                dve.wait_ge(s_S, n + 1)
                if n >= 2:
                    dve.wait_ge(s_PT, ROUND0[n - 1])
                first, lo0 = LOWEST, split(i)
                if lo0:
                    V.tensor_tensor_reduce(L[:, n % 2, 0:lo0], ps[:, 2, 0:lo0], scores[:, SC0[i]:SC0[i] + lo0],
                                           1.0, first, ALU.add, ALU.max, mx[:, n, 1:2]).then_inc(s_meta, 1)
                    dve.wait_ge(s_meta, h + 1)
                    first = mx[:, n, 1:2]
                if far:
                    V.tensor_tensor_reduce(L[:, n % 2, lo0:far], lg[:, 0:far - lo0],
                                           scores[:, SC0[i] + lo0:SC0[i] + far],
                                           1.0, first, ALU.add, ALU.max, mx[:, n, 0:1]).then_inc(s_far, 1)
                    dve.wait_ge(s_far, n + 1 - HA)
                    first = mx[:, n, 0:1]
                dve.wait_ge(s_mbn, n + 1)
                V.tensor_tensor_reduce(L[:, n % 2, far:KEYS[i]], lg[:, far - lo0:KEYS[i] - lo0], mbn[:, n % 2, 0:near],
                                       1.0, first, ALU.add, ALU.max, mx[:, n, 1:2]).then_inc(s_red, 1)
                dve.wait_ge(s_red, n + 1)
                V.tensor_scalar(nm[:, n:n + 1], mx[:, n, 1:2], -1.0, None, ALU.mult).then_inc(s_nm, 1)

            def copy_even_rounds(n):
                for r, tiles in enumerate(rounds(n // HA)):
                    rr = ROUND0[n] + r
                    if rr % 2 == 0:
                        dve.wait_ge(s_PT, rr + 1)
                        if n >= 2:
                            dve.wait_ge(s_o, n - 1)
                        copy_round(V.tensor_copy, n, rr, tiles).then_inc(s_PTe, 1)

            def gate_block(i):
                dve.wait_ge(s_P, HA * (i + 1))
                V.reciprocal(rinv, rs[:, HA * i:HA * i + HA])
                dve.wait_ge(s_o, HA * (i + 1))
                dve.wait_ge(s_za[i % 2], 16 * (i // 2 + 1))
                if i:
                    dve.wait_ge(s_oo, 16 * i)
                V.tensor_tensor(oA, ps[:, 5, :], zA[:, i % 2, :], ALU.mult).then_inc(s_on, 1)
                dve.wait_ge(s_on, i + 1)
                o3 = oA.rearrange("p (h d) -> p h d", h=HA)
                V.tensor_tensor(o3, o3, per_head(rinv, 128, DA, HA), ALU.mult).then_inc(s_or, 1)
                dve.wait_ge(s_or, i + 1)

            for m in range(HA * NB + 2):
                if m < HA * NB:
                    logits(m)
                if 1 <= m <= HA * NB:
                    copy_even_rounds(m - 1)
                if m >= 2 and (m - 2) % HA == HA - 1:
                    gate_block((m - 2) // HA)
            g = [0]

            def glink(ins):
                g[0] += 1
                ins.then_inc(s_gd, 1)
                dve.wait_ge(s_gd, g[0])

            dve.wait_ge(s_c1, NT)
            glink(V.tensor_tensor(t2[:, :, 4:8], ba[:, :, 4:8], all_heads(dtb, 128, 4, NT), ALU.add))
            glink(V.tensor_scalar(t2[:, :, 0:4], ba[:, :, 0:4], -1.0, None, ALU.mult))
            glink(V.tensor_scalar(t1, t2, -1.0, None, ALU.mult))
            glink(V.tensor_tensor(t1, t1, t2, ALU.max))
            glink(V.tensor_scalar(t2, t2, 0.0, None, ALU.max))
            dve.wait_ge(s_ga, 3)
            glink(V.tensor_tensor(t1, t1, t2, ALU.add))
            glink(V.tensor_scalar(lnb, t1[:, :, 0:4], -1.0, None, ALU.mult))
            dve.wait_ge(s_ssq, NT)
            V.tensor_copy(ssq[0:META, 0, :], ps[0:META, 0, 0:8])
            glink(V.tensor_copy(ssq[:, 1:, :], ps[:, 0, 8:8 * NT].rearrange("p (t c) -> p t c", c=8)))
            glink(V.scalar_tensor_tensor(gg, t1[:, :, 4:8], -1.0, all_heads(alog, 128, 4, NT), ALU.mult, ALU.mult))
            dve.wait_ge(s_gp, 1)
            p1 = ps[:, 1, 0:8 * NT].rearrange("p (c t h) -> p c t h", c=2, h=4)
            V.tensor_copy(dec, p1[:, 0])
            glink(V.tensor_copy(tot, p1[:, 1]))
            dve.wait_ge(s_ga, 4)
            glink(V.scalar_tensor_tensor(rv1, ssq[:, :, 4:8], -0.5, dec, ALU.mult, ALU.add))
            glink(V.tensor_tensor(rv1, rv1, lnb, ALU.add))
            V.scalar_tensor_tensor(rv2, ssq[:, :, 0:4], -0.5, dec, ALU.mult, ALU.add)
            glink(V.scalar_tensor_tensor(cb, ssq[:, :, 4:8], -0.5, dec, ALU.mult, ALU.subtract))
            glink(V.tensor_scalar(rv2, rv2, -0.5 * math.log(DG), None, ALU.add))
            glink(V.tensor_tensor(t2[:, :, 0:4], cb, tot, ALU.add))
            dve.wait_ge(s_ga, 8)
            glink(V.tensor_scalar(skbe, skbe, -1.0, None, ALU.mult))
            glink(V.memset(AT, 0.0))
            glink(V.memset(ic, 0.0))
            for b in range(4):
                rows = slice(32 * b, 32 * b + 32)
                glink(V.tensor_copy(ic[rows], ident[rows, 32 * b:32 * b + 32]))
            for n, l in enumerate(COMPACT + FULL):
                m = masks[:, n, :].rearrange("p (b c f) -> p b c f", c=2, f=l)
                glink(V.memset(m[:, :, 0, :], 0.0))
            glink(V.memset(negc1, 0.0))
            glink(V.tensor_scalar(negc1.rearrange("p (b c) -> p b c", c=2)[:, :, 1],
                                  ic.rearrange("p (b c) -> p b c", c=2)[:, :, 0], -1.0, None, ALU.mult))
            for t in range(NT):
                n = ROWS[t]
                comp, full = gdn_levels(t)

                def bank(b, k=4):
                    return ps[:, b, :].rearrange("p (h t) -> p h t", h=k)

                def step(ins, name=None):
                    ins.then_inc(g_dve, 1)
                    if name:
                        dve.wait_ge(g_dve, DV(t, name))

                dve.wait_ge(g_pe, PE(t, "kn"))
                if t:
                    dve.wait_ge(g_pe, PE(t - 1, "s"))
                step(V.tensor_tensor(kbe[0:n], bank(0)[0:n], per_head(skbe[0:n, t], n), ALU.mult))
                step(V.tensor_tensor(kdec[0:n], bank(0)[0:n], per_head(skd[0:n, t], n), ALU.mult))
                dve.wait_ge(g_pe, PE(t, "vn"))
                step(V.tensor_tensor(bv[0:n], bank(1)[0:n], per_head(beta[0:n, t], n), ALU.mult))
                dve.wait_ge(g_pe, PE(t, "rb"))
                step(V.tensor_tensor(ga[0:n, :, 0:n], bank(4)[0:n, :, 0:n], all_heads(maskS[0:n, 0:n], n, n), ALU.add))
                step(V.tensor_tensor(gq[0:n, :, 0:n], bank(5)[0:n, :, 0:n], all_heads(maskI[0:n, 0:n], n, n), ALU.add))
                kk = pf[0:n, 1024:2048].rearrange("p (h g t) -> p h g t", h=HG, g=2)
                dve.wait_ge(g_pe, PE(t, "kk"))
                dve.wait_ge(g_act, AC(t, "ga3"))
                if t:
                    dve.wait_ge(g_pool, PO(t - 1, f"m{8 if t == 1 else 64}"))
                step(V.tensor_tensor(AT[0:n, :, 0:n], kk[:, :, 1, 0:n], ga[0:n, :, 0:n], ALU.mult), "at")
                dve.wait_ge(g_act, AC(t, "gq3"))
                step(V.tensor_tensor(aq[0:n, :, 0:n], kk[:, :, 0, 0:n], gq[0:n, :, 0:n], ALU.mult))
                for b in range(4):
                    rows = slice(32 * b, 32 * b + 32)
                    step(V.tensor_tensor(TTc[rows], AT[rows, :, 32 * b:32 * b + 32],
                                         all_heads(negc1[rows], 32, 32), ALU.mult), f"t{b}")
                step(V.tensor_tensor(TTc, TTc, all_heads(ic, 128, 32), ALU.add), "tc1")
                step(V.transpose(Tc.rearrange("p h t -> p (h t)"), TTc.rearrange("p h t -> p (h t)")), "ttc1")

                def spread(dst, src):
                    return V.tensor_tensor(dst.rearrange("p h (b t) -> p h b t", b=4),
                                           src.unsqueeze(2).broadcast_to([128, HG, 4, 32]),
                                           bd32, ALU.mult)

                bd32 = masks[:, 6, :].rearrange("p (b t) -> p b t", b=4).unsqueeze(1).broadcast_to([128, HG, 4, 32])
                step(spread(TTf, TTc), "ttf1")
                for l in comp:
                    dve.wait_ge(g_pe, PE(t, f"y{l}"))
                    step(V.tensor_tensor(Tc, Tc, ps[:, 1, 0:128].rearrange("p (h t) -> p h t", h=HG), ALU.subtract),
                         f"tc{l}")
                    step(V.transpose(TTc.rearrange("p h t -> p (h t)"), Tc.rearrange("p h t -> p (h t)")), f"ttc{l}")
                    if l == 16:
                        step(spread(Tf, Tc))
                    step(spread(TTf, TTc), f"ttf{l}")
                for l in full:
                    dve.wait_ge(g_pe, PE(t, f"y{l}"))
                    if l == 32:
                        step(V.tensor_tensor(Tf, Tf, bank(1), ALU.subtract))
                    step(V.tensor_tensor(TTf, TTf, bank(2), ALU.subtract), f"ttf{l}")
                dve.wait_ge(g_pe, PE(t, "v"))
                step(V.tensor_copy(vnew[0:n], bank(6)[0:n]))
                dve.wait_ge(g_pe, PE(t, "s"))
                if t == 0:
                    step(V.tensor_copy(S, bank(1)))
                else:
                    for h in range(HG):
                        step(V.scalar_tensor_tensor(S[:, h, :], S[:, h, :], cd[:, t, h:h + 1], bank(1)[:, h, :],
                                                    ALU.mult, ALU.add))
                    u = t - 1
                    dve.wait_ge(g_act, AC(t, "ro"))
                    dve.wait_ge(g_pool, PO(t, "zg"))
                    if u >= 2:
                        dve.wait_ge(g_pe, PE(t - 2, "yt"))
                    for h in range(HG):
                        step(V.scalar_tensor_tensor(ycat[:, u % 2, 512 + 128 * h:640 + 128 * h], bank(7)[:, h, :],
                                                    ro[:, h:h + 1], zG[:, u % 2, 128 * h:128 * h + 128], ALU.mult,
                                                    ALU.mult))
                    dve.wait_ge(g_pe, PE(t, "yt"))
                    if t > 1:
                        dve.wait_ge(g_pe, PE(t - 1, "out"))
                    step(V.tensor_copy(yT[:, 4:8, :], bank(5)))
                    dve.wait_ge(g_pe, PE(t, "out"))
                    dve.wait_ge(s_xr[u % 2], 16 * (u // 2 + 1))
                    step(V.tensor_tensor(xres[:, u % 2, :], pf[:, 1024:2048], xres[:, u % 2, :], ALU.add))

        @block.tensor
        def _(pe):
            mm, turn = nc.tensor.matmul, nc.tensor.transpose
            pe.wait_ge(s_const, N_CONST)

            def turn_x(t):
                n = ROWS[t]
                pe.wait_ge(s_xn, t + 1)
                for b in range(2):
                    if t >= 2:
                        pe.wait_ge(s_hn, 2 * (t - 2) + b + 1)
                    for k in range(4):
                        ins = turn(ps[:, 2 * (t % 2) + b, 128 * k:128 * k + n],
                                   xin[0:n, t % 2, 128 * (4 * b + k):128 * (4 * b + k + 1)], ident[0:n, 0:n])
                    ins.then_inc(s_xT, 1)

            def proj_a(t):
                n, b = ROWS[t], 4 + t % 2
                pe.wait_ge(s_hn, 2 * (t + 1))
                if t == 0:
                    pe.wait_ge(s_w[0], 16 * 2 * KD)
                if t >= 2:
                    pe.wait_ge(s_c1, t - 1)
                    pe.wait_ge(s_cn, t - 1)
                for k in range(KD):
                    ins = mm(ps[0:n, b, 0:NA], hT[:, k, tok(t)], wslot[:, 0, k, 0:NA], start=k == 0, stop=k == KD - 1)
                ins.then_inc(s_pA, 1)

            def turn_c(t):
                n = ROWS[t]
                pe.wait_ge(s_cn, t + 1)
                pe.wait_ge(s_c1, t + 1)
                if t >= 2:
                    pe.wait_ge(s_ceD, t - 1)
                    pe.wait_ge(s_ceA, t - 1)
                for k in range(4):
                    ins = turn(ps[:, 6 + t % 2, 128 * k:128 * k + n], cn[0:n, t % 2, 128 * k:128 * k + 128],
                               ident[0:n, 0:n])
                ins.then_inc(s_cT, 1)

            for t in range(NT + 2):
                if t < NT:
                    turn_x(t)
                if 1 <= t <= NT:
                    proj_a(t - 1)
                if t >= 2:
                    turn_c(t - 2)
            pe.wait_ge(s_ceD, NT)
            pe.wait_ge(s_ceA, NT)
            pe.nop().then_inc(s_grp, 1)

            pe.wait_ge(s_small, 48)

            def up(t):
                n, b = ROWS[t], 2 * (t % 2)
                if t >= 2:
                    pe.wait_ge(s_kqn, t - 1)
                    pe.wait_ge(s_v, t - 1)
                mm(ps[0:n, b, :], cT[:, 2, tok(t)], wukv[:, 0:512], start=True, stop=True)
                for k in range(2):
                    ins = mm(ps[0:n, b + 1, :], cT[:, k, tok(t)], wuq[:, k, :], start=k == 0, stop=k == 1)
                mm(ps[0:n, 4 + t % 2, :], cT[:, 2, tok(t)], wukv[:, 512:1024], start=True, stop=True).then_inc(s_kq, 1)

            def turn_kq(t):
                n = ROWS[t]
                pe.wait_ge(s_kqn, t + 1)
                if t >= 1:
                    pe.wait_ge(s_kTe, t)
                if t >= 2:
                    pe.wait_ge(s_qTe, t - 1)
                for j in range(8 if t else 4):
                    ins = turn(ps[:, 6 + j // 4, 128 * (j % 4):128 * (j % 4) + n],
                               qkn[0:n, t % 2, 128 * j:128 * j + 128], ident[0:n, 0:n])
                ins.then_inc(s_kqT, 1)

            for t in range(NT + 1):
                if t < NT:
                    up(t)
                if t:
                    turn_kq(t - 1)
            pe.wait_ge(s_kTe, NT)
            pe.wait_ge(s_qTe, NB)
            for n in range(4):
                m, cc = n // 2, n % 2
                if n >= 2:
                    pe.wait_ge(s_qie, n - 1)
                for k in range(2):
                    ins = mm(ps[:, 6 + n % 2, :], wqi[:, k, 128 * m:128 * m + 128],
                             cT[:, k, META + 512 * cc:META + 512 * cc + 512], start=k == 0, stop=k == 1)
                ins.then_inc(s_qi, 1)
            pe.wait_ge(s_qie, 4)
            pe.wait_ge(s_kqn, NT)
            pe.wait_ge(s_v, NT)
            for n in range(HI * (NB - 1)):
                i, h = 1 + n // HI, n % HI
                if n >= 2:
                    pe.wait_ge(s_relu, n - 1)
                r = slice(64 * (h % 2), 64 * (h % 2) + 64)
                for lo, hi in pieces(KEYS[i]):
                    ins = mm(pf[:, 1536 * (n % 2) + lo:1536 * (n % 2) + hi], qiT[r, h // 2, 128 * i:128 * i + 128],
                             kiT[r, lo:hi], start=True, stop=True)
                ins.then_inc(s_iq, 1)
            pe.wait_ge(s_skr, 16)
            pe.wait_ge(s_par, N_PAR)
            for h in range(HA):
                if h >= 2:
                    pe.wait_ge(s_rbe, h - 1)
                mm(ps[:, 6 + h % 2, 0:SKEW], relt[:, h:h + 1].broadcast_to([N_REL, 128]), oneh[0:N_REL],
                   start=True, stop=True).then_inc(s_rb, 1)
            pe.wait_ge(s_relu, HI * (NB - 1))
            for g in (1, 2):
                pe.wait_ge(s_w[g % 2], 16 if g == 1 else 16 * (2 * KD + 1))
                for u in range(NB):
                    n = (g - 1) * NB + u
                    if n >= 4:
                        pe.wait_ge(s_ze, n - 3)
                    for k in range(KD):
                        ins = mm(ps[:, n % 4, :], hT[:, k, tok(u + 1)], wslot[:, g % 2, k, :], start=k == 0,
                                 stop=k == KD - 1)
                    ins.then_inc(s_z, 1)
                pe.wait_ge(s_ze, NB * g)
                pe.nop().then_inc(s_grp, 1)
            for n in range(36):
                g, m, (lo, hi) = 3 + n // 12, n // 3 % 4, CHUNKS[n % 3]
                if n % 12 == 0:
                    pe.wait_ge(s_w[g % 2], {3: 32, 4: 16 * (2 * KD + 2), 5: 48}[g])
                if n >= 4:
                    pe.wait_ge(s_che, n - 3)
                for k in range(KD):
                    ins = mm(ps[:, n % 4, 0:hi - lo], wslot[:, g % 2, k, 128 * m:128 * m + 128], hT[:, k, lo:hi],
                             start=k == 0, stop=k == KD - 1)
                ins.then_inc(s_ch, 1)
                if n % 12 == 11:
                    pe.wait_ge(s_che, n + 1)
                    pe.nop().then_inc(s_grp, 1)

            def dots(n):
                i, h = n // HA, n % HA
                if n >= 2:
                    pe.wait_ge(s_red, n - 1)
                r = slice(64 * (h % 2), 64 * (h % 2) + 64)
                lo0 = split(i)
                for lo, hi in pieces(KEYS[i] - lo0):
                    ins = mm(pf[:, 1536 * (n % 2) + lo:1536 * (n % 2) + hi], qT[r, h // 2, 128 * i:128 * i + 128],
                             kT[r, h // 2, lo0 + lo:lo0 + hi], start=True, stop=True)
                if lo0:
                    if h:
                        pe.wait_ge(s_meta, h)
                    ins = mm(ps[:, 2, 0:META], qT[r, h // 2, 128 * i:128 * i + 128], kT[r, h // 2, 0:META],
                             start=True, stop=True)
                ins.then_inc(s_S, 1)

            def turn_p(n):
                i = n // HA
                pe.wait_ge(s_P, n + 1)
                for r, tiles in enumerate(rounds(i)):
                    rr = ROUND0[n] + r
                    if rr >= 2:
                        pe.wait_ge(*turned(rr - 2))
                    for j, kt in enumerate(tiles):
                        ins = turn(ps[0:ROWS[kt], 6 + rr % 2, 128 * j:128 * j + 128], L[:, n % 2, tok(kt)], ident)
                    ins.then_inc(s_PT, 1)

            def weigh(n):
                i, h = n // HA, n % HA
                if h == 0 and i:
                    pe.wait_ge(s_on, i)
                for r, tiles in enumerate(rounds(i)):
                    pe.wait_ge(*turned(ROUND0[n] + r))
                    for kt in tiles:
                        o = ps[:, 5, DA * h:DA * h + DA]
                        ins = mm(o, pT[0:ROWS[kt], n % 2, kt, :], vN[0:ROWS[kt], kt, DA * h:DA * h + DA],
                                 start=kt == 0, stop=kt == i + 1)
                ins.then_inc(s_o, 1)

            for n in range(HA * NB + 2):
                if n < HA * NB:
                    dots(n)
                if 1 <= n <= HA * NB:
                    turn_p(n - 1)
                if n >= 2:
                    weigh(n - 2)

            pe.wait_ge(s_or, NB)
            for t in range(NT):
                n = ROWS[t]
                pe.wait_ge(s_sqk, t + 1)
                for j in range(8):
                    ins = mm(ps[0:n, 0, 8 * t + j:8 * t + j + 1], sqk[:, t % 2, 128 * j:128 * j + n], ones[:, 0:1],
                             start=True, stop=True)
                ins.then_inc(s_ssq, 1)
            pe.wait_ge(s_gd, 10 - 1)
            pe.wait_ge(s_gd, 9)
            for cidx, m in ((0, triu), (1, ones)):
                o = ps[:, 1, 36 * cidx:36 * cidx + 36].rearrange("p (t h) -> p t h", h=4)
                mm(o[:, 0, :], m[0:META, :], gg[0:META, 0, :], start=True, stop=True)
                ins = mm(o[:, 1:, :], m, gg[:, 1:, :], start=True, stop=True)
            ins.then_inc(s_gp, 1)
            NGD = 30
            pe.wait_ge(s_gd, NGD)
            pe.wait_ge(s_ga, 8)
            for t in range(NT):
                n = ROWS[t]
                comp, full = gdn_levels(t)
                cols = slice(3 + OFF[t], 3 + OFF[t] + n)

                def inc(ins):
                    ins.then_inc(g_pe, 1)

                if t:
                    pe.wait_ge(g_dve, DV(t - 1, "out") if t > 1 else DV(0, "s"))
                for b, g in ((0, 1), (1, 2)):
                    for h in range(HG):
                        ins = turn(ps[0:n, b, 128 * h:128 * h + 128], conv4[:, g, h, cols], ident)
                    inc(ins)
                for h in range(HG):
                    o = pf[0:n, 1024 + 256 * h:1280 + 256 * h].rearrange("p (g t) -> p g t", g=2)[:, :, 0:n]
                    ins = mm(o, conv4[:, 1, h, cols], conv4[:, 0:2, h, cols], start=True, stop=True)
                inc(ins)
                for b, rv in ((4, rv1), (5, rv2)):
                    for h in range(HG):
                        ins = mm(ps[:, b, 128 * h:128 * h + n], rv[0:n, t, h:h + 1].broadcast_to([n, 128]),
                                 ident[0:n, 0:n], start=True, stop=True)
                inc(ins)
                prev = 1
                for l in comp:
                    pe.wait_ge(g_pool, PO(t, f"m{l}"))
                    pe.wait_ge(g_dve, DV(t, f"ttf{prev}"))
                    for h in range(HG):
                        ins = mm(ps[:, 0, 32 * h:32 * h + 32], ATm[l][:, h, :], Tc[:, h, :], start=True, stop=True)
                    inc(ins)
                    pe.wait_ge(g_act, AC(t, f"x{l}"))
                    for h in range(HG):
                        ins = mm(ps[:, 1, 32 * h:32 * h + 32], TTf[:, h, :], Xc[:, h, :], start=True, stop=True)
                    inc(ins)
                    prev = l
                for l in full:
                    pe.wait_ge(g_pool, PO(t, f"m{l}"))
                    pe.wait_ge(g_dve, DV(t, f"ttf{prev}"))
                    for h in range(HG):
                        ins = mm(ps[:, 0, 128 * h:128 * h + 128], ATm[l][:, h, :], Tf[:, h, :], start=True, stop=True)
                    inc(ins)
                    pe.wait_ge(g_act, AC(t, f"x{l}"))
                    for h in range(HG):
                        if l == 32:
                            mm(ps[:, 1, 128 * h:128 * h + 128], TTf[:, h, :], Xf[:, h, :], start=True, stop=True)
                        ins = mm(ps[:, 2, 128 * h:128 * h + 128], Xf[:, h, :], TTf[:, h, :], start=True, stop=True)
                    inc(ins)
                    prev = l
                pe.wait_ge(g_dve, DV(t, f"ttf{prev}"))
                for h in range(HG):
                    ins = mm(ps[:, 3, 128 * h:128 * h + n], kbe[0:n, h, :], TTf[0:n, h, 0:n], start=True, stop=True)
                inc(ins)
                pe.wait_ge(g_act, AC(t, "w"))
                if t:
                    pe.wait_ge(g_dve, DV(t - 1, "s"))
                for h in range(HG):
                    ins = mm(ps[0:n, 6, 128 * h:128 * h + 128], TTf[0:n, h, 0:n], bv[0:n, h, :], start=True, stop=t == 0)
                    if t:
                        ins = mm(ps[:, 6, 128 * h:128 * h + 128], wT[:, h, :], S[:, h, :], start=False, stop=True)
                inc(ins)
                pe.wait_ge(g_dve, DV(t, "vnew"))
                if t:
                    pe.wait_ge(g_pool, PO(t, "qd"))
                    for h in range(HG):
                        mm(ps[:, 7, 128 * h:128 * h + 128], qd[:, h, :], S[:, h, :], start=True, stop=False)
                        ins = mm(ps[:, 7, 128 * h:128 * h + 128], aq[:, h, :], vnew[:, h, :], start=False, stop=True)
                    inc(ins)
                for h in range(HG):
                    ins = mm(ps[:, 1, 128 * h:128 * h + 128], kdec[0:n, h, :], vnew[0:n, h, :], start=True, stop=True)
                inc(ins)
                if t:
                    u = t - 1
                    if t == 1:
                        pe.wait_ge(s_w[0], 16 * (2 * KD + 3))
                        pe.wait_ge(s_w[1], 16 * 4)
                    pe.wait_ge(s_yc[u % 2], 16 * (u // 2 + 1))
                    pe.wait_ge(g_dve, DV(t, "y"))
                    for j in range(8):
                        ins = turn(ps[:, 4 + j // 4, 128 * (j % 4):128 * (j % 4) + 128],
                                   ycat[:, u % 2, 128 * j:128 * j + 128], ident)
                    inc(ins)
                    pe.wait_ge(g_act, AC(t, "yt"))
                    pe.wait_ge(g_dve, DV(t, "yt"))
                    for half in range(2):
                        for k in range(8):
                            ins = mm(ps[:, 2 + half, :], yT[:, k, :], wslot[:, half, k, :], start=k == 0, stop=k == 7)
                    inc(ins)


_INS = ["x", "meta_tokens", "rel_bias_table", "norm_gain", "w_in", "cq_norm_gain", "ckv_norm_gain", "w_uq", "w_ukv",
        "w_q_idx", "q_norm_gain", "k_norm_gain", "conv_w", "a_log", "dt_bias", "gdn_norm_gain", "w_out", "onehot"]


def kernel(**inputs):
    import concourse.bacc as bacc
    from concourse.bass_utils import run_bass_kernel_spmd

    inputs = dict(inputs, onehot=rel_onehot())
    nc = bacc.Bacc("TRN2", target_bir_lowering=False, num_devices=1)
    arrays, args = {}, []
    for name in _INS:
        arr = np.ascontiguousarray(inputs[name])
        arrays[f"in_{name}"] = arr
        args.append(nc.dram_tensor(f"in_{name}", arr.shape, mybir.dt.from_np(arr.dtype), kind="ExternalInput").ap())
    y = nc.dram_tensor("y", (1, SEQ, D), F32, kind="ExternalOutput").ap()
    hybrid(nc, *args, y)
    r = run_bass_kernel_spmd(nc, [arrays], core_ids=[0])
    return r.results[0]["y"]
```

```python
import math
from contextlib import ExitStack

import concourse.bass as bass
import numpy as np
from concourse import mybir

F32 = mybir.dt.float32
BF16 = mybir.dt.bfloat16
I32 = mybir.dt.int32
ALU = mybir.AluOpType
ACT = mybir.ActivationFunctionType
AX = mybir.AxisListType

D, SEQ, META, EPS = 1024, 1024, 16, 1e-6
T = META + SEQ
HA, DA = 8, 64
HG, DG = 4, 128
HI = 4
TOPK = 256
CONV = 4
NB = SEQ // 128
NT = NB + 1
ROWS = [META] + [128] * NB
OFF = [0] + [META + 128 * i for i in range(NB)]
KEYS = [META + 128 * (i + 1) for i in range(NB)]
SC0 = [sum(KEYS[:i]) for i in range(NB + 1)]
KD = D // 128
NA = 460
CHUNKS = [(0, 272), (272, 656), (656, 1040)]
FILL = -1.0e30
LOWEST = -3.0e38
TOPBITS = 32
N_REL = 32
SKEW = 383


def rel_onehot():
    dist = np.arange(SKEW, dtype=np.int32)[::-1] - 127
    n = np.maximum(dist, 0)
    nf = np.maximum(n, 1).astype(np.float32)
    large = 16 + (np.log(nf / 16) / math.log(128 / 16) * 16).astype(np.int32)
    bucket = np.where(n < 16, n, np.minimum(large, 31))
    out = np.zeros((N_REL, SKEW), np.float32)
    out[bucket, np.arange(SKEW)] += 1.0
    out[N_REL - 1, :] -= 1.0
    return out


LEVELS = [2, 4, 8, 16, 32, 64]
PRE = ["nat", "rb", "kk"] + [f"{c}{l}" for l in LEVELS for c in "xy"] + ["w"]


def levels(t):
    return LEVELS[:3] if t == 0 else LEVELS


def rec_stages(tiles):
    out = []
    for t in tiles:
        out += [(t, "v"), (t, "os")] + ([(t, "yt")] if t == tiles[0] and t else [])
    for t in tiles:
        if t:
            out += ([(t, "yt")] if t != tiles[0] else []) + [(t, f"o{q}") for q in range(4)] + [(t, "fin")]
    return out


def stage_order():
    groups = [(0, 1), (2, 3), (4, 5), (6, 7), (8,)]
    order, last = [], []
    for tiles in groups:
        for n, stage in enumerate(PRE):
            order += [(t, stage) for t in tiles if stage[0] not in "xy" or int(stage[1:]) in levels(t)]
            if n < len(last):
                order.append(last[n])
        order += last[len(PRE):]
        last = rec_stages(tiles)
    return order + last


def pe_steps(t, stage):
    return {"nat": ["kn", "vn"], "os": ["o", "s"] if t else ["s"], "o0": [], "o1": [], "o2": [], "o3": ["out"],
            "fin": []}.get(stage, [stage])


def dve_steps(t, stage):
    if stage[0] == "y" and stage != "yt":
        l = int(stage[1:])
        return ([f"tc{l}", f"ttc{l}"] + ["tf16"] * (l == 16) if l <= 16 else ["tf32"] * (l == 32)) + [f"ttf{l}"]
    return {"nat": ["kbe", "kdec", "bv"], "rb": ["ga", "gq"],
            "kk": ["at", "aq", "t0", "t1", "t2", "t3", "tc1", "ttc1", "ttf1"], "v": ["vnew"],
            "os": ["s0", "s1", "s2", "s"] if t else ["s"], "yt": ["y0", "y1", "y2", "y"], "o0": ["yt"],
            "fin": ["out"]}.get(stage, [])


def act_steps(t, stage):
    if stage[0] == "x":
        return [stage]
    return {"rb": [f"{g}{h}" for g in ("ga", "gq") for h in range(4)] + (["eq"] if t else []), "w": ["w"],
            "os": ["so0", "so1", "so2", "so3", "ln", "ro"] if t else [], "o0": ["yt"]}.get(stage, [])


def pool_steps(t, stage):
    ls = levels(t)
    if stage == "kk":
        return [f"m{l}" for l in ls[:2]]
    if stage[0] == "x":
        k = ls.index(int(stage[1:])) + 2
        return [f"m{ls[k]}"] if k < len(ls) else []
    return {"rb": ["qd"], "v": ["zg"]}.get(stage, []) if t else []


class Steps:

    def __init__(self, order, steps):
        self.value = {}
        for t, stage in order:
            for name in steps(t, stage):
                assert (t, name) not in self.value
                self.value[t, name] = len(self.value) + 1

    def __call__(self, t, name):
        return self.value[t, name]


def hybrid(nc, x, meta, rel, norm_gain, w_in, g_cq, g_ckv, w_uq, w_ukv, w_qi, g_qn, g_kn, conv_w, a_log,
           dt_bias, g_gdn, w_out, onehot, out):
    ctx = ExitStack()
    with ctx:
        def sb(name, shape, dt=F32):
            return ctx.enter_context(nc.sbuf_tensor(name, shape, dt))

        def sem(name):
            return ctx.enter_context(nc.semaphore(name))

        areaH = sb("areaH", [128, KD * T])
        areaW = sb("areaW", [128, 2 * KD * 512])
        areaC = sb("areaC", [128, 12876])
        areaQ = sb("areaQ", [128, 4 * SEQ + 4 * T + NT * 512])
        scores = sb("scores", [128, SC0[NB]])
        tmp = sb("tmp", [128, 2 * T])
        zst = sb("zst", [128, 2, 512])
        junk = sb("junk", [128, T], BF16)

        class Area:
            def __init__(self, ap):
                self.ap, self.at = ap, 0

            def take(self, *shape):
                n = int(np.prod(shape))
                v = self.ap[:, self.at:self.at + n]
                self.at += n
                assert self.at <= self.ap.shape[1], (self.at, self.ap.shape)
                if len(shape) == 2:
                    v = v.rearrange("p (a b) -> p a b", a=shape[0])
                if len(shape) == 3:
                    v = v.rearrange("p (a b c) -> p a b c", a=shape[0], b=shape[1])
                return v

        hT = areaH[:, :].rearrange("p (k t) -> p k t", k=KD)
        wslot = areaW[:, :].rearrange("p (s k n) -> p s k n", s=2, k=KD)

        c = Area(areaC)
        xin = c.take(2, D)
        cn = c.take(2, 512)
        qkn = c.take(2, 1024)
        cT = c.take(3, T)
        kiT = c.take(T)
        wuq = c.take(2, 512)
        wukv = c.take(1024)
        wqi = c.take(2, 256)
        qiT = c.ap[:, 0:2 * SEQ].rearrange("p (m t) -> p m t", m=2)
        PADT = CONV - 1 + T
        conv = areaC[:, 0:12 * PADT].rearrange("p (m t) -> p m t", m=12)
        conv4 = areaC[:, 0:12 * PADT].rearrange("p (g h t) -> p g h t", g=3, h=4)

        a = Area(areaQ)
        qT, kT, vN = a.take(4, SEQ), a.take(4, T), a.take(NT, 512)

        a = Area(areaH)
        L = a.take(2, T)
        pT = a.take(2, NT, 128)
        bias = a.take(HA, 256)
        mbn = a.take(2, 256)
        zA = a.take(2, 512)
        oA = zst[:, 0, :]

        free = [ar[:, 512 * j:512 * j + 512] for ar in (areaQ[:, :], areaH[:, :], scores[:, :], tmp[:, :],
                                                        zst[:, :, :].rearrange("p a b -> p (a b)"))
                for j in range(ar.shape[1] // 512)]

        def blocks(n):
            return [free.pop(0).rearrange("p (h t) -> p h t", h=HG) for _ in range(n)]

        a = Area(areaQ[:, 0:6656])
        del free[0:13]
        zG, ycat, yT, xres = a.take(2, 512), a.take(2, D), a.take(8, 128), a.take(2, D)
        lnb, gg, dec, tot = a.take(NT, 4), a.take(NT, 4), a.take(NT, 4), a.take(NT, 4)
        rv1, rv2, cb = a.take(NT, 4), a.take(NT, 4), a.take(NT, 4)
        so, ro = a.take(4), a.take(4)
        sqk = ycat
        kdec, bv, TTf, wT, qd, aq = (blocks(4) for _ in range(6))
        kbe, AT, ATm0, ATm1, Tf, Xf = (blocks(2) for _ in range(6))
        ATm = [ATm0, ATm1]
        compact = [free.pop(0) for _ in range(2)]
        TTc, Tc, Xc = ([b[:, 128 * j:128 * j + 128].rearrange("p (h t) -> p h t", h=HG) for b in compact]
                       for j in range(3))
        vnew, S = blocks(2)
        sc = Area(free.pop(0))
        t1, t2 = sc.take(NT, 8), sc.take(NT, 8)
        skbe, skd, beta, cd = sc.take(NT, 4), sc.take(NT, 4), sc.take(NT, 4), sc.take(NT, 4)
        a = Area(tmp)
        R = a.take(2, T)
        cum = tmp[:, 0:T]
        eqb = tmp[:, T:2 * T].bitcast(BF16)
        eq, drop = eqb[:, 0:T], eqb[:, T:2 * T]

        small = sb("small", [128, 1500])
        s = Area(small)
        ident, triu, ones = s.take(128), s.take(128), s.take(128)
        maskS, maskI = s.take(128), s.take(128)
        ic, negc1 = s.take(32), s.take(32)
        gain = s.take(KD)
        gc = s.take(3)
        gq8, gk = s.take(1), s.take(1)
        epst = s.take(1)
        epsn = s.take(1)
        cw = s.take(CONV, 12)
        alog, dtb = s.take(HG), s.take(HG)
        ggd = s.take(128)
        ss, rx = s.take(NT), s.take(NT)
        st, rc = s.take(2, 2), s.take(2, 2)
        ssk, rk = s.take(2, 16), s.take(2, 16)
        widx = s.take(NT, 4)
        ba = s.take(NT, 8)
        cnt, need = s.take(8), s.take(8)
        mx, nm = s.take(HA * NB, 2), s.take(HA * NB)
        rs = s.take(HA * NB)
        rinv = s.take(8)
        ssq = s.take(NT, 8)
        masks = sb("masks", [128, 7, 128], BF16)
        iw = sb("iw", [128, 6, 8], I32)
        bits, cand, flip, pat, hit = (iw[:, j, :] for j in range(5))
        patf = pat.bitcast(F32)
        relt = sb("relt", [N_REL, HA])
        oneh = zst[:, 0, 0:SKEW]
        rowst = zst[:, 1, 0:SKEW]

        ps = ctx.enter_context(nc.psum_tensor("ps", [128, 8, 512], F32))
        pf = ps[:, :, :].rearrange("p b n -> p (b n)")

        skew_d = nc.dram_tensor("skew_scratch", [HA, 128 * SKEW], F32).ap()
        za_d = nc.dram_tensor("gate_a_scratch", [SEQ, 512], F32).ap()
        zg_d = nc.dram_tensor("gate_g_scratch", [SEQ, 512], F32).ap()
        oa_d = nc.dram_tensor("attn_scratch", [SEQ, 512], F32).ap()

        s_par, s_small, s_const, s_dconst = sem("params_in"), sem("lat_weights_in"), sem("consts"), sem("dve_consts")
        s_w = [sem("w_in0"), sem("w_in1")]
        s_x = [sem("x_in0"), sem("x_in1")]
        s_rx, s_xn, s_xT, s_hn = sem("x_rstd"), sem("x_scaled"), sem("x_turned"), sem("hT_ready")
        s_al = sem("act_own")
        s_pA, s_rc, s_c1, s_cn, s_cT, s_ceD, s_ceA = (sem(n) for n in (
            "projA_done", "c_rstd", "c_copied", "c_scaled", "c_turned", "cT_ready", "kiT_ready"))
        s_kq, s_sq, s_ssk, s_rk, s_kqn, s_kqT, s_kTe, s_qTe, s_v = (sem(n) for n in (
            "kq_done", "kq_squared", "kq_sumsq", "kq_rstd", "kq_scaled", "kq_turned", "kT_ready", "qT_ready", "v_ready"))
        s_qi, s_qie, s_iq, s_relu, s_acc, s_caus = (sem(n) for n in (
            "qi_done", "qiT_ready", "index_dots", "index_relu", "index_scores", "scores_causal"))
        s_tk, s_tl, s_pen, s_mb = sem("topk_steps"), sem("topk_own"), sem("penalty"), sem("penalty_causal")
        s_rb, s_rbe, s_sk, s_skr, s_bias = (sem(n) for n in (
            "bias_rows", "bias_rows_out", "skew_written", "skew_last", "bias_in"))
        s_z, s_ze, s_zo = sem("z_done"), sem("z_ready"), [sem("z_out0"), sem("z_out1")]
        s_ch, s_che, s_pad, s_cv, s_cve, s_cvl = (sem(n) for n in (
            "chan_done", "chan_ready", "pads_zero", "conv_sum", "conv_ready", "conv_own"))
        s_grp = sem("group_done")
        s_S, s_red, s_far, s_nm, s_P, s_mbn, s_PT, s_PTe, s_o, s_on, s_or = (sem(n) for n in (
            "logits", "row_max", "row_max_far", "neg_max", "probs", "bias_mask", "probs_turned", "probsT_ready",
            "attn_out", "attn_gated", "attn_scaled"))
        s_meta = sem("meta_logits_read")
        s_PTa = sem("probsT_ready_act")
        s_za, s_oo = [sem("za_in0"), sem("za_in1")], sem("attn_stored")
        s_sqk, s_ssq, s_gd, s_ga, s_gp = (sem(n) for n in (
            "k_squared", "sumsq_dots", "gates_dve", "gates_act", "gates_pe"))
        g_pe, g_dve, g_act, g_pool = sem("gdn_pe"), sem("gdn_dve"), sem("gdn_act"), sem("gdn_pool")
        s_zg, s_yc, s_xr, s_out = ([sem(f"{n}{i}") for i in range(2)] for n in ("zg_in", "oa_in", "xres_in", "y_out"))
        s_outT = sem("final")
        ORDER = stage_order()
        PE, DV, AC, PO = (Steps(ORDER, f) for f in (pe_steps, dve_steps, act_steps, pool_steps))
        N_CONST, N_DCONST, N_PAR = 22, 6, 16 * 15

        def tok(t):
            return slice(OFF[t], OFF[t] + ROWS[t])

        def per_head(ap, n, width=128, heads=HG):
            return ap.unsqueeze(2).broadcast_to([n, heads, width])

        def all_heads(ap, n, width=128, heads=HG):
            return ap.unsqueeze(1).broadcast_to([n, heads, width])

        def pieces(n):
            return [(j, min(j + 512, n)) for j in range(0, n, 512)]

        def split(i):
            return META if KEYS[i] > 1024 else 0

        def rounds(i):
            tiles = list(range(i + 2))
            return [tiles[j:j + 4] for j in range(0, len(tiles), 4)]

        sq2 = areaC[:, 12876 - 1024:12876]

        def copy_round(copy, n, rr, tiles):
            src = ps[:, 6 + rr % 2, :].rearrange("p (k t) -> p k t", k=4)
            if tiles[0] == 0:
                copy(pT[0:META, n % 2, 0, :], src[0:META, 0, :])
                return copy(pT[:, n % 2, 1:len(tiles), :], src[:, 1:len(tiles), :])
            return copy(pT[:, n % 2, tiles[0]:tiles[-1] + 1, :], src[:, 0:len(tiles), :])

        ROUND0 = [0]
        for i in range(NB):
            for h in range(HA):
                ROUND0.append(ROUND0[-1] + len(rounds(i)))

        def turned(r):
            return ((s_PTe, r // 2 + 1) if r % 2 == 0 else (s_PTa, r // 2 + 1))

        zc = 452
        GROUPS = [None, zc, zc + 2048, zc + 512, zc + 1024, zc + 1536, None, None]

        ctx.enter_context(nc.allow_non_contiguous_dma(reason="gains and conv taps, a few KB, go one to a partition"))
        block = ctx.enter_context(nc.Block())

        @block.sync
        def _(sp):
            x2 = x.rearrange("a s d -> (a s) d")

            def load_x(t):
                if t >= 2:
                    sp.wait_ge(s_xT, 2 * (t - 1))
                src = meta if t == 0 else x2[128 * (t - 1):128 * t, :]
                sp.dma_start(xin[0:ROWS[t], t % 2, :], src).then_inc(s_x[t % 2], 16)

            load_x(0)
            load_x(1)
            wv = w_in[0].rearrange("(k p) n -> p k n", p=128)
            for k in range(KD):
                sp.dma_start(wslot[:, 0, k, 0:452], wv[:, k, 0:452]).then_inc(s_w[0], 16)
                sp.dma_start(wslot[:, 0, k, 452:460], wv[:, k, 3012:3020]).then_inc(s_w[0], 16)
            for t in range(2, NT):
                load_x(t)
            sp.dma_start(wuq, w_uq[0].rearrange("(k p) n -> p k n", p=128)).then_inc(s_small, 16)
            sp.dma_start(wukv, w_ukv[0]).then_inc(s_small, 16)
            sp.dma_start(wqi, w_qi[0].rearrange("(k p) n -> p k n", p=128)).then_inc(s_small, 16)

            def load_group(g):
                if g >= 2:
                    sp.wait_ge(s_grp, g - 1)
                if g < 6:
                    src = wv[:, :, GROUPS[g]:GROUPS[g] + 512]
                else:
                    src = w_out[0].rearrange("(k p) n -> p k n", p=128)[:, :, 512 * (g - 6):512 * (g - 5)]
                sp.dma_start(wslot[:, g % 2, :, :], src).then_inc(s_w[g % 2], 16)

            load_group(1)
            sp.dma_start(oneh[0:N_REL], onehot).then_inc(s_skr, 16)
            for h in range(HA):
                sp.wait_ge(s_rbe, h + 1)
                sp.dma_start(skew_d[h].rearrange("(p m) -> p m", p=128), rowst).then_inc(s_sk, 16)
            load_group(2)

            def store_z(g, u):
                n = (g - 1) * NB + u
                sp.wait_ge(s_ze, n + 1)
                dst = (za_d if g == 1 else zg_d)[128 * u:128 * u + 128, :]
                sp.dma_start(dst, zst[:, n % 2, :]).then_inc(s_zo[n % 2], 16)

            for u in range(NB):
                store_z(1, u)
            load_group(3)
            for u in range(NB):
                store_z(2, u)
            for g in range(4, 8):
                load_group(g)
            sp.wait_ge(s_sk, 16 * HA)
            sp.wait_ge(s_grp, 6)
            for h in range(HA):
                src = skew_d[h, 127:127 + 128 * (SKEW - 1)].rearrange("(p m) -> p m", p=128)[:, 0:256]
                sp.dma_start(bias[:, h, :], src).then_inc(s_bias, 16)
            sp.wait_ge(s_zo[0], 16 * NB)
            sp.wait_ge(s_zo[1], 16 * NB)
            for i in range(NB):
                if i >= 2:
                    sp.wait_ge(s_on, i - 1)
                sp.dma_start(zA[:, i % 2, :], za_d[128 * i:128 * i + 128, :]).then_inc(s_za[i % 2], 16)
                if i:
                    sp.wait_ge(s_or, i)
                    sp.dma_start(oa_d[128 * (i - 1):128 * i, :], oA).then_inc(s_oo, 16)
            sp.wait_ge(s_or, NB)
            sp.dma_start(oa_d[128 * (NB - 1):128 * NB, :], oA).then_inc(s_oo, 16)
            sp.wait_ge(s_oo, 16 * NB)

            def store(t):
                u = t - 1
                sp.wait_ge(g_dve, DV(t, "out"))
                sp.dma_start(out[0, 128 * u:128 * u + 128, :], xres[:, u % 2, :]).then_inc(s_out[u % 2], 16)

            sp.wait_ge(s_ssq, NT)
            for t in range(1, NT):
                u = t - 1
                if u >= 2:
                    store(t - 2)
                    sp.wait_ge(s_out[u % 2], 16 * (u // 2))
                sp.dma_start(zG[:, u % 2, :], zg_d[128 * u:128 * u + 128, :]).then_inc(s_zg[u % 2], 16)
                sp.dma_start(ycat[:, u % 2, 0:512], oa_d[128 * u:128 * u + 128, :]).then_inc(s_yc[u % 2], 16)
                sp.dma_start(xres[:, u % 2, :], x2[128 * u:128 * u + 128, :]).then_inc(s_xr[u % 2], 16)
            store(NB - 1)
            store(NB)
            for q in s_out:
                sp.wait_ge(q, 16 * (NB // 2))

        @block.gpsimd
        def _(pool):
            par = [
                (gain, norm_gain[0].rearrange("(k p) -> p k", p=128)),
                (gc[:, 0:2], g_cq[0].rearrange("(k p) -> p k", p=128)),
                (gc[:, 2:3], g_ckv[0].rearrange("(k p) -> p k", p=128)),
                (gq8[0:64], g_qn[0].rearrange("(k p) -> p k", p=64)),
                (gq8[64:128], g_qn[0].rearrange("(k p) -> p k", p=64)),
                (gk[0:64], g_kn[0].rearrange("(k p) -> p k", p=64)),
                (gk[64:128], g_kn[0].rearrange("(k p) -> p k", p=64)),
                (alog, a_log[0].partition_broadcast(128)),
                (dtb, dt_bias[0].partition_broadcast(128)),
                (ggd, g_gdn[0].partition_broadcast(128)),
                (relt[:, :], rel),
            ] + [(cw[:, j, :], conv_w[0, j].rearrange("(m p) -> p m", p=128)) for j in range(CONV)]
            for dst, src in par[0:3]:
                pool.dma_start(dst, src).then_inc(s_par, 16)
            done = [0]

            def link(ins):
                done[0] += 1
                ins.then_inc(s_const, 1)
                pool.wait_ge(s_const, done[0])

            link(nc.gpsimd.memset(ones, 1.0))
            sel = nc.gpsimd.affine_select
            link(nc.gpsimd.memset(ident, 0.0))
            link(sel(out=ident, in_=ident, compare_op=ALU.not_equal, fill=1.0, base=0, pattern=[[-1, 128]],
                     channel_multiplier=1))
            for dst, src in par[3:]:
                pool.dma_start(dst, src).then_inc(s_par, 16)
            link(sel(out=triu, in_=ones, compare_op=ALU.is_ge, fill=0.0, base=0, pattern=[[1, 128]],
                     channel_multiplier=-1))
            link(nc.gpsimd.memset(maskS, 0.0))
            link(sel(out=maskI, in_=maskS, compare_op=ALU.is_ge, fill=FILL, base=0, pattern=[[1, 128]],
                     channel_multiplier=-1))
            link(sel(out=maskS, in_=maskS, compare_op=ALU.is_gt, fill=FILL, base=0, pattern=[[1, 128]],
                     channel_multiplier=-1))
            for n, l in enumerate(LEVELS):
                m = masks[:, n, :].rearrange("p (b f) -> p b f", f=2 * l)
                link(sel(out=m, in_=ones.rearrange("p (b f) -> p b f", f=2 * l), compare_op=ALU.is_ge, fill=0.0,
                         base=0, pattern=[[-2 * l, 128 // (2 * l)], [0, 2 * l]], channel_multiplier=1))
                link(sel(out=m, in_=m, compare_op=ALU.is_ge, fill=0.0, base=l - 1,
                         pattern=[[2 * l, 128 // (2 * l)], [0, 2 * l]], channel_multiplier=-1))
            m = masks[:, 6, :].rearrange("p (b f) -> p b f", f=32)
            link(sel(out=m, in_=ones.rearrange("p (b f) -> p b f", f=32), compare_op=ALU.is_ge, fill=0.0, base=0,
                     pattern=[[-32, 4], [0, 32]], channel_multiplier=1))
            link(sel(out=m, in_=m, compare_op=ALU.is_ge, fill=0.0, base=31, pattern=[[32, 4], [0, 32]],
                     channel_multiplier=-1))
            link(nc.gpsimd.memset(ssq, 1.0))
            assert done[0] == N_CONST, done
            for i in range(1, NB):
                sc = scores[:, SC0[i + 1] - 128:SC0[i + 1]]
                pool.wait_ge(s_acc, HI * i)
                sel(out=sc, in_=sc, compare_op=ALU.is_ge, fill=LOWEST, base=0, pattern=[[-1, 128]],
                    channel_multiplier=1).then_inc(s_caus, 1)
            for i in range(NB):
                sc = scores[:, SC0[i + 1] - 128:SC0[i + 1]]
                pool.wait_ge(s_pen, i + 1)
                sel(out=sc, in_=sc, compare_op=ALU.is_ge, fill=FILL, base=0, pattern=[[-1, 128]],
                    channel_multiplier=1).then_inc(s_mb, 1)
            pool.wait_ge(s_mb, NB)
            pool.wait_ge(s_bias, 16 * HA)
            for i in range(NB):
                near = 144 if i == 0 else 256
                for h in range(HA):
                    n = HA * i + h
                    if n >= 2:
                        pool.wait_ge(s_red, n - 1)
                    nc.gpsimd.tensor_tensor(mbn[:, n % 2, 0:near], scores[:, SC0[i + 1] - near:SC0[i + 1]],
                                            bias[:, h, 256 - near:256], ALU.add).then_inc(s_mbn, 1)
            pool.wait_ge(s_cve, 12)
            pool.wait_ge(s_or, NB)
            pool.wait_ge(s_oo, 16 * NB)
            for t in range(NT):
                n = ROWS[t]
                if t >= 2:
                    pool.wait_ge(s_ssq, t - 1)
                v = conv[:, 0:8, 3 + OFF[t]:3 + OFF[t] + n]
                o = sqk[:, t % 2, :].rearrange("p (m t) -> p m t", m=8)[:, :, 0:n]
                nc.gpsimd.tensor_tensor(o, v, v, ALU.mult).then_inc(s_sqk, 1)

            def mask(t, k):
                l = levels(t)[k]
                nc.gpsimd.tensor_tensor(ATm[k % 2][t % 2], AT[t % 2], all_heads(masks[:, LEVELS.index(l), :], 128),
                                        ALU.mult).then_inc(g_pool, 1)

            for t, stage in ORDER:
                if stage == "rb" and t:
                    pool.wait_ge(g_act, AC(t, "eq"))
                    q = qd[t % 4]
                    nc.gpsimd.tensor_tensor(q, q, conv[:, 0:4, 3 + OFF[t]:3 + OFF[t] + 128],
                                            ALU.mult).then_inc(g_pool, 1)
                if stage == "kk":
                    pool.wait_ge(g_dve, DV(t, "at"))
                    if t >= 2:
                        pool.wait_ge(g_pe, PE(t - 2, f"x{levels(t - 2)[-1]}"))
                    mask(t, 0)
                    mask(t, 1)
                if stage[0] == "x":
                    k = levels(t).index(int(stage[1:]))
                    if k + 2 < len(levels(t)):
                        pool.wait_ge(g_pe, PE(t, stage))
                        mask(t, k + 2)
                if stage == "v" and t:
                    u = t - 1
                    pool.wait_ge(s_zg[u % 2], 16 * (u // 2 + 1))
                    z4 = zG[:, u % 2, :].rearrange("p (h d) -> p h d", h=HG)
                    nc.gpsimd.tensor_tensor(z4, z4, all_heads(ggd, 128), ALU.mult).then_inc(g_pool, 1)

        @block.scalar
        def _(act):
            A = nc.scalar.activation
            own = [0]

            def link(ins):
                own[0] += 1
                ins.then_inc(s_al, 1)
                act.wait_ge(s_al, own[0])

            nc.scalar.preload_act_table_set("natural_log_exp_and_others")
            act.wait_ge(s_dconst, N_DCONST)
            def x_rstd(t):
                n = ROWS[t]
                act.wait_ge(s_x[t % 2], 16 * (t // 2 + 1))
                link(A(junk[0:n, 0:D], xin[0:n, t % 2, :], ACT.Square, accum_out=ss[0:n, t:t + 1]))
                link(A(rx[0:n, t:t + 1], ss[0:n, t:t + 1], ACT.Ln, scale=1.0 / D, bias=epst[0:n]))
                A(rx[0:n, t:t + 1], rx[0:n, t:t + 1], ACT.Exp, scale=-0.5).then_inc(s_rx, 1)

            def latents(t):
                n, b = ROWS[t], 4 + t % 2
                act.wait_ge(s_pA, t + 1)
                if t >= 2:
                    act.wait_ge(s_cT, t - 1)
                    act.wait_ge(s_cn, t - 1)
                A(junk[0:n, 0:256], ps[0:n, b, 0:256], ACT.Square, scale=1 / 16,
                  accum_out=st[0:n, t % 2, 0:1])
                link(A(junk[0:n, 256:384], ps[0:n, b, 256:384], ACT.Square, scale=128 ** -0.5,
                       accum_out=st[0:n, t % 2, 1:2]))
                nc.scalar.copy(cn[0:n, t % 2, 384:448], ps[0:n, b, 384:448])
                nc.scalar.copy(cn[0:n, t % 2, 448:512], ps[0:n, b, 384:448])
                nc.scalar.mul(widx[0:n, t, :], ps[0:n, b, 448:452], (HI * DA) ** -0.5)
                nc.scalar.copy(ba[0:n, t, :], ps[0:n, b, 452:460]).then_inc(s_c1, 1)
                link(A(rc[0:n, t % 2, :], st[0:n, t % 2, :], ACT.Ln, bias=epst[0:n]))
                A(rc[0:n, t % 2, :], rc[0:n, t % 2, :], ACT.Exp, scale=-0.5).then_inc(s_rc, 1)

            for t in range(NT + 3):
                if t < NT:
                    x_rstd(t)
                if 2 <= t < NT + 2:
                    latents(t - 2)
                if t >= 3:
                    act.wait_ge(s_cT, t - 2)
                    nc.scalar.copy(kiT[:, tok(t - 3)], ps[:, 6 + (t - 3) % 2, 384:384 + ROWS[t - 3]]).then_inc(s_ceA, 1)
            for t in range(NT):
                n, b = ROWS[t], 2 * (t % 2)
                kq = pf[0:n, 512 * b:512 * b + 1024]
                act.wait_ge(s_kq, t + 1)
                A(sq2[0:n], kq, ACT.Square, scale=1 / 8).then_inc(s_sq, 1)
                nc.scalar.copy(vN[0:n, t, :], ps[0:n, 4 + t % 2, :]).then_inc(s_v, 1)
                act.wait_ge(s_ssk, t + 1)
                link(A(rk[0:n, t % 2, :], ssk[0:n, t % 2, :], ACT.Ln, bias=epst[0:n]))
                A(rk[0:n, t % 2, :], rk[0:n, t % 2, :], ACT.Exp, scale=-0.5).then_inc(s_rk, 1)
                act.wait_ge(s_kqT, t + 1)
                A(kT[:, :, tok(t)], ps[:, 6, :].rearrange("p (h t) -> p h t", h=4)[:, :, 0:n], ACT.Copy,
                  scale=gk).then_inc(s_kTe, 1)
            for n in range(4):
                act.wait_ge(s_qi, n + 1)
                nc.scalar.copy(qiT[:, n // 2, 512 * (n % 2):512 * (n % 2) + 512], ps[:, 6 + n % 2, :]).then_inc(s_qie, 1)
            for n in range(HI * (NB - 1)):
                i = 1 + n // HI
                act.wait_ge(s_iq, n + 1)
                if n >= 2:
                    act.wait_ge(s_acc, n - 1)
                A(R[:, n % 2, 0:KEYS[i]], pf[:, 1536 * (n % 2):1536 * (n % 2) + KEYS[i]], ACT.Relu).then_inc(s_relu, 1)
            for h in range(HA):
                act.wait_ge(s_rb, h + 1)
                if h:
                    act.wait_ge(s_sk, 16 * h)
                nc.scalar.copy(rowst, ps[:, 6 + h % 2, 0:SKEW]).then_inc(s_rbe, 1)
            act.wait_ge(s_sk, 16 * HA)
            for n in range(2 * NB):
                act.wait_ge(s_z, n + 1)
                if n >= 2:
                    act.wait_ge(s_zo[n % 2], 16 * (n // 2))
                A(zst[:, n % 2, :], ps[:, n % 4, :], ACT.Silu).then_inc(s_ze, 1)
            for n in range(36):
                m, (lo, hi) = n // 3, CHUNKS[n % 3]
                act.wait_ge(s_ch, n + 1)
                nc.scalar.copy(conv[:, m, 3 + lo:3 + hi], ps[:, n % 4, 0:hi - lo]).then_inc(s_che, 1)
            for m in range(12):
                act.wait_ge(s_cv, CONV * (m + 1))
                A(conv[:, m, 3:], tmp[:, T * (m % 2):T * (m % 2) + T], ACT.Silu).then_inc(s_cve, 1)
            for m in range(HA * NB + 1):
                if m < HA * NB:
                    nk = KEYS[m // HA]
                    act.wait_ge(s_nm, m + 1)
                    A(L[:, m % 2, 0:nk], L[:, m % 2, 0:nk], ACT.Exp, bias=nm[:, m:m + 1],
                      accum_out=rs[:, m:m + 1]).then_inc(s_P, 1)
                if m:
                    n = m - 1
                    for r, tiles in enumerate(rounds(n // HA)):
                        rr = ROUND0[n] + r
                        if rr % 2:
                            act.wait_ge(s_PT, rr + 1)
                            if n >= 2:
                                act.wait_ge(s_o, n - 1)
                            copy_round(nc.scalar.copy, n, rr, tiles).then_inc(s_PTa, 1)
            g = [0]

            def glink(ins):
                g[0] += 1
                ins.then_inc(s_ga, 1)
                act.wait_ge(s_ga, g[0])

            nc.scalar.preload_act_table_set("natural_log_exp_and_others")
            act.wait_ge(s_gd, 5)
            glink(A(t1, t1, ACT.Exp, scale=-1.0))
            glink(A(t1, t1, ACT.Ln, bias=1.0))
            glink(A(alog, alog, ACT.Exp))
            act.wait_ge(s_gd, 9)
            glink(A(ssq, ssq, ACT.Ln, bias=epst))
            act.wait_ge(s_gd, 15)
            glink(A(skbe, rv1, ACT.Exp))
            glink(A(skd, t2[:, :, 0:4], ACT.Exp))
            glink(A(beta, lnb, ACT.Exp))
            glink(A(cd, tot, ACT.Exp))

            def heads(b):
                return ps[:, b, :].rearrange("p (h t) -> p h t", h=HG)

            for t, stage in ORDER:
                n, s_, r_ = ROWS[t], t % 2, t % 4
                if stage == "rb":
                    for name, buf in (("ga", AT[s_]), ("gq", aq[r_])):
                        act.wait_ge(g_dve, DV(t, name))
                        for h in range(HG):
                            A(buf[0:n, h, 0:n], buf[0:n, h, 0:n], ACT.Exp, bias=cb[0:n, t, h:h + 1]).then_inc(g_act, 1)
                    if t:
                        if t >= 5:
                            act.wait_ge(g_pe, PE(t - 4, "o"))
                        A(qd[r_], heads(2 * s_ + 1), ACT.Exp).then_inc(g_act, 1)
                if stage[0] == "x":
                    act.wait_ge(g_pe, PE(t, stage))
                    if int(stage[1:]) <= 16:
                        nc.scalar.copy(Xc[s_], ps[:, 2 * s_, 0:128].rearrange("p (h t) -> p h t", h=HG)).then_inc(g_act, 1)
                    else:
                        nc.scalar.copy(Xf[s_], heads(2 * s_)).then_inc(g_act, 1)
                if stage == "w":
                    act.wait_ge(g_pe, PE(t, "w"))
                    if t >= 5:
                        act.wait_ge(g_pe, PE(t - 4, "v"))
                    nc.scalar.copy(wT[r_][:, :, 0:n], heads(2 * s_)[:, :, 0:n]).then_inc(g_act, 1)
                if stage == "os" and t:
                    act.wait_ge(g_pe, PE(t, "o"))
                    if t > 1:
                        act.wait_ge(g_dve, DV(t - 1, "y"))
                    for h in range(HG):
                        A(junk[:, 128 * h:128 * h + 128], ps[:, 5, 128 * h:128 * h + 128], ACT.Square,
                          scale=DG ** -0.5, accum_out=so[:, h:h + 1]).then_inc(g_act, 1)
                    act.wait_ge(g_act, AC(t, "so3"))
                    A(ro, so, ACT.Ln, bias=epst).then_inc(g_act, 1)
                    act.wait_ge(g_act, AC(t, "ln"))
                    A(ro, ro, ACT.Exp, scale=-0.5).then_inc(g_act, 1)
                if stage == "o0":
                    act.wait_ge(g_pe, PE(t, "yt"))
                    nc.scalar.copy(yT[:, 0:4, :], heads(6)).then_inc(g_act, 1)

        @block.vector
        def _(dve):
            V = nc.vector
            d = [0]

            def dlink(ins):
                d[0] += 1
                ins.then_inc(s_dconst, 1)
                dve.wait_ge(s_dconst, d[0])

            dlink(V.memset(epst, EPS))
            dlink(V.memset(epsn, EPS))
            dlink(V.memset(ba, 0.0))
            dlink(V.memset(junk[:, :], 0.0))
            dlink(V.memset(bits, 0))
            dlink(V.memset(cand, 0))
            def scale_x(t):
                n = ROWS[t]
                dve.wait_ge(s_rx, t + 1)
                V.tensor_scalar(xin[0:n, t % 2, :], xin[0:n, t % 2, :], rx[0:n, t:t + 1], None, ALU.mult).then_inc(s_xn, 1)

            def h_turned(t):
                n = ROWS[t]
                for b in range(2):
                    dve.wait_ge(s_xT, 2 * t + b + 1)
                    bank = ps[:, 2 * (t % 2) + b, :].rearrange("p (k t) -> p k t", k=4)[:, :, 0:n]
                    V.tensor_tensor(hT[:, 4 * b:4 * b + 4, tok(t)], bank, per_head(gain[:, 4 * b:4 * b + 4], 128, n, 4),
                                    ALU.mult).then_inc(s_hn, 1)

            def scale_c(t):
                n, b = ROWS[t], 4 + t % 2
                dve.wait_ge(s_rc, t + 1)
                if t >= 2:
                    dve.wait_ge(s_cT, t - 1)
                V.tensor_scalar(cn[0:n, t % 2, 0:256], ps[0:n, b, 0:256], rc[0:n, t % 2, 0:1], None, ALU.mult)
                V.tensor_scalar(cn[0:n, t % 2, 256:384], ps[0:n, b, 256:384], rc[0:n, t % 2, 1:2], None,
                                ALU.mult).then_inc(s_cn, 1)

            def c_turned(t):
                n = ROWS[t]
                dve.wait_ge(s_cT, t + 1)
                dve.wait_ge(s_ceA, t + 1)
                src = ps[:, 6 + t % 2, 0:384].rearrange("p (k t) -> p k t", k=3)[:, :, 0:n]
                V.tensor_tensor(cT[:, :, tok(t)], src, per_head(gc, 128, n, 3), ALU.mult).then_inc(s_ceD, 1)

            for t in range(NT + 3):
                if t < NT:
                    scale_x(t)
                if t == 1:
                    dve.wait_ge(s_par, N_PAR)
                if 1 <= t <= NT:
                    h_turned(t - 1)
                if 2 <= t < NT + 2:
                    scale_c(t - 2)
                if t >= 3:
                    c_turned(t - 3)
            V.tensor_scalar(gq8, gq8, DA ** -0.5, None, ALU.mult).then_inc(s_tl, 1)
            dve.wait_ge(s_tl, 1)
            for t in range(NT):
                n, b = ROWS[t], 2 * (t % 2)
                dve.wait_ge(s_sq, t + 1)
                if t >= 2:
                    dve.wait_ge(s_rk, t - 1)
                V.tensor_reduce(ssk[0:n, t % 2, :], sq2[0:n].rearrange("p (h d) -> p h d", h=16), AX.X,
                                ALU.add).then_inc(s_ssk, 1)
                dve.wait_ge(s_rk, t + 1)
                if t >= 2:
                    dve.wait_ge(s_kqT, t - 1)
                V.tensor_tensor(qkn[0:n, t % 2, :].rearrange("p (h d) -> p h d", h=16),
                                pf[0:n, 512 * b:512 * b + 1024].rearrange("p (h d) -> p h d", h=16),
                                per_head(rk[0:n, t % 2, :], n, DA, 16), ALU.mult).then_inc(s_kqn, 1)
                if t:
                    dve.wait_ge(s_kqT, t + 1)
                    V.tensor_scalar(qT[:, :, 128 * (t - 1):128 * t], ps[:, 7, :].rearrange("p (h t) -> p h t", h=4),
                                    gq8, None, ALU.mult).then_inc(s_qTe, 1)
            for n in range(HI * (NB - 1)):
                i, h = 1 + n // HI, n % HI
                sc = scores[:, SC0[i]:SC0[i] + KEYS[i]]
                dve.wait_ge(s_relu, n + 1)
                if h == 0:
                    V.tensor_scalar(sc, R[:, n % 2, 0:KEYS[i]], widx[:, i + 1, h:h + 1], None,
                                    ALU.mult).then_inc(s_acc, 1)
                else:
                    dve.wait_ge(s_acc, n)
                    V.scalar_tensor_tensor(sc, R[:, n % 2, 0:KEYS[i]], widx[:, i + 1, h:h + 1], sc, ALU.mult,
                                           ALU.add).then_inc(s_acc, 1)
            NI = NB - 1
            dve.wait_ge(s_caus, NI)
            base = 1
            U, B = iw[:, 5, 0:NI], bits[:, 0:NI]
            V.memset(U, 0).then_inc(s_tl, 1)
            V.memset(B, -2 ** 31).then_inc(s_tl, 1)
            dve.wait_ge(s_tl, base + 2)
            PER = 6 + NI
            with dve.Fori(0, TOPBITS) as it:
                cd_, fl, pt, ht = (v[:, 0:NI] for v in (cand, flip, pat, hit))
                V.tensor_tensor(cd_, U, B, ALU.bitwise_or).then_inc(s_tk, 1)
                dve.wait_ge(s_tk, it * PER + 1)
                V.tensor_scalar(fl, cd_, 31, -1, ALU.arith_shift_right, ALU.bitwise_xor).then_inc(s_tk, 1)
                dve.wait_ge(s_tk, it * PER + 2)
                V.scalar_tensor_tensor(pt, fl, -2 ** 31, cd_, ALU.bitwise_or, ALU.bitwise_xor).then_inc(s_tk, 1)
                dve.wait_ge(s_tk, it * PER + 3)
                for i in range(1, NB):
                    V.tensor_scalar(junk[:, 0:KEYS[i]], scores[:, SC0[i]:SC0[i] + KEYS[i]],
                                    patf[:, i - 1:i], 0.0, ALU.is_ge, ALU.add,
                                    accum_out=cnt[:, i - 1:i]).then_inc(s_tk, 1)
                    dve.wait_ge(s_tk, it * PER + 3 + i)
                V.tensor_scalar(ht, cnt[:, 0:NI], float(TOPK), -1.0, ALU.is_ge, ALU.mult).then_inc(s_tk, 1)
                V.tensor_scalar(B, B, 1, None, ALU.logical_shift_right)
                dve.wait_ge(s_tk, it * PER + 4 + NI)
                V.tensor_tensor(ht, ht, cd_, ALU.bitwise_and).then_inc(s_tk, 1)
                dve.wait_ge(s_tk, it * PER + 5 + NI)
                V.tensor_tensor(U, U, ht, ALU.bitwise_or).then_inc(s_tk, 1)
                dve.wait_ge(s_tk, it * PER + 6 + NI)
            V.tensor_scalar(flip[:, 0:NI], U, 31, -1, ALU.arith_shift_right, ALU.bitwise_xor).then_inc(s_tl, 1)
            dve.wait_ge(s_tl, base + 3)
            V.scalar_tensor_tensor(pat[:, 0:NI], flip[:, 0:NI], -2 ** 31, U, ALU.bitwise_or,
                                   ALU.bitwise_xor).then_inc(s_tl, 1)
            dve.wait_ge(s_tl, base + 4)
            for i in range(1, NB):
                V.tensor_scalar(junk[:, 0:KEYS[i]], scores[:, SC0[i]:SC0[i] + KEYS[i]], patf[:, i - 1:i], 0.0,
                                ALU.is_gt, ALU.add, accum_out=cnt[:, i - 1:i]).then_inc(s_tl, 1)
                dve.wait_ge(s_tl, base + 4 + i)
            base += NI - 1
            V.tensor_scalar(need[:, 0:NI], cnt[:, 0:NI], -1.0, float(TOPK), ALU.mult, ALU.add).then_inc(s_tl, 1)
            V.memset(scores[:, 0:KEYS[0]], 0.0).then_inc(s_pen, 1)
            dve.wait_ge(s_tl, base + 6)
            k = base + 6
            for i in range(1, NB):
                sc, thr, nk = scores[:, SC0[i]:SC0[i] + KEYS[i]], patf[:, i - 1:i], KEYS[i]
                V.tensor_scalar(eq[:, 0:nk], sc, thr, None, ALU.is_equal).then_inc(s_tl, 1)
                dve.wait_ge(s_tl, k + 1)
                V.tensor_tensor_scan(cum[:, 0:nk], eq[:, 0:nk], junk[:, 0:nk], 0.0, ALU.add,
                                     ALU.bypass).then_inc(s_tl, 1)
                dve.wait_ge(s_tl, k + 2)
                V.scalar_tensor_tensor(drop[:, 0:nk], cum[:, 0:nk], need[:, i - 1:i], eq[:, 0:nk], ALU.is_gt,
                                       ALU.mult).then_inc(s_tl, 1)
                dve.wait_ge(s_tl, k + 3)
                V.scalar_tensor_tensor(sc, sc, thr, drop[:, 0:nk], ALU.is_ge, ALU.subtract).then_inc(s_tl, 1)
                dve.wait_ge(s_tl, k + 4)
                k += 4
                V.tensor_scalar(sc, sc, -1.0, -FILL, ALU.add, ALU.mult).then_inc(s_pen, 1)
            dve.wait_ge(s_qie, 4)
            dve.wait_ge(s_che, 1)
            V.memset(conv[:, :, 0:3], 0.0).then_inc(s_pad, 1)
            dve.wait_ge(s_pad, 1)
            for m in range(12):
                dve.wait_ge(s_che, 3 * (m + 1))
                acc = tmp[:, T * (m % 2):T * (m % 2) + T]
                if m >= 2:
                    dve.wait_ge(s_cve, m - 1)
                for j in range(CONV):
                    if j == 0:
                        V.tensor_scalar(acc, conv[:, m, 0:T], cw[:, 0, m:m + 1], None, ALU.mult).then_inc(s_cv, 1)
                    else:
                        dve.wait_ge(s_cv, CONV * m + j)
                        V.scalar_tensor_tensor(acc, conv[:, m, j:j + T], cw[:, j, m:m + 1], acc, ALU.mult,
                                               ALU.add).then_inc(s_cv, 1)
            dve.wait_ge(s_grp, 6)
            dve.wait_ge(s_mb, NB)
            def logits(n):
                i, h = n // HA, n % HA
                near = 144 if i == 0 else 256
                far = KEYS[i] - near
                lg = pf[:, 1536 * (n % 2):1536 * (n % 2) + KEYS[i]]
                dve.wait_ge(s_S, n + 1)
                if n >= 2:
                    dve.wait_ge(s_PT, ROUND0[n - 1])
                first, lo0 = LOWEST, split(i)
                if lo0:
                    V.tensor_tensor_reduce(L[:, n % 2, 0:lo0], ps[:, 2, 0:lo0], scores[:, SC0[i]:SC0[i] + lo0],
                                           1.0, first, ALU.add, ALU.max, mx[:, n, 1:2]).then_inc(s_meta, 1)
                    dve.wait_ge(s_meta, h + 1)
                    first = mx[:, n, 1:2]
                if far:
                    V.tensor_tensor_reduce(L[:, n % 2, lo0:far], lg[:, 0:far - lo0],
                                           scores[:, SC0[i] + lo0:SC0[i] + far],
                                           1.0, first, ALU.add, ALU.max, mx[:, n, 0:1]).then_inc(s_far, 1)
                    dve.wait_ge(s_far, n + 1 - HA)
                    first = mx[:, n, 0:1]
                dve.wait_ge(s_mbn, n + 1)
                V.tensor_tensor_reduce(L[:, n % 2, far:KEYS[i]], lg[:, far - lo0:KEYS[i] - lo0], mbn[:, n % 2, 0:near],
                                       1.0, first, ALU.add, ALU.max, mx[:, n, 1:2]).then_inc(s_red, 1)
                dve.wait_ge(s_red, n + 1)
                V.tensor_scalar(nm[:, n:n + 1], mx[:, n, 1:2], -1.0, None, ALU.mult).then_inc(s_nm, 1)

            def copy_even_rounds(n):
                for r, tiles in enumerate(rounds(n // HA)):
                    rr = ROUND0[n] + r
                    if rr % 2 == 0:
                        dve.wait_ge(s_PT, rr + 1)
                        if n >= 2:
                            dve.wait_ge(s_o, n - 1)
                        copy_round(V.tensor_copy, n, rr, tiles).then_inc(s_PTe, 1)

            def gate_block(i):
                dve.wait_ge(s_P, HA * (i + 1))
                V.reciprocal(rinv, rs[:, HA * i:HA * i + HA])
                dve.wait_ge(s_o, HA * (i + 1))
                dve.wait_ge(s_za[i % 2], 16 * (i // 2 + 1))
                if i:
                    dve.wait_ge(s_oo, 16 * i)
                V.tensor_tensor(oA, ps[:, 5, :], zA[:, i % 2, :], ALU.mult).then_inc(s_on, 1)
                dve.wait_ge(s_on, i + 1)
                o3 = oA.rearrange("p (h d) -> p h d", h=HA)
                V.tensor_tensor(o3, o3, per_head(rinv, 128, DA, HA), ALU.mult).then_inc(s_or, 1)
                dve.wait_ge(s_or, i + 1)

            for m in range(HA * NB + 2):
                if m < HA * NB:
                    logits(m)
                if 1 <= m <= HA * NB:
                    copy_even_rounds(m - 1)
                if m >= 2 and (m - 2) % HA == HA - 1:
                    gate_block((m - 2) // HA)
            g = [0]

            def glink(ins):
                g[0] += 1
                ins.then_inc(s_gd, 1)
                dve.wait_ge(s_gd, g[0])

            dve.wait_ge(s_c1, NT)
            glink(V.tensor_tensor(t2[:, :, 4:8], ba[:, :, 4:8], all_heads(dtb, 128, 4, NT), ALU.add))
            glink(V.tensor_scalar(t2[:, :, 0:4], ba[:, :, 0:4], -1.0, None, ALU.mult))
            glink(V.tensor_scalar(t1, t2, -1.0, None, ALU.mult))
            glink(V.tensor_tensor(t1, t1, t2, ALU.max))
            glink(V.tensor_scalar(t2, t2, 0.0, None, ALU.max))
            dve.wait_ge(s_ga, 3)
            glink(V.tensor_tensor(t1, t1, t2, ALU.add))
            glink(V.tensor_scalar(lnb, t1[:, :, 0:4], -1.0, None, ALU.mult))
            dve.wait_ge(s_ssq, NT)
            V.tensor_copy(ssq[0:META, 0, :], ps[0:META, 0, 0:8])
            glink(V.tensor_copy(ssq[:, 1:, :], ps[:, 0, 8:8 * NT].rearrange("p (t c) -> p t c", c=8)))
            glink(V.scalar_tensor_tensor(gg, t1[:, :, 4:8], -1.0, all_heads(alog, 128, 4, NT), ALU.mult, ALU.mult))
            dve.wait_ge(s_gp, 1)
            p1 = ps[:, 1, 0:8 * NT].rearrange("p (c t h) -> p c t h", c=2, h=4)
            V.tensor_copy(dec, p1[:, 0])
            glink(V.tensor_copy(tot, p1[:, 1]))
            dve.wait_ge(s_ga, 4)
            glink(V.scalar_tensor_tensor(rv1, ssq[:, :, 4:8], -0.5, dec, ALU.mult, ALU.add))
            glink(V.tensor_tensor(rv1, rv1, lnb, ALU.add))
            V.scalar_tensor_tensor(rv2, ssq[:, :, 0:4], -0.5, dec, ALU.mult, ALU.add)
            glink(V.scalar_tensor_tensor(cb, ssq[:, :, 4:8], -0.5, dec, ALU.mult, ALU.subtract))
            glink(V.tensor_scalar(rv2, rv2, -0.5 * math.log(DG), None, ALU.add))
            glink(V.tensor_tensor(t2[:, :, 0:4], cb, tot, ALU.add))
            dve.wait_ge(s_ga, 8)
            glink(V.tensor_scalar(skbe, skbe, -1.0, None, ALU.mult))
            glink(V.memset(AT[0], 0.0))
            glink(V.memset(ic, 0.0))
            for b in range(4):
                rows = slice(32 * b, 32 * b + 32)
                glink(V.tensor_copy(ic[rows], ident[rows, 32 * b:32 * b + 32]))
            for n, l in enumerate(LEVELS):
                m = masks[:, n, :].rearrange("p (b c f) -> p b c f", c=2, f=l)
                glink(V.memset(m[:, :, 0, :], 0.0))
            glink(V.memset(negc1, 0.0))
            glink(V.tensor_scalar(negc1.rearrange("p (b c) -> p b c", c=2)[:, :, 1],
                                  ic.rearrange("p (b c) -> p b c", c=2)[:, :, 0], -1.0, None, ALU.mult))

            def bank(b):
                return ps[:, b, :].rearrange("p (h t) -> p h t", h=HG)

            def flat(ap):
                return ap.rearrange("p h t -> p (h t)")

            bd32 = masks[:, 6, :].rearrange("p (b t) -> p b t", b=4).unsqueeze(1).broadcast_to([128, HG, 4, 32])

            def spread(dst, src):
                return V.tensor_tensor(dst.rearrange("p h (b t) -> p h b t", b=4),
                                       src.unsqueeze(2).broadcast_to([128, HG, 4, 32]), bd32, ALU.mult)

            def norm_keys(t):
                n, s_, r_ = ROWS[t], t % 2, t % 4
                dve.wait_ge(g_pe, PE(t, "kn"))
                if t >= 4:
                    dve.wait_ge(g_pe, PE(t - 4, "s"))
                V.tensor_tensor(kbe[s_][0:n], bank(2 * s_)[0:n], per_head(skbe[0:n, t], n), ALU.mult).then_inc(g_dve, 1)
                V.tensor_tensor(kdec[r_][0:n], bank(2 * s_)[0:n], per_head(skd[0:n, t], n), ALU.mult).then_inc(g_dve, 1)
                dve.wait_ge(g_pe, PE(t, "vn"))
                V.tensor_tensor(bv[r_][0:n], bank(2 * s_ + 1)[0:n], per_head(beta[0:n, t], n), ALU.mult).then_inc(g_dve, 1)

            def exponents(t):
                n, s_, r_ = ROWS[t], t % 2, t % 4
                dve.wait_ge(g_pe, PE(t, "rb"))
                if t >= 2:
                    dve.wait_ge(g_pool, PO(t - 2, f"m{levels(t - 2)[-1]}"))
                V.tensor_tensor(AT[s_][0:n, :, 0:n], bank(2 * s_)[0:n, :, 0:n], all_heads(maskS[0:n, 0:n], n, n),
                                ALU.add).then_inc(g_dve, 1)
                V.tensor_tensor(aq[r_][0:n, :, 0:n], bank(2 * s_ + 1)[0:n, :, 0:n], all_heads(maskI[0:n, 0:n], n, n),
                                ALU.add).then_inc(g_dve, 1)

            def products(t):
                n, s_, r_ = ROWS[t], t % 2, t % 4
                kk = pf[0:n, 1024 * s_:1024 * s_ + 1024].rearrange("p (h g t) -> p h g t", h=HG, g=2)
                at, q = AT[s_], aq[r_]
                dve.wait_ge(g_pe, PE(t, "kk"))
                dve.wait_ge(g_act, AC(t, "gq3"))
                V.tensor_tensor(at[0:n, :, 0:n], kk[:, :, 1, 0:n], at[0:n, :, 0:n], ALU.mult).then_inc(g_dve, 1)
                V.tensor_tensor(q[0:n, :, 0:n], kk[:, :, 0, 0:n], q[0:n, :, 0:n], ALU.mult).then_inc(g_dve, 1)
                dve.wait_ge(g_dve, DV(t, "at"))
                for b in range(4):
                    rows = slice(32 * b, 32 * b + 32)
                    V.tensor_tensor(TTc[s_][rows], at[rows, :, 32 * b:32 * b + 32], all_heads(negc1[rows], 32, 32),
                                    ALU.mult).then_inc(g_dve, 1)
                dve.wait_ge(g_dve, DV(t, "t3"))
                V.tensor_tensor(TTc[s_], TTc[s_], all_heads(ic, 128, 32), ALU.add).then_inc(g_dve, 1)
                dve.wait_ge(g_dve, DV(t, "tc1"))
                V.transpose(flat(Tc[s_]), flat(TTc[s_])).then_inc(g_dve, 1)
                spread(TTf[r_], TTc[s_]).then_inc(g_dve, 1)

            def merge(t, l):
                s_, r_ = t % 2, t % 4
                dve.wait_ge(g_pe, PE(t, f"y{l}"))
                if l <= 16:
                    V.tensor_tensor(Tc[s_], Tc[s_], ps[:, 2 * s_ + 1, 0:128].rearrange("p (h t) -> p h t", h=HG),
                                    ALU.subtract).then_inc(g_dve, 1)
                    dve.wait_ge(g_dve, DV(t, f"tc{l}"))
                    V.transpose(flat(TTc[s_]), flat(Tc[s_])).then_inc(g_dve, 1)
                    if l == 16:
                        spread(Tf[s_], Tc[s_]).then_inc(g_dve, 1)
                    dve.wait_ge(g_dve, DV(t, f"ttc{l}"))
                    spread(TTf[r_], TTc[s_]).then_inc(g_dve, 1)
                else:
                    if l == 32:
                        V.tensor_tensor(Tf[s_], Tf[s_], bank(2 * s_ + 1), ALU.subtract).then_inc(g_dve, 1)
                    b = 2 * s_ if l == 32 else 2 * s_ + 1
                    V.tensor_tensor(TTf[r_], TTf[r_], bank(b), ALU.subtract).then_inc(g_dve, 1)

            def state(t):
                dve.wait_ge(g_pe, PE(t, "s"))
                if t == 0:
                    V.tensor_copy(S, bank(4)).then_inc(g_dve, 1)
                    return
                for h in range(HG):
                    V.scalar_tensor_tensor(S[:, h, :], S[:, h, :], cd[:, t, h:h + 1], bank(4)[:, h, :], ALU.mult,
                                           ALU.add).then_inc(g_dve, 1)

            def gate_tile(t):
                u = t - 1
                dve.wait_ge(g_act, AC(t, "ro"))
                dve.wait_ge(g_pool, PO(t, "zg"))
                if u >= 2:
                    dve.wait_ge(g_pe, PE(t - 2, "yt"))
                for h in range(HG):
                    V.scalar_tensor_tensor(ycat[:, u % 2, 512 + 128 * h:640 + 128 * h], bank(5)[:, h, :],
                                           ro[:, h:h + 1], zG[:, u % 2, 128 * h:128 * h + 128], ALU.mult,
                                           ALU.mult).then_inc(g_dve, 1)

            for t, stage in ORDER:
                u = t - 1
                if stage == "nat":
                    norm_keys(t)
                elif stage == "rb":
                    exponents(t)
                elif stage == "kk":
                    products(t)
                elif stage == "v":
                    dve.wait_ge(g_pe, PE(t, "v"))
                    V.tensor_copy(vnew[0:ROWS[t]], bank(4)[0:ROWS[t]]).then_inc(g_dve, 1)
                elif stage == "os":
                    state(t)
                elif stage == "yt":
                    gate_tile(t)
                elif stage[0] == "y":
                    merge(t, int(stage[1:]))
                elif stage == "o0":
                    dve.wait_ge(g_pe, PE(t, "yt"))
                    V.tensor_copy(yT[:, 4:8, :], bank(7)).then_inc(g_dve, 1)
                elif stage == "fin":
                    dve.wait_ge(g_pe, PE(t, "out"))
                    dve.wait_ge(s_xr[u % 2], 16 * (u // 2 + 1))
                    V.tensor_tensor(xres[:, u % 2, :], pf[:, 3072:4096], xres[:, u % 2, :], ALU.add).then_inc(g_dve, 1)

        @block.tensor
        def _(pe):
            mm, turn = nc.tensor.matmul, nc.tensor.transpose
            pe.wait_ge(s_const, N_CONST)

            def turn_x(t):
                n = ROWS[t]
                pe.wait_ge(s_xn, t + 1)
                for b in range(2):
                    if t >= 2:
                        pe.wait_ge(s_hn, 2 * (t - 2) + b + 1)
                    for k in range(4):
                        ins = turn(ps[:, 2 * (t % 2) + b, 128 * k:128 * k + n],
                                   xin[0:n, t % 2, 128 * (4 * b + k):128 * (4 * b + k + 1)], ident[0:n, 0:n])
                    ins.then_inc(s_xT, 1)

            def proj_a(t):
                n, b = ROWS[t], 4 + t % 2
                pe.wait_ge(s_hn, 2 * (t + 1))
                if t == 0:
                    pe.wait_ge(s_w[0], 16 * 2 * KD)
                if t >= 2:
                    pe.wait_ge(s_c1, t - 1)
                    pe.wait_ge(s_cn, t - 1)
                for k in range(KD):
                    ins = mm(ps[0:n, b, 0:NA], hT[:, k, tok(t)], wslot[:, 0, k, 0:NA], start=k == 0, stop=k == KD - 1)
                ins.then_inc(s_pA, 1)

            def turn_c(t):
                n = ROWS[t]
                pe.wait_ge(s_cn, t + 1)
                pe.wait_ge(s_c1, t + 1)
                if t >= 2:
                    pe.wait_ge(s_ceD, t - 1)
                    pe.wait_ge(s_ceA, t - 1)
                for k in range(4):
                    ins = turn(ps[:, 6 + t % 2, 128 * k:128 * k + n], cn[0:n, t % 2, 128 * k:128 * k + 128],
                               ident[0:n, 0:n])
                ins.then_inc(s_cT, 1)

            for t in range(NT + 2):
                if t < NT:
                    turn_x(t)
                if 1 <= t <= NT:
                    proj_a(t - 1)
                if t >= 2:
                    turn_c(t - 2)
            pe.wait_ge(s_ceD, NT)
            pe.wait_ge(s_ceA, NT)
            pe.nop().then_inc(s_grp, 1)

            pe.wait_ge(s_small, 48)

            def up(t):
                n, b = ROWS[t], 2 * (t % 2)
                if t >= 2:
                    pe.wait_ge(s_kqn, t - 1)
                    pe.wait_ge(s_v, t - 1)
                mm(ps[0:n, b, :], cT[:, 2, tok(t)], wukv[:, 0:512], start=True, stop=True)
                for k in range(2):
                    ins = mm(ps[0:n, b + 1, :], cT[:, k, tok(t)], wuq[:, k, :], start=k == 0, stop=k == 1)
                mm(ps[0:n, 4 + t % 2, :], cT[:, 2, tok(t)], wukv[:, 512:1024], start=True, stop=True).then_inc(s_kq, 1)

            def turn_kq(t):
                n = ROWS[t]
                pe.wait_ge(s_kqn, t + 1)
                if t >= 1:
                    pe.wait_ge(s_kTe, t)
                if t >= 2:
                    pe.wait_ge(s_qTe, t - 1)
                for j in range(8 if t else 4):
                    ins = turn(ps[:, 6 + j // 4, 128 * (j % 4):128 * (j % 4) + n],
                               qkn[0:n, t % 2, 128 * j:128 * j + 128], ident[0:n, 0:n])
                ins.then_inc(s_kqT, 1)

            for t in range(NT + 1):
                if t < NT:
                    up(t)
                if t:
                    turn_kq(t - 1)
            pe.wait_ge(s_kTe, NT)
            pe.wait_ge(s_qTe, NB)
            for n in range(4):
                m, cc = n // 2, n % 2
                if n >= 2:
                    pe.wait_ge(s_qie, n - 1)
                for k in range(2):
                    ins = mm(ps[:, 6 + n % 2, :], wqi[:, k, 128 * m:128 * m + 128],
                             cT[:, k, META + 512 * cc:META + 512 * cc + 512], start=k == 0, stop=k == 1)
                ins.then_inc(s_qi, 1)
            pe.wait_ge(s_qie, 4)
            pe.wait_ge(s_kqn, NT)
            pe.wait_ge(s_v, NT)
            for n in range(HI * (NB - 1)):
                i, h = 1 + n // HI, n % HI
                if n >= 2:
                    pe.wait_ge(s_relu, n - 1)
                r = slice(64 * (h % 2), 64 * (h % 2) + 64)
                for lo, hi in pieces(KEYS[i]):
                    ins = mm(pf[:, 1536 * (n % 2) + lo:1536 * (n % 2) + hi], qiT[r, h // 2, 128 * i:128 * i + 128],
                             kiT[r, lo:hi], start=True, stop=True)
                ins.then_inc(s_iq, 1)
            pe.wait_ge(s_skr, 16)
            pe.wait_ge(s_par, N_PAR)
            for h in range(HA):
                if h >= 2:
                    pe.wait_ge(s_rbe, h - 1)
                mm(ps[:, 6 + h % 2, 0:SKEW], relt[:, h:h + 1].broadcast_to([N_REL, 128]), oneh[0:N_REL],
                   start=True, stop=True).then_inc(s_rb, 1)
            pe.wait_ge(s_relu, HI * (NB - 1))
            for g in (1, 2):
                pe.wait_ge(s_w[g % 2], 16 if g == 1 else 16 * (2 * KD + 1))
                for u in range(NB):
                    n = (g - 1) * NB + u
                    if n >= 4:
                        pe.wait_ge(s_ze, n - 3)
                    for k in range(KD):
                        ins = mm(ps[:, n % 4, :], hT[:, k, tok(u + 1)], wslot[:, g % 2, k, :], start=k == 0,
                                 stop=k == KD - 1)
                    ins.then_inc(s_z, 1)
                pe.wait_ge(s_ze, NB * g)
                pe.nop().then_inc(s_grp, 1)
            for n in range(36):
                g, m, (lo, hi) = 3 + n // 12, n // 3 % 4, CHUNKS[n % 3]
                if n % 12 == 0:
                    pe.wait_ge(s_w[g % 2], {3: 32, 4: 16 * (2 * KD + 2), 5: 48}[g])
                if n >= 4:
                    pe.wait_ge(s_che, n - 3)
                for k in range(KD):
                    ins = mm(ps[:, n % 4, 0:hi - lo], wslot[:, g % 2, k, 128 * m:128 * m + 128], hT[:, k, lo:hi],
                             start=k == 0, stop=k == KD - 1)
                ins.then_inc(s_ch, 1)
                if n % 12 == 11:
                    pe.wait_ge(s_che, n + 1)
                    pe.nop().then_inc(s_grp, 1)

            def dots(n):
                i, h = n // HA, n % HA
                if n >= 2:
                    pe.wait_ge(s_red, n - 1)
                r = slice(64 * (h % 2), 64 * (h % 2) + 64)
                lo0 = split(i)
                for lo, hi in pieces(KEYS[i] - lo0):
                    ins = mm(pf[:, 1536 * (n % 2) + lo:1536 * (n % 2) + hi], qT[r, h // 2, 128 * i:128 * i + 128],
                             kT[r, h // 2, lo0 + lo:lo0 + hi], start=True, stop=True)
                if lo0:
                    if h:
                        pe.wait_ge(s_meta, h)
                    ins = mm(ps[:, 2, 0:META], qT[r, h // 2, 128 * i:128 * i + 128], kT[r, h // 2, 0:META],
                             start=True, stop=True)
                ins.then_inc(s_S, 1)

            def turn_p(n):
                i = n // HA
                pe.wait_ge(s_P, n + 1)
                for r, tiles in enumerate(rounds(i)):
                    rr = ROUND0[n] + r
                    if rr >= 2:
                        pe.wait_ge(*turned(rr - 2))
                    for j, kt in enumerate(tiles):
                        ins = turn(ps[0:ROWS[kt], 6 + rr % 2, 128 * j:128 * j + 128], L[:, n % 2, tok(kt)], ident)
                    ins.then_inc(s_PT, 1)

            def weigh(n):
                i, h = n // HA, n % HA
                if h == 0 and i:
                    pe.wait_ge(s_on, i)
                for r, tiles in enumerate(rounds(i)):
                    pe.wait_ge(*turned(ROUND0[n] + r))
                    for kt in tiles:
                        o = ps[:, 5, DA * h:DA * h + DA]
                        ins = mm(o, pT[0:ROWS[kt], n % 2, kt, :], vN[0:ROWS[kt], kt, DA * h:DA * h + DA],
                                 start=kt == 0, stop=kt == i + 1)
                ins.then_inc(s_o, 1)

            for n in range(HA * NB + 2):
                if n < HA * NB:
                    dots(n)
                if 1 <= n <= HA * NB:
                    turn_p(n - 1)
                if n >= 2:
                    weigh(n - 2)

            pe.wait_ge(s_or, NB)
            for t in range(NT):
                n = ROWS[t]
                pe.wait_ge(s_sqk, t + 1)
                for j in range(8):
                    ins = mm(ps[0:n, 0, 8 * t + j:8 * t + j + 1], sqk[:, t % 2, 128 * j:128 * j + n], ones[:, 0:1],
                             start=True, stop=True)
                ins.then_inc(s_ssq, 1)
            pe.wait_ge(s_gd, 10 - 1)
            pe.wait_ge(s_gd, 9)
            for cidx, m in ((0, triu), (1, ones)):
                o = ps[:, 1, 36 * cidx:36 * cidx + 36].rearrange("p (t h) -> p t h", h=4)
                mm(o[:, 0, :], m[0:META, :], gg[0:META, 0, :], start=True, stop=True)
                ins = mm(o[:, 1:, :], m, gg[:, 1:, :], start=True, stop=True)
            ins.then_inc(s_gp, 1)
            NGD = 30
            pe.wait_ge(s_gd, NGD)
            pe.wait_ge(s_ga, 8)

            def col(b, h, w=128):
                return ps[:, b, 128 * h:128 * h + w]

            for t, stage in ORDER:
                n, s_, r_, u = ROWS[t], t % 2, t % 4, t - 1
                cols = slice(3 + OFF[t], 3 + OFF[t] + n)
                b0, b1 = 2 * s_, 2 * s_ + 1
                if stage == "nat":
                    if t >= 2:
                        pe.wait_ge(g_act, AC(t - 2, "w"))
                    for b, g in ((b0, 1), (b1, 2)):
                        for h in range(HG):
                            ins = turn(ps[0:n, b, 128 * h:128 * h + 128], conv4[:, g, h, cols], ident)
                        ins.then_inc(g_pe, 1)
                elif stage == "rb":
                    for b, rv, name in ((b0, rv1, "kdec"), (b1, rv2, "bv")):
                        pe.wait_ge(g_dve, DV(t, name))
                        for h in range(HG):
                            ins = mm(col(b, h, n), rv[0:n, t, h:h + 1].broadcast_to([n, 128]), ident[0:n, 0:n],
                                     start=True, stop=True)
                    ins.then_inc(g_pe, 1)
                elif stage == "kk":
                    pe.wait_ge(g_dve, DV(t, "gq"))
                    if t:
                        pe.wait_ge(g_act, AC(t, "eq"))
                    for h in range(HG):
                        o = pf[0:n, 512 * b0 + 256 * h:512 * b0 + 256 * h + 256]
                        ins = mm(o.rearrange("p (g t) -> p g t", g=2)[:, :, 0:n], conv4[:, 1, h, cols],
                                 conv4[:, 0:2, h, cols], start=True, stop=True)
                    ins.then_inc(g_pe, 1)
                elif stage[0] == "x":
                    l = int(stage[1:])
                    k = levels(t).index(l)
                    pe.wait_ge(g_pool, PO(t, f"m{l}"))
                    pe.wait_ge(g_dve, DV(t, f"ttf{l // 2}"))
                    for h in range(HG):
                        if l <= 16:
                            ins = mm(ps[:, b0, 32 * h:32 * h + 32], ATm[k % 2][s_][:, h, :], Tc[s_][:, h, :],
                                     start=True, stop=True)
                        else:
                            ins = mm(col(b0, h), ATm[k % 2][s_][:, h, :], Tf[s_][:, h, :], start=True, stop=True)
                    ins.then_inc(g_pe, 1)
                elif stage[0] == "y" and stage != "yt":
                    l = int(stage[1:])
                    pe.wait_ge(g_act, AC(t, f"x{l}"))
                    for h in range(HG):
                        if l <= 16:
                            ins = mm(ps[:, b1, 32 * h:32 * h + 32], TTf[r_][:, h, :], Xc[s_][:, h, :],
                                     start=True, stop=True)
                        else:
                            if l == 32:
                                mm(col(b1, h), TTf[r_][:, h, :], Xf[s_][:, h, :], start=True, stop=True)
                            ins = mm(col(b0 if l == 32 else b1, h), Xf[s_][:, h, :], TTf[r_][:, h, :],
                                     start=True, stop=True)
                    ins.then_inc(g_pe, 1)
                elif stage == "w":
                    pe.wait_ge(g_dve, DV(t, f"ttf{levels(t)[-1]}"))
                    for h in range(HG):
                        ins = mm(col(b0, h, n), kbe[s_][0:n, h, :], TTf[r_][0:n, h, 0:n], start=True, stop=True)
                    ins.then_inc(g_pe, 1)
                elif stage == "v":
                    pe.wait_ge(g_act, AC(t, "w"))
                    if t:
                        pe.wait_ge(g_dve, DV(t - 1, "s"))
                    for h in range(HG):
                        o = ps[0:n, 4, 128 * h:128 * h + 128]
                        ins = mm(o, TTf[r_][0:n, h, 0:n], bv[r_][0:n, h, :], start=True, stop=t == 0)
                        if t:
                            ins = mm(o, wT[r_][:, h, :], S[:, h, :], start=False, stop=True)
                    ins.then_inc(g_pe, 1)
                elif stage == "os":
                    pe.wait_ge(g_dve, DV(t, "vnew"))
                    if t:
                        pe.wait_ge(g_pool, PO(t, "qd"))
                        if t > 1:
                            pe.wait_ge(g_dve, DV(t - 1, "y"))
                        for h in range(HG):
                            mm(col(5, h), qd[r_][:, h, :], S[:, h, :], start=True, stop=False)
                            ins = mm(col(5, h), aq[r_][:, h, :], vnew[:, h, :], start=False, stop=True)
                        ins.then_inc(g_pe, 1)
                    for h in range(HG):
                        ins = mm(col(4, h), kdec[r_][0:n, h, :], vnew[0:n, h, :], start=True, stop=True)
                    ins.then_inc(g_pe, 1)
                elif stage == "yt":
                    pe.wait_ge(s_yc[u % 2], 16 * (u // 2 + 1))
                    pe.wait_ge(g_dve, DV(t, "y"))
                    if t > 1:
                        pe.wait_ge(g_dve, DV(t - 1, "out"))
                    for j in range(8):
                        ins = turn(ps[:, 6 + j // 4, 128 * (j % 4):128 * (j % 4) + 128],
                                   ycat[:, u % 2, 128 * j:128 * j + 128], ident)
                    ins.then_inc(g_pe, 1)
                elif stage[0] == "o":
                    if stage == "o0":
                        if t == 1:
                            pe.wait_ge(s_w[0], 16 * (2 * KD + 3))
                            pe.wait_ge(s_w[1], 16 * 4)
                        pe.wait_ge(g_act, AC(t, "yt"))
                        pe.wait_ge(g_dve, DV(t, "yt"))
                    q = int(stage[1])
                    for k in range(4 * (q % 2), 4 * (q % 2) + 4):
                        ins = mm(ps[:, 6 + q // 2, :], yT[:, k, :], wslot[:, q // 2, k, :], start=k == 0, stop=k == 7)
                    if q == 3:
                        ins.then_inc(g_pe, 1)


_INS = ["x", "meta_tokens", "rel_bias_table", "norm_gain", "w_in", "cq_norm_gain", "ckv_norm_gain", "w_uq", "w_ukv",
        "w_q_idx", "q_norm_gain", "k_norm_gain", "conv_w", "a_log", "dt_bias", "gdn_norm_gain", "w_out", "onehot"]


def kernel(**inputs):
    import concourse.bacc as bacc
    from concourse.bass_utils import run_bass_kernel_spmd

    inputs = dict(inputs, onehot=rel_onehot())
    nc = bacc.Bacc("TRN2", target_bir_lowering=False, num_devices=1)
    arrays, args = {}, []
    for name in _INS:
        arr = np.ascontiguousarray(inputs[name])
        arrays[f"in_{name}"] = arr
        args.append(nc.dram_tensor(f"in_{name}", arr.shape, mybir.dt.from_np(arr.dtype), kind="ExternalInput").ap())
    y = nc.dram_tensor("y", (1, SEQ, D), F32, kind="ExternalOutput").ap()
    hybrid(nc, *args, y)
    r = run_bass_kernel_spmd(nc, [arrays], core_ids=[0])
    return r.results[0]["y"]
```

```python
import math
from contextlib import ExitStack

import concourse.bass as bass
import numpy as np
from concourse import mybir

F32 = mybir.dt.float32
BF16 = mybir.dt.bfloat16
I32 = mybir.dt.int32
ALU = mybir.AluOpType
ACT = mybir.ActivationFunctionType
AX = mybir.AxisListType

D, SEQ, META, EPS = 1024, 1024, 16, 1e-6
T = META + SEQ
HA, DA = 8, 64
HG, DG = 4, 128
HI = 4
TOPK = 256
CONV = 4
NB = SEQ // 128
NT = NB + 1
ROWS = [META] + [128] * NB
OFF = [0] + [META + 128 * i for i in range(NB)]
KEYS = [META + 128 * (i + 1) for i in range(NB)]
SC0 = [sum(KEYS[:i]) for i in range(NB + 1)]
KD = D // 128
NA = 460
CHUNKS = [(0, 272), (272, 656), (656, 1040)]
FILL = -1.0e30
LOWEST = -3.0e38
TOPBITS = 32
N_REL = 32
SKEW = 383


def rel_onehot():
    dist = np.arange(SKEW, dtype=np.int32)[::-1] - 127
    n = np.maximum(dist, 0)
    nf = np.maximum(n, 1).astype(np.float32)
    large = 16 + (np.log(nf / 16) / math.log(128 / 16) * 16).astype(np.int32)
    bucket = np.where(n < 16, n, np.minimum(large, 31))
    out = np.zeros((N_REL, SKEW), np.float32)
    out[bucket, np.arange(SKEW)] += 1.0
    out[N_REL - 1, :] -= 1.0
    return out


LEVELS = [2, 4, 8, 16, 32, 64]
PRE = ["nat", "rb", "kk"] + [f"{c}{l}" for l in LEVELS for c in "xy"] + ["w"]


def levels(t):
    return LEVELS[:3] if t == 0 else LEVELS


REC = [["0v"], ["0os"], ["0o0"], ["0yt", "1v"], ["0c"], ["1os", "0o1"], ["0o2"], ["0o3", "0fin"], ["1o0"], ["1yt"], ["1c"],
       ["1o1"], ["1o2"], ["1o3", "1fin"]]


def rec_stages(tiles):
    return [[(tiles[int(r[0])], r[1:]) for r in line
             if int(r[0]) < len(tiles) and (tiles[int(r[0])] or r[1:] in ("v", "os"))] for line in REC]


def stage_order():
    order, last = [], []
    for tiles in [(0, 1), (2, 3), (4, 5), (6, 7), (8,)]:
        for n, stage in enumerate(PRE):
            order += [(t, stage) for t in tiles if stage[0] not in "xy" or int(stage[1:]) in levels(t)]
            order += last[n] if n < len(last) else []
        last = rec_stages(tiles)
    return order + sum(last, [])


def pe_steps(t, stage):
    return {"nat": ["kn", "vn"], "os": ["o", "s"] if t else ["s"], "o0": [], "o1": [], "o2": [], "o3": ["out"],
            "fin": [], "c": []}.get(stage, [stage])


def dve_steps(t, stage):
    if stage[0] == "y" and stage != "yt":
        l = int(stage[1:])
        return ([f"tc{l}"] + ["tf16"] * (l == 16) + [f"ttc{l}"] if l <= 16 else ["tf32"] * (l == 32)) + [f"ttf{l}"]
    return {"nat": ["kbe", "kdec", "bv"], "rb": ["ga", "gq"],
            "kk": ["at", "aq", "t0", "t1", "t2", "t3", "tc1", "ttc1", "ttf1"], "v": ["vnew"],
            "os": ["s0", "s1", "s2", "s"] if t else ["s"], "yt": ["y0", "y1", "y2", "y"], "c": ["yt"],
            "fin": ["out"]}.get(stage, [])


def act_steps(t, stage):
    if stage[0] == "x":
        return [stage]
    return {"rb": [f"{g}{h}" for g in ("ga", "gq") for h in range(4)] + (["eq"] if t else []), "w": ["w"],
            "os": ["so0", "so1", "so2", "so3", "ln", "ro"] if t else []}.get(stage, [])


def pool_steps(t, stage):
    ls = levels(t)
    if stage == "kk":
        return [f"m{l}" for l in ls[:2]]
    if stage[0] == "x":
        k = ls.index(int(stage[1:])) + 2
        return [f"m{ls[k]}"] if k < len(ls) else []
    return {"rb": ["qd"], "w": ["zg"]}.get(stage, []) if t else []


class Steps:

    def __init__(self, order, steps):
        self.value = {}
        for t, stage in order:
            for name in steps(t, stage):
                assert (t, name) not in self.value
                self.value[t, name] = len(self.value) + 1

    def __call__(self, t, name):
        return self.value[t, name]


def hybrid(nc, x, meta, rel, norm_gain, w_in, g_cq, g_ckv, w_uq, w_ukv, w_qi, g_qn, g_kn, conv_w, a_log,
           dt_bias, g_gdn, w_out, onehot, out):
    ctx = ExitStack()
    with ctx:
        def sb(name, shape, dt=F32):
            return ctx.enter_context(nc.sbuf_tensor(name, shape, dt))

        def sem(name):
            return ctx.enter_context(nc.semaphore(name))

        areaH = sb("areaH", [128, KD * T])
        areaW = sb("areaW", [128, 2 * KD * 512])
        areaC = sb("areaC", [128, 12 * (CONV - 1 + T)])
        areaQ = sb("areaQ", [128, 4 * SEQ + 4 * T + NT * 512])
        scores = sb("scores", [128, SC0[NB]])
        tmp = sb("tmp", [128, 2 * T])
        staging = sb("staging", [128, T])
        zst = staging[:, 0:1024].rearrange("p (s n) -> p s n", s=2)
        junk = sb("junk", [128, T], BF16)

        class Area:
            def __init__(self, ap):
                self.ap, self.at = ap, 0

            def take(self, *shape):
                n = int(np.prod(shape))
                v = self.ap[:, self.at:self.at + n]
                self.at += n
                assert self.at <= self.ap.shape[1], (self.at, self.ap.shape)
                if len(shape) == 2:
                    v = v.rearrange("p (a b) -> p a b", a=shape[0])
                if len(shape) == 3:
                    v = v.rearrange("p (a b c) -> p a b c", a=shape[0], b=shape[1])
                return v

        hT = areaH[:, :].rearrange("p (k t) -> p k t", k=KD)
        wslot = areaW[:, :].rearrange("p (s k n) -> p s k n", s=2, k=KD)

        c = Area(areaC)
        xin = c.take(2, D)
        cn = c.take(2, 512)
        qkn = c.take(2, 1024)
        cT = c.take(3, T)
        kiT = c.take(T)
        wuq = c.take(2, 512)
        wukv = c.take(1024)
        wqi = c.take(2, 256)
        qiT = c.ap[:, 0:2 * SEQ].rearrange("p (m t) -> p m t", m=2)
        sq2 = c.ap[:, 0:1024]
        PADT = CONV - 1 + T
        conv = areaC[:, 0:12 * PADT].rearrange("p (m t) -> p m t", m=12)
        conv4 = areaC[:, 0:12 * PADT].rearrange("p (g h t) -> p g h t", g=3, h=4)

        a = Area(areaQ)
        qT, kT, vN = a.take(4, SEQ), a.take(4, T), a.take(NT, 512)

        a = Area(areaH)
        L = a.take(3, T)
        pT = a.take(2, NT, 128)
        sqk = a.take(D)
        mbn = a.take(2, 256)
        zA = a.take(2, 512)
        diag = a.take(2, 128)
        oA = zst[:, 0, :]

        free = [ar[:, 512 * j:512 * j + 512] for ar in (areaQ[:, :], areaH[:, :], scores[:, :], tmp[:, :],
                                                        staging[:, :])
                for j in range(ar.shape[1] // 512)]

        def blocks(n):
            return [free.pop(0).rearrange("p (h t) -> p h t", h=HG) for _ in range(n)]

        a = Area(areaQ[:, 0:5632])
        del free[0:11]
        zG, ygdn, yT, yA, xres = a.take(2, 512), a.take(2, 512), a.take(4, 128), a.take(2, 4, 128), a.take(2, D)
        kdec, bv, TTf, wT, qd, aq = (blocks(4) for _ in range(6))
        kbe, AT, ATm0, ATm1, Tf, Xf = (blocks(2) for _ in range(6))
        ATm = [ATm0, ATm1]
        compact = [free.pop(0) for _ in range(2)]
        TTc, Tc, Xc = ([b[:, 128 * j:128 * j + 128].rearrange("p (h t) -> p h t", h=HG) for b in compact]
                       for j in range(3))
        vnew, S = blocks(2)
        a = Area(tmp)
        R = a.take(2, T)
        cum = tmp[:, 0:T]
        eqb = tmp[:, T:2 * T].bitcast(BF16)
        eq, drop = eqb[:, 0:T], eqb[:, T:2 * T]
        bias = tmp[:, 0:HA * 256].rearrange("p (h m) -> p h m", h=HA)
        a = Area(sb("scalars", [128, 560])[:, :])
        t1, t2 = a.take(NT, 8), a.take(NT, 8)
        lnb, gg, dec, tot = a.take(NT, 4), a.take(NT, 4), a.take(NT, 4), a.take(NT, 4)
        rv1, rv2, cb = a.take(NT, 4), a.take(NT, 4), a.take(NT, 4)
        skbe, skd, beta, cd = a.take(NT, 4), a.take(NT, 4), a.take(NT, 4), a.take(NT, 4)
        so, ro = a.take(4), a.take(4)

        small = sb("small", [128, 1500])
        s = Area(small)
        ident, triu, ones = s.take(128), s.take(128), s.take(128)
        maskS, maskI = s.take(128), s.take(128)
        ic, negc1 = s.take(32), s.take(32)
        gain = s.take(KD)
        gc = s.take(3)
        gq8, gk = s.take(1), s.take(1)
        epst = s.take(1)
        cw = s.take(CONV, 12)
        alog, dtb = s.take(HG), s.take(HG)
        ggd = s.take(128)
        ss, rx = s.take(NT), s.take(NT)
        st, rc = s.take(2, 2), s.take(2, 2)
        ssk, rk = s.take(2, 16), s.take(2, 16)
        widx = s.take(NT, 4)
        ba = s.take(NT, 8)
        cnt, need = s.take(8), s.take(8)
        mx, nm = s.take(HA * NB, 2), s.take(HA * NB)
        rs = s.take(HA * NB)
        rinv = s.take(2)
        ssq = s.take(NT, 8)
        masks = sb("masks", [128, 7, 128], BF16)
        iw = sb("iw", [128, 6, 8], I32)
        bits, cand, flip, pat, hit = (iw[:, j, :] for j in range(5))
        patf = pat.bitcast(F32)
        relt = sb("relt", [N_REL, HA])
        oneh = zst[:, 0, 0:SKEW]
        rowst = areaC[:, 1024:3072].rearrange("p (s m) -> p s m", s=4)[:, :, 0:SKEW]

        ps = ctx.enter_context(nc.psum_tensor("ps", [128, 8, 512], F32))
        pf = ps[:, :, :].rearrange("p b n -> p (b n)")

        skew_d = nc.dram_tensor("skew_scratch", [HA, 128 * SKEW], F32).ap()
        za_d = nc.dram_tensor("gate_a_scratch", [NB, 128, 4, 128], F32).ap()
        zg_d = nc.dram_tensor("gate_g_scratch", [SEQ, 512], F32).ap()
        oa_d = nc.dram_tensor("attn_scratch", [NB, 128, 512], F32).ap()

        s_gain, s_par, s_small, s_const, s_dconst = sem("gains_in"), sem("params_in"), sem("lat_weights_in"), sem("consts"), sem("dve_consts")
        s_w = [sem("w_in0"), sem("w_in1")]
        s_x = [sem("x_in0"), sem("x_in1")]
        s_rx, s_xn, s_xT, s_hn = sem("x_rstd"), sem("x_scaled"), sem("x_turned"), sem("hT_ready")
        s_al = sem("act_own")
        s_pA, s_rc, s_c1, s_cn, s_cT, s_ceD, s_ceA = (sem(n) for n in (
            "projA_done", "c_rstd", "c_copied", "c_scaled", "c_turned", "cT_ready", "kiT_ready"))
        s_kq, s_kqn, s_kqT, s_kTe, s_qTe, s_v = (sem(n) for n in (
            "kq_done", "kq_scaled", "kq_turned", "kT_ready", "qT_ready", "v_ready"))
        s_qi, s_qie, s_iq, s_relu, s_acc, s_caus = (sem(n) for n in (
            "qi_done", "qiT_ready", "index_dots", "index_relu", "index_scores", "scores_causal"))
        s_tk, s_tl, s_pen, s_mb = sem("topk_steps"), sem("topk_own"), sem("penalty"), sem("penalty_causal")
        s_rb, s_rbe, s_oneh, s_bias = (sem(n) for n in ("bias_rows", "bias_rows_out", "onehot_in", "bias_in"))
        s_sk = [sem(f"skew_written{i}") for i in range(4)]
        s_z, s_ze, s_zo = sem("z_done"), sem("z_ready"), [sem("z_out0"), sem("z_out1")]
        s_ch, s_che, s_pad, s_tap, s_prod, s_cvP, s_cvD, s_cve = (sem(n) for n in (
            "chan_done", "chan_ready", "pads_zero", "conv_first_tap", "conv_products", "conv_sums_pool", "conv_sums_dve", "conv_ready"))
        s_S, s_red, s_far, s_nm, s_P, s_mbn, s_PT, s_PTe, s_o, s_on, s_ri, s_dg = (sem(n) for n in (
            "logits", "row_max", "row_max_far", "neg_max", "probs", "bias_mask", "probs_turned", "probsT_ready",
            "attn_out", "attn_gated", "sum_reciprocal", "sum_diagonal"))
        s_meta = sem("meta_logits_read")
        s_PTa = sem("probsT_ready_act")
        s_za, s_oo = [sem("za_in0"), sem("za_in1")], sem("attn_stored")
        s_sqk, s_ssq, s_gd, s_ga, s_gp = (sem(n) for n in (
            "k_squared", "sumsq_dots", "gates_dve", "gates_act", "gates_pe"))
        g_pe, g_dve, g_act, g_pool = sem("gdn_pe"), sem("gdn_dve"), sem("gdn_act"), sem("gdn_pool")
        s_zg, s_yc, s_xr, s_out = ([sem(f"{n}{i}") for i in range(2)] for n in ("zg_in", "oa_in", "xres_in", "y_out"))
        ORDER = stage_order()
        PE, DV, AC, PO = (Steps(ORDER, f) for f in (pe_steps, dve_steps, act_steps, pool_steps))
        N_CONST, N_DCONST, N_PAR = 22, 5, 16 * 12

        def tok(t):
            return slice(OFF[t], OFF[t] + ROWS[t])

        def per_head(ap, n, width=128, heads=HG):
            return ap.unsqueeze(2).broadcast_to([n, heads, width])

        def all_heads(ap, n, width=128, heads=HG):
            return ap.unsqueeze(1).broadcast_to([n, heads, width])

        def pieces(n):
            return [(j, min(j + 512, n)) for j in range(0, n, 512)]

        def split(i):
            return META if KEYS[i] > 1024 else 0

        def rounds(i):
            tiles = list(range(i + 2))
            return [tiles[j:j + 4] for j in range(0, len(tiles), 4)]

        def copy_round(copy, n, rr, tiles):
            src = ps[:, 6 + rr % 2, :].rearrange("p (k t) -> p k t", k=4)
            if tiles[0] == 0:
                copy(pT[0:META, n % 2, 0, :], src[0:META, 0, :])
                return copy(pT[:, n % 2, 1:len(tiles), :], src[:, 1:len(tiles), :])
            return copy(pT[:, n % 2, tiles[0]:tiles[-1] + 1, :], src[:, 0:len(tiles), :])

        ROUND0 = [0]
        for i in range(NB):
            for h in range(HA):
                ROUND0.append(ROUND0[-1] + len(rounds(i)))

        def turned(r):
            return ((s_PTe, r // 2 + 1) if r % 2 == 0 else (s_PTa, r // 2 + 1))

        zc = 452
        GROUPS = [None, zc, zc + 2048, zc + 512, zc + 1024, zc + 1536, None, None]
        WFREE = {2: (s_pA, NT), 3: (s_z, NB), 4: (s_z, 2 * NB), 5: (s_ch, 12), 6: (s_ch, 24), 7: (s_ch, 36)}
        CONV_POOL = 10

        def conv_sum(m):
            return (s_cvP, 6 * (m + 1)) if m < CONV_POOL else (s_cvD, 3 * (m + 1 - CONV_POOL))

        H2 = T // 2

        def half(k):
            lo = H2 * (k % 2)
            return staging[:, lo:lo + H2], conv[:, 11, 3 + lo:3 + lo + H2]

        GATES = [(2 * t, 2 * t + 1) for t in range(6)] + [(12,), (13,), (14,), (15,)]
        COPIES_FIRST = 4 * HA
        SQ0 = 3 * HA
        G_ABS, G_GG, G_DEC = 5, 8, 21
        G_SSQ, G_CB, G_ALL = 22, 27, 29

        ctx.enter_context(nc.allow_non_contiguous_dma(reason="gains and conv taps, a few KB, go one to a partition"))
        block = ctx.enter_context(nc.Block())

        @block.sync
        def _(sp):
            x2 = x.rearrange("a s d -> (a s) d")

            def load_x(t):
                if t >= 2:
                    sp.wait_ge(s_xT, 2 * (t - 1))
                src = meta if t == 0 else x2[128 * (t - 1):128 * t, :]
                sp.dma_start(xin[0:ROWS[t], t % 2, :], src).then_inc(s_x[t % 2], 16)

            load_x(0)
            load_x(1)
            wv = w_in[0].rearrange("(k p) n -> p k n", p=128)
            for k in range(KD):
                sp.dma_start(wslot[:, 0, k, 0:452], wv[:, k, 0:452]).then_inc(s_w[0], 16)
                sp.dma_start(wslot[:, 0, k, 452:460], wv[:, k, 3012:3020]).then_inc(s_w[0], 16)
            for t in range(2, NT):
                load_x(t)
            sp.dma_start(wuq, w_uq[0].rearrange("(k p) n -> p k n", p=128)).then_inc(s_small, 16)
            sp.dma_start(wukv, w_ukv[0]).then_inc(s_small, 16)
            sp.dma_start(wqi, w_qi[0].rearrange("(k p) n -> p k n", p=128)).then_inc(s_small, 16)

            def load_group(g):
                if g in WFREE:
                    sp.wait_ge(*WFREE[g])
                if g < 6:
                    src = wv[:, :, GROUPS[g]:GROUPS[g] + 512]
                else:
                    src = w_out[0].rearrange("(k p) n -> p k n", p=128)[:, :, 512 * (g - 6):512 * (g - 5)]
                sp.dma_start(wslot[:, g % 2, :, :], src).then_inc(s_w[g % 2], 16)

            load_group(1)
            sp.dma_start(oneh[0:N_REL], onehot).then_inc(s_oneh, 16)
            for h in range(HA):
                sp.wait_ge(s_rbe, h + 1)
                sp.dma_start(skew_d[h].rearrange("(p m) -> p m", p=128), rowst[:, h % 4, :]).then_inc(s_sk[h % 4], 16)
            load_group(2)

            def store_z(g, u):
                n = (g - 1) * NB + u
                sp.wait_ge(s_ze, n + 1)
                if g == 1:
                    m, cc = u // 2, u % 2
                    sp.dma_start(za_d[4 * cc:4 * cc + 4, :, m, :].rearrange("b p t -> p b t"),
                                 zst[:, n % 2, :].rearrange("p (b t) -> p b t", b=4)).then_inc(s_zo[n % 2], 16)
                else:
                    sp.dma_start(zg_d[128 * u:128 * u + 128, :], zst[:, n % 2, :]).then_inc(s_zo[n % 2], 16)

            for u in range(NB):
                store_z(1, u)
            load_group(3)
            for u in range(NB):
                store_z(2, u)
            for g in range(4, 7):
                load_group(g)
            for q in s_sk:
                sp.wait_ge(q, 16 * HA // 4)
            sp.wait_ge(s_pen, NB)
            for h in range(HA):
                src = skew_d[h, 127:127 + 128 * (SKEW - 1)].rearrange("(p m) -> p m", p=128)[:, 0:256]
                sp.dma_start(bias[:, h, :], src).then_inc(s_bias, 16)
            sp.wait_ge(s_zo[0], 16 * NB)
            sp.wait_ge(s_zo[1], 16 * NB)
            load_group(7)
            for i in range(NB):
                if i >= 2:
                    sp.wait_ge(s_on, i - 1)
                sp.dma_start(zA[:, i % 2, :], za_d[i].rearrange("p m t -> p (m t)")).then_inc(s_za[i % 2], 16)
                if i:
                    sp.wait_ge(s_on, i)
                    sp.dma_start(oa_d[i - 1], oA).then_inc(s_oo, 16)
            sp.wait_ge(s_on, NB)
            sp.dma_start(oa_d[NB - 1], oA).then_inc(s_oo, 16)
            sp.wait_ge(s_oo, 16 * NB)

            def store(t):
                u = t - 1
                sp.wait_ge(g_dve, DV(t, "out"))
                sp.dma_start(out[0, 128 * u:128 * u + 128, :], xres[:, u % 2, :]).then_inc(s_out[u % 2], 16)

            for t in range(1, NT):
                u = t - 1
                if u >= 2:
                    store(t - 2)
                    sp.wait_ge(s_out[u % 2], 16 * (u // 2))
                sp.dma_start(zG[:, u % 2, :], zg_d[128 * u:128 * u + 128, :]).then_inc(s_zg[u % 2], 16)
                sp.dma_start(yA[:, u % 2], oa_d[u].rearrange("p (m t) -> p m t", m=4)).then_inc(s_yc[u % 2], 16)
                sp.dma_start(xres[:, u % 2, :], x2[128 * u:128 * u + 128, :]).then_inc(s_xr[u % 2], 16)
            store(NB - 1)
            store(NB)
            for q in s_out:
                sp.wait_ge(q, 16 * (NB // 2))

        @block.gpsimd
        def _(pool):
            par = [
                (gain, norm_gain[0].rearrange("(k p) -> p k", p=128)),
                (gc[:, 0:2], g_cq[0].rearrange("(k p) -> p k", p=128)),
                (gc[:, 2:3], g_ckv[0].rearrange("(k p) -> p k", p=128)),
                (gq8[0:64], g_qn[0].rearrange("(k p) -> p k", p=64)),
                (gq8[64:128], g_qn[0].rearrange("(k p) -> p k", p=64)),
                (gk[0:64], g_kn[0].rearrange("(k p) -> p k", p=64)),
                (gk[64:128], g_kn[0].rearrange("(k p) -> p k", p=64)),
                (alog, a_log[0].partition_broadcast(128)),
                (dtb, dt_bias[0].partition_broadcast(128)),
                (ggd, g_gdn[0].partition_broadcast(128)),
                (relt[:, :], rel),
            ] + [(cw[:, j, :], conv_w[0, j].rearrange("(m p) -> p m", p=128)) for j in range(CONV)]
            for dst, src in par[0:3]:
                pool.dma_start(dst, src).then_inc(s_gain, 16)
            done = [0]

            def link(ins):
                done[0] += 1
                ins.then_inc(s_const, 1)
                pool.wait_ge(s_const, done[0])

            link(nc.gpsimd.memset(ones, 1.0))
            sel = nc.gpsimd.affine_select
            link(nc.gpsimd.memset(ident, 0.0))
            link(sel(out=ident, in_=ident, compare_op=ALU.not_equal, fill=1.0, base=0, pattern=[[-1, 128]],
                     channel_multiplier=1))
            for dst, src in par[3:]:
                pool.dma_start(dst, src).then_inc(s_par, 16)
            link(sel(out=triu, in_=ones, compare_op=ALU.is_ge, fill=0.0, base=0, pattern=[[1, 128]],
                     channel_multiplier=-1))
            link(nc.gpsimd.memset(maskS, 0.0))
            link(sel(out=maskI, in_=maskS, compare_op=ALU.is_ge, fill=FILL, base=0, pattern=[[1, 128]],
                     channel_multiplier=-1))
            link(sel(out=maskS, in_=maskS, compare_op=ALU.is_gt, fill=FILL, base=0, pattern=[[1, 128]],
                     channel_multiplier=-1))
            for n, l in enumerate(LEVELS):
                m = masks[:, n, :].rearrange("p (b f) -> p b f", f=2 * l)
                link(sel(out=m, in_=ones.rearrange("p (b f) -> p b f", f=2 * l), compare_op=ALU.is_ge, fill=0.0,
                         base=0, pattern=[[-2 * l, 128 // (2 * l)], [0, 2 * l]], channel_multiplier=1))
                link(sel(out=m, in_=m, compare_op=ALU.is_ge, fill=0.0, base=l - 1,
                         pattern=[[2 * l, 128 // (2 * l)], [0, 2 * l]], channel_multiplier=-1))
            m = masks[:, 6, :].rearrange("p (b f) -> p b f", f=32)
            link(sel(out=m, in_=ones.rearrange("p (b f) -> p b f", f=32), compare_op=ALU.is_ge, fill=0.0, base=0,
                     pattern=[[-32, 4], [0, 32]], channel_multiplier=1))
            link(sel(out=m, in_=m, compare_op=ALU.is_ge, fill=0.0, base=31, pattern=[[32, 4], [0, 32]],
                     channel_multiplier=-1))
            link(nc.gpsimd.memset(ssq, 1.0))
            assert done[0] == N_CONST, done
            for i in range(1, NB):
                sc = scores[:, SC0[i + 1] - 128:SC0[i + 1]]
                pool.wait_ge(s_acc, HI * i)
                sel(out=sc, in_=sc, compare_op=ALU.is_ge, fill=LOWEST, base=0, pattern=[[-1, 128]],
                    channel_multiplier=1).then_inc(s_caus, 1)
            pool.wait_ge(s_che, 1)
            nc.gpsimd.memset(conv[:, :, 0:3], 0.0).then_inc(s_pad, 1)
            for m in range(CONV_POOL):
                pool.wait_ge(s_tap, m + 1)
                for k in range(2 * (CONV - 1)):
                    pool.wait_ge(s_prod, 6 * m + k + 1)
                    if k >= 2:
                        pool.wait_ge(s_cvP, 6 * m + k - 1)
                    sums, prod = half(k)
                    nc.gpsimd.tensor_tensor(sums, sums, prod, ALU.add).then_inc(s_cvP, 1)
            for i in range(NB):
                sc = scores[:, SC0[i + 1] - 128:SC0[i + 1]]
                pool.wait_ge(s_pen, i + 1)
                sel(out=sc, in_=sc, compare_op=ALU.is_ge, fill=FILL, base=0, pattern=[[-1, 128]],
                    channel_multiplier=1).then_inc(s_mb, 1)
            pool.wait_ge(s_mb, NB)
            pool.wait_ge(s_bias, 16 * HA)
            pool.wait_ge(s_ch, 36)
            for n in range(HA * NB):
                i, h = n // HA, n % HA
                near = 144 if i == 0 else 256
                if n >= 2:
                    pool.wait_ge(s_red, n - 1)
                nc.gpsimd.tensor_tensor(mbn[:, n % 2, 0:near], scores[:, SC0[i + 1] - near:SC0[i + 1]],
                                        bias[:, h, 256 - near:256], ALU.add).then_inc(s_mbn, 1)
                t = (n - SQ0) // 3
                if n >= SQ0 and (n - SQ0) % 3 == 0 and t < NT:
                    if t == 0:
                        pool.wait_ge(s_cve, 12)
                    else:
                        pool.wait_ge(s_ssq, t)
                    v = conv[:, 0:8, 3 + OFF[t]:3 + OFF[t] + ROWS[t]]
                    o = sqk.rearrange("p (m t) -> p m t", m=8)[:, :, 0:ROWS[t]]
                    nc.gpsimd.tensor_tensor(o, v, v, ALU.mult).then_inc(s_sqk, 1)
            pool.wait_ge(s_on, NB)
            pool.wait_ge(s_oo, 16 * NB)

            def mask(t, k):
                l = levels(t)[k]
                nc.gpsimd.tensor_tensor(ATm[k % 2][t % 2], AT[t % 2], all_heads(masks[:, LEVELS.index(l), :], 128),
                                        ALU.mult).then_inc(g_pool, 1)

            for t, stage in ORDER:
                if stage == "rb" and t:
                    pool.wait_ge(g_act, AC(t, "eq"))
                    q = qd[t % 4]
                    nc.gpsimd.tensor_tensor(q, q, conv[:, 0:4, 3 + OFF[t]:3 + OFF[t] + 128],
                                            ALU.mult).then_inc(g_pool, 1)
                if stage == "kk":
                    pool.wait_ge(g_dve, DV(t, "at"))
                    if t >= 2:
                        pool.wait_ge(g_pe, PE(t - 2, f"x{levels(t - 2)[-1]}"))
                    mask(t, 0)
                    mask(t, 1)
                if stage[0] == "x":
                    k = levels(t).index(int(stage[1:]))
                    if k + 2 < len(levels(t)):
                        pool.wait_ge(g_pe, PE(t, stage))
                        mask(t, k + 2)
                if stage == "w" and t:
                    u = t - 1
                    pool.wait_ge(s_zg[u % 2], 16 * (u // 2 + 1))
                    z4 = zG[:, u % 2, :].rearrange("p (h d) -> p h d", h=HG)
                    nc.gpsimd.tensor_tensor(z4, z4, all_heads(ggd, 128), ALU.mult).then_inc(g_pool, 1)

        @block.scalar
        def _(act):
            A = nc.scalar.activation
            own = [0]

            def link(ins):
                own[0] += 1
                ins.then_inc(s_al, 1)
                act.wait_ge(s_al, own[0])

            nc.scalar.preload_act_table_set("natural_log_exp_and_others")
            act.wait_ge(s_dconst, N_DCONST)
            def x_rstd(t):
                n = ROWS[t]
                act.wait_ge(s_x[t % 2], 16 * (t // 2 + 1))
                link(A(junk[0:n, 0:D], xin[0:n, t % 2, :], ACT.Square, accum_out=ss[0:n, t:t + 1]))
                link(A(rx[0:n, t:t + 1], ss[0:n, t:t + 1], ACT.Ln, scale=1.0 / D, bias=epst[0:n]))
                A(rx[0:n, t:t + 1], rx[0:n, t:t + 1], ACT.Exp, scale=-0.5).then_inc(s_rx, 1)

            def latents(t):
                n, b = ROWS[t], 4 + t % 2
                act.wait_ge(s_pA, t + 1)
                if t >= 2:
                    act.wait_ge(s_cT, t - 1)
                    act.wait_ge(s_cn, t - 1)
                A(junk[0:n, 0:256], ps[0:n, b, 0:256], ACT.Square, scale=1 / 16,
                  accum_out=st[0:n, t % 2, 0:1])
                link(A(junk[0:n, 256:384], ps[0:n, b, 256:384], ACT.Square, scale=128 ** -0.5,
                       accum_out=st[0:n, t % 2, 1:2]))
                nc.scalar.copy(cn[0:n, t % 2, 384:448], ps[0:n, b, 384:448])
                nc.scalar.copy(cn[0:n, t % 2, 448:512], ps[0:n, b, 384:448])
                nc.scalar.mul(widx[0:n, t, :], ps[0:n, b, 448:452], (HI * DA) ** -0.5)
                nc.scalar.copy(ba[0:n, t, :], ps[0:n, b, 452:460]).then_inc(s_c1, 1)
                link(A(rc[0:n, t % 2, :], st[0:n, t % 2, :], ACT.Ln, bias=epst[0:n]))
                A(rc[0:n, t % 2, :], rc[0:n, t % 2, :], ACT.Exp, scale=-0.5).then_inc(s_rc, 1)

            for t in range(NT + 3):
                if t < NT:
                    x_rstd(t)
                if 2 <= t < NT + 2:
                    latents(t - 2)
                if t >= 3:
                    act.wait_ge(s_cT, t - 2)
                    nc.scalar.copy(kiT[:, tok(t - 3)], ps[:, 6 + (t - 3) % 2, 384:384 + ROWS[t - 3]]).then_inc(s_ceA, 1)
            g = [0]

            def glink(ins):
                g[0] += 1
                ins.then_inc(s_ga, 1)
                act.wait_ge(s_ga, g[0])

            act.wait_ge(s_gd, G_ABS)
            glink(A(t1, t1, ACT.Exp, scale=-1.0))
            glink(A(t1, t1, ACT.Ln, bias=1.0))
            glink(A(alog, alog, ACT.Exp))
            for n in range(4):
                act.wait_ge(s_qi, n + 1)
                nc.scalar.copy(qiT[:, n // 2, 512 * (n % 2):512 * (n % 2) + 512], ps[:, 6 + n % 2, :]).then_inc(s_qie, 1)
            for n in range(HI * (NB - 1)):
                i = 1 + n // HI
                act.wait_ge(s_iq, n + 1)
                if n >= 2:
                    act.wait_ge(s_acc, n - 1)
                A(R[:, n % 2, 0:KEYS[i]], pf[:, 1536 * (n % 2):1536 * (n % 2) + KEYS[i]], ACT.Relu).then_inc(s_relu, 1)
            for h in range(HA):
                act.wait_ge(s_rb, h + 1)
                if h >= 4:
                    act.wait_ge(s_sk[h % 4], 16)
                nc.scalar.copy(rowst[:, h % 4, :], ps[:, 6 + h % 2, 0:SKEW]).then_inc(s_rbe, 1)
            def norm_kq(t):
                n = ROWS[t]
                act.wait_ge(s_kq, t + 1)
                for h in range(16):
                    ins = A(sq2[0:n, 64 * h:64 * h + 64], pf[0:n, 64 * h:64 * h + 64], ACT.Square, scale=1 / 8,
                            accum_out=ssk[0:n, t % 2, h:h + 1])
                link(ins)
                nc.scalar.copy(vN[0:n, t, :], ps[0:n, 4, :]).then_inc(s_v, 1)
                nc.scalar.preload_act_table_set("natural_log_exp_and_others")
                link(A(rk[0:n, t % 2, :], ssk[0:n, t % 2, :], ACT.Ln, bias=epst[0:n]))
                link(A(rk[0:n, t % 2, :], rk[0:n, t % 2, :], ACT.Exp, scale=-0.5))
                if t >= 2:
                    act.wait_ge(s_kqT, t - 1)
                for h in range(16):
                    ins = A(qkn[0:n, t % 2, 64 * h:64 * h + 64], pf[0:n, 64 * h:64 * h + 64], ACT.Copy,
                            scale=rk[0:n, t % 2, h:h + 1])
                ins.then_inc(s_kqn, 1)

            def gate(n):
                act.wait_ge(s_z, n + 1)
                if n >= 2:
                    act.wait_ge(s_zo[n % 2], 16 * (n // 2))
                A(zst[:, n % 2, :], ps[:, 2 + n % 2, :], ACT.Silu).then_inc(s_ze, 1)

            def turned_kq(t):
                act.wait_ge(s_kqT, t + 1)
                A(kT[:, :, tok(t)], ps[:, 6, :].rearrange("p (h t) -> p h t", h=4)[:, :, 0:ROWS[t]], ACT.Copy,
                  scale=gk).then_inc(s_kTe, 1)
                if t:
                    A(qT[:, :, 128 * (t - 1):128 * t], ps[:, 7, :].rearrange("p (h t) -> p h t", h=4), ACT.Copy,
                      scale=gq8).then_inc(s_qTe, 1)

            for t in range(NT + 1):
                if t < NT:
                    norm_kq(t)
                gate(GATES[t][0])
                if t:
                    turned_kq(t - 1)
                for n in GATES[t][1:]:
                    gate(n)
            def conv_out(m):
                act.wait_ge(*conv_sum(m))
                A(conv[:, m, 3:], staging[:, :], ACT.Silu).then_inc(s_cve, 1)

            for q in s_sk:
                act.wait_ge(q, 16 * HA // 4)
            for m in range(12):
                for j, (lo, hi) in enumerate(CHUNKS):
                    n = 3 * m + j
                    act.wait_ge(s_ch, n + 1)
                    nc.scalar.copy(conv[:, m, 3 + lo:3 + hi], ps[:, n % 4, 0:hi - lo]).then_inc(s_che, 1)
                    if j == 1 and m:
                        conv_out(m - 1)
                if m == 0:
                    act.wait_ge(s_zo[0], 16 * NB)
                    act.wait_ge(s_zo[1], 16 * NB)
                    act.wait_ge(s_pad, 1)
                act.wait_ge(s_che, 3 * m + 3)
                A(staging[:, :], conv[:, m, 0:T], ACT.Copy, scale=cw[:, 0, m:m + 1]).then_inc(s_tap, 1)
                if m < CONV_POOL:
                    for k in range(2 * (CONV - 1)):
                        lo = 1 + k // 2 + H2 * (k % 2)
                        if m or k >= 2:
                            act.wait_ge(s_cvP, 6 * m + k - 1)
                        A(half(k)[1], conv[:, m, lo:lo + H2], ACT.Copy,
                          scale=cw[:, 1 + k // 2, m:m + 1]).then_inc(s_prod, 1)
            def probabilities(n):
                nk = KEYS[n // HA]
                act.wait_ge(s_nm, n + 1)
                A(L[:, n % 3, 0:nk], L[:, n % 3, 0:nk], ACT.Exp, bias=nm[:, n:n + 1],
                  accum_out=rs[:, n:n + 1]).then_inc(s_P, 1)

            def copy_odd_rounds(n):
                for r, tiles in enumerate(rounds(n // HA)):
                    rr = ROUND0[n] + r
                    if rr % 2:
                        act.wait_ge(s_PT, rr + 1)
                        if n >= 2:
                            act.wait_ge(s_o, n - 1)
                        copy_round(nc.scalar.copy, n, rr, tiles).then_inc(s_PTa, 1)

            for m in range(HA * NB + 2):
                if m < COPIES_FIRST:
                    probabilities(m)
                if m >= 2:
                    copy_odd_rounds(m - 2)
                if COPIES_FIRST <= m < HA * NB:
                    probabilities(m)
                if m == 6:
                    conv_out(11)
                    nc.scalar.preload_act_table_set("natural_log_exp_and_others")
                if m == SQ0 + 3 * NT + 2:
                    act.wait_ge(s_gd, G_SSQ)
                    glink(A(ssq, ssq, ACT.Ln, bias=epst))
                if m == SQ0 + 3 * NT + 6:
                    act.wait_ge(s_gd, G_CB)
                    glink(A(skbe, rv1, ACT.Exp))
                    glink(A(skd, t2[:, :, 0:4], ACT.Exp))
                    glink(A(beta, lnb, ACT.Exp))
                    glink(A(cd, tot, ACT.Exp))
            def heads(b):
                return ps[:, b, :].rearrange("p (h t) -> p h t", h=HG)

            for t, stage in ORDER:
                n, s_, r_ = ROWS[t], t % 2, t % 4
                if stage == "rb":
                    for name, buf in (("ga", AT[s_]), ("gq", aq[r_])):
                        act.wait_ge(g_dve, DV(t, name))
                        for h in range(HG):
                            A(buf[0:n, h, 0:n], buf[0:n, h, 0:n], ACT.Exp, bias=cb[0:n, t, h:h + 1]).then_inc(g_act, 1)
                    if t:
                        if t >= 5:
                            act.wait_ge(g_pe, PE(t - 4, "o"))
                        A(qd[r_], heads(2 * s_ + 1), ACT.Exp).then_inc(g_act, 1)
                if stage[0] == "x":
                    act.wait_ge(g_pe, PE(t, stage))
                    if int(stage[1:]) <= 16:
                        nc.scalar.copy(Xc[s_], ps[:, 2 * s_, 0:128].rearrange("p (h t) -> p h t", h=HG)).then_inc(g_act, 1)
                    else:
                        nc.scalar.copy(Xf[s_], heads(2 * s_)).then_inc(g_act, 1)
                if stage == "w":
                    act.wait_ge(g_pe, PE(t, "w"))
                    if t >= 5:
                        act.wait_ge(g_pe, PE(t - 4, "v"))
                    nc.scalar.copy(wT[r_][:, :, 0:n], heads(2 * s_)[:, :, 0:n]).then_inc(g_act, 1)
                if stage == "os" and t:
                    act.wait_ge(g_pe, PE(t, "o"))
                    if t > 1:
                        act.wait_ge(g_dve, DV(t - 1, "y"))
                    for h in range(HG):
                        A(junk[:, 128 * h:128 * h + 128], ps[:, 5, 128 * h:128 * h + 128], ACT.Square,
                          scale=DG ** -0.5, accum_out=so[:, h:h + 1]).then_inc(g_act, 1)
                    act.wait_ge(g_act, AC(t, "so3"))
                    A(ro, so, ACT.Ln, bias=epst).then_inc(g_act, 1)
                    act.wait_ge(g_act, AC(t, "ln"))
                    A(ro, ro, ACT.Exp, scale=-0.5).then_inc(g_act, 1)

        @block.vector
        def _(dve):
            V = nc.vector
            d = [0]

            def dlink(ins):
                d[0] += 1
                ins.then_inc(s_dconst, 1)
                dve.wait_ge(s_dconst, d[0])

            dlink(V.memset(epst, EPS))
            dlink(V.memset(ba, 0.0))
            dlink(V.memset(junk[:, :], 0.0))
            dlink(V.memset(bits, 0))
            dlink(V.memset(cand, 0))
            def scale_x(t):
                n = ROWS[t]
                dve.wait_ge(s_rx, t + 1)
                V.tensor_scalar(xin[0:n, t % 2, :], xin[0:n, t % 2, :], rx[0:n, t:t + 1], None, ALU.mult).then_inc(s_xn, 1)

            def h_turned(t):
                n = ROWS[t]
                for b in range(2):
                    dve.wait_ge(s_xT, 2 * t + b + 1)
                    bank = ps[:, 2 * (t % 2) + b, :].rearrange("p (k t) -> p k t", k=4)[:, :, 0:n]
                    V.tensor_tensor(hT[:, 4 * b:4 * b + 4, tok(t)], bank, per_head(gain[:, 4 * b:4 * b + 4], 128, n, 4),
                                    ALU.mult).then_inc(s_hn, 1)

            def scale_c(t):
                n, b = ROWS[t], 4 + t % 2
                dve.wait_ge(s_rc, t + 1)
                if t >= 2:
                    dve.wait_ge(s_cT, t - 1)
                V.tensor_scalar(cn[0:n, t % 2, 0:256], ps[0:n, b, 0:256], rc[0:n, t % 2, 0:1], None, ALU.mult)
                V.tensor_scalar(cn[0:n, t % 2, 256:384], ps[0:n, b, 256:384], rc[0:n, t % 2, 1:2], None,
                                ALU.mult).then_inc(s_cn, 1)

            def c_turned(t):
                n = ROWS[t]
                dve.wait_ge(s_cT, t + 1)
                dve.wait_ge(s_ceA, t + 1)
                src = ps[:, 6 + t % 2, 0:384].rearrange("p (k t) -> p k t", k=3)[:, :, 0:n]
                V.tensor_tensor(cT[:, :, tok(t)], src, per_head(gc, 128, n, 3), ALU.mult).then_inc(s_ceD, 1)

            for t in range(NT + 3):
                if t < NT:
                    scale_x(t)
                if t == 1:
                    dve.wait_ge(s_gain, 48)
                if 1 <= t <= NT:
                    h_turned(t - 1)
                if 2 <= t < NT + 2:
                    scale_c(t - 2)
                if t >= 3:
                    c_turned(t - 3)
            dve.wait_ge(s_par, N_PAR)
            V.tensor_scalar(gq8, gq8, DA ** -0.5, None, ALU.mult).then_inc(s_tl, 1)
            dve.wait_ge(s_tl, 1)
            g = [0]

            def glink(ins):
                g[0] += 1
                ins.then_inc(s_gd, 1)
                dve.wait_ge(s_gd, g[0])

            dve.wait_ge(s_c1, NT)
            glink(V.tensor_tensor(t2[:, :, 4:8], ba[:, :, 4:8], all_heads(dtb, 128, 4, NT), ALU.add))
            glink(V.tensor_scalar(t2[:, :, 0:4], ba[:, :, 0:4], -1.0, None, ALU.mult))
            glink(V.tensor_scalar(t1, t2, -1.0, None, ALU.mult))
            glink(V.tensor_tensor(t1, t1, t2, ALU.max))
            glink(V.tensor_scalar(t2, t2, 0.0, None, ALU.max))
            assert g[0] == G_ABS
            dve.wait_ge(s_ga, 3)
            glink(V.tensor_tensor(t1, t1, t2, ALU.add))
            glink(V.tensor_scalar(lnb, t1[:, :, 0:4], -1.0, None, ALU.mult))
            glink(V.scalar_tensor_tensor(gg, t1[:, :, 4:8], -1.0, all_heads(alog, 128, 4, NT), ALU.mult, ALU.mult))
            assert g[0] == G_GG
            dve.wait_ge(s_const, N_CONST)
            glink(V.memset(ic, 0.0))
            for b in range(4):
                rows = slice(32 * b, 32 * b + 32)
                glink(V.tensor_copy(ic[rows], ident[rows, 32 * b:32 * b + 32]))
            for n, l in enumerate(LEVELS):
                m = masks[:, n, :].rearrange("p (b c f) -> p b c f", c=2, f=l)
                glink(V.memset(m[:, :, 0, :], 0.0))
            glink(V.memset(negc1, 0.0))
            V.tensor_scalar(negc1.rearrange("p (b c) -> p b c", c=2)[:, :, 1],
                            ic.rearrange("p (b c) -> p b c", c=2)[:, :, 0], -1.0, None, ALU.mult)
            dve.wait_ge(s_gp, 1)
            p1 = ps[:, 5, 0:8 * NT].rearrange("p (c t h) -> p c t h", c=2, h=4)
            V.tensor_copy(dec, p1[:, 0])
            glink(V.tensor_copy(tot, p1[:, 1]))
            assert g[0] == G_DEC, g
            for n in range(HI * (NB - 1)):
                i, h = 1 + n // HI, n % HI
                sc = scores[:, SC0[i]:SC0[i] + KEYS[i]]
                dve.wait_ge(s_relu, n + 1)
                if h == 0:
                    V.tensor_scalar(sc, R[:, n % 2, 0:KEYS[i]], widx[:, i + 1, h:h + 1], None,
                                    ALU.mult).then_inc(s_acc, 1)
                else:
                    dve.wait_ge(s_acc, n)
                    V.scalar_tensor_tensor(sc, R[:, n % 2, 0:KEYS[i]], widx[:, i + 1, h:h + 1], sc, ALU.mult,
                                           ALU.add).then_inc(s_acc, 1)
            NI = NB - 1
            dve.wait_ge(s_caus, NI)
            base = 1
            U, B = iw[:, 5, 0:NI], bits[:, 0:NI]
            V.memset(U, 0).then_inc(s_tl, 1)
            V.memset(B, -2 ** 31).then_inc(s_tl, 1)
            dve.wait_ge(s_tl, base + 2)
            PER = 6 + NI
            with dve.Fori(0, TOPBITS) as it:
                cd_, fl, pt, ht = (v[:, 0:NI] for v in (cand, flip, pat, hit))
                V.tensor_tensor(cd_, U, B, ALU.bitwise_or).then_inc(s_tk, 1)
                dve.wait_ge(s_tk, it * PER + 1)
                V.tensor_scalar(fl, cd_, 31, -1, ALU.arith_shift_right, ALU.bitwise_xor).then_inc(s_tk, 1)
                dve.wait_ge(s_tk, it * PER + 2)
                V.scalar_tensor_tensor(pt, fl, -2 ** 31, cd_, ALU.bitwise_or, ALU.bitwise_xor).then_inc(s_tk, 1)
                dve.wait_ge(s_tk, it * PER + 3)
                for i in range(1, NB):
                    V.tensor_scalar(junk[:, 0:KEYS[i]], scores[:, SC0[i]:SC0[i] + KEYS[i]],
                                    patf[:, i - 1:i], 0.0, ALU.is_ge, ALU.add,
                                    accum_out=cnt[:, i - 1:i]).then_inc(s_tk, 1)
                    dve.wait_ge(s_tk, it * PER + 3 + i)
                V.tensor_scalar(ht, cnt[:, 0:NI], float(TOPK), -1.0, ALU.is_ge, ALU.mult).then_inc(s_tk, 1)
                V.tensor_scalar(B, B, 1, None, ALU.logical_shift_right)
                dve.wait_ge(s_tk, it * PER + 4 + NI)
                V.tensor_tensor(ht, ht, cd_, ALU.bitwise_and).then_inc(s_tk, 1)
                dve.wait_ge(s_tk, it * PER + 5 + NI)
                V.tensor_tensor(U, U, ht, ALU.bitwise_or).then_inc(s_tk, 1)
                dve.wait_ge(s_tk, it * PER + 6 + NI)
            V.tensor_scalar(flip[:, 0:NI], U, 31, -1, ALU.arith_shift_right, ALU.bitwise_xor).then_inc(s_tl, 1)
            dve.wait_ge(s_tl, base + 3)
            V.scalar_tensor_tensor(pat[:, 0:NI], flip[:, 0:NI], -2 ** 31, U, ALU.bitwise_or,
                                   ALU.bitwise_xor).then_inc(s_tl, 1)
            dve.wait_ge(s_tl, base + 4)
            for i in range(1, NB):
                V.tensor_scalar(junk[:, 0:KEYS[i]], scores[:, SC0[i]:SC0[i] + KEYS[i]], patf[:, i - 1:i], 0.0,
                                ALU.is_gt, ALU.add, accum_out=cnt[:, i - 1:i]).then_inc(s_tl, 1)
                dve.wait_ge(s_tl, base + 4 + i)
            base += NI - 1
            V.tensor_scalar(need[:, 0:NI], cnt[:, 0:NI], -1.0, float(TOPK), ALU.mult, ALU.add).then_inc(s_tl, 1)
            V.memset(scores[:, 0:KEYS[0]], 0.0).then_inc(s_pen, 1)
            dve.wait_ge(s_tl, base + 6)
            k = base + 6
            for i in range(1, NB):
                sc, thr, nk = scores[:, SC0[i]:SC0[i] + KEYS[i]], patf[:, i - 1:i], KEYS[i]
                V.tensor_scalar(eq[:, 0:nk], sc, thr, None, ALU.is_equal).then_inc(s_tl, 1)
                dve.wait_ge(s_tl, k + 1)
                V.tensor_tensor_scan(cum[:, 0:nk], eq[:, 0:nk], junk[:, 0:nk], 0.0, ALU.add,
                                     ALU.bypass).then_inc(s_tl, 1)
                dve.wait_ge(s_tl, k + 2)
                V.scalar_tensor_tensor(drop[:, 0:nk], cum[:, 0:nk], need[:, i - 1:i], eq[:, 0:nk], ALU.is_gt,
                                       ALU.mult).then_inc(s_tl, 1)
                dve.wait_ge(s_tl, k + 3)
                V.scalar_tensor_tensor(sc, sc, thr, drop[:, 0:nk], ALU.is_ge, ALU.subtract).then_inc(s_tl, 1)
                dve.wait_ge(s_tl, k + 4)
                k += 4
                V.tensor_scalar(sc, sc, -1.0, -FILL, ALU.add, ALU.mult).then_inc(s_pen, 1)
            def conv_tap(m, j):
                dve.wait_ge(s_tap, m + 1)
                if j > 1:
                    dve.wait_ge(s_cvD, 3 * (m - CONV_POOL) + j - 1)
                V.scalar_tensor_tensor(staging[:, :], conv[:, m, j:j + T], cw[:, j, m:m + 1], staging[:, :],
                                       ALU.mult, ALU.add).then_inc(s_cvD, 1)

            for m in range(CONV_POOL, 11):
                for j in range(1, CONV):
                    conv_tap(m, j)
            dve.wait_ge(s_ch, 36)
            dve.wait_ge(s_mb, NB)
            def logits(n):
                i, h = n // HA, n % HA
                near = 144 if i == 0 else 256
                far = KEYS[i] - near
                lg = pf[:, 1536 * (n % 2):1536 * (n % 2) + KEYS[i]]
                dve.wait_ge(s_S, n + 1)
                if n >= 3:
                    dve.wait_ge(s_PT, ROUND0[n - 2])
                first, lo0 = LOWEST, split(i)
                if lo0:
                    V.tensor_tensor_reduce(L[:, n % 3, 0:lo0], ps[:, 2, 0:lo0], scores[:, SC0[i]:SC0[i] + lo0],
                                           1.0, first, ALU.add, ALU.max, mx[:, n, 1:2]).then_inc(s_meta, 1)
                    dve.wait_ge(s_meta, h + 1)
                    first = mx[:, n, 1:2]
                if far:
                    V.tensor_tensor_reduce(L[:, n % 3, lo0:far], lg[:, 0:far - lo0],
                                           scores[:, SC0[i] + lo0:SC0[i] + far],
                                           1.0, first, ALU.add, ALU.max, mx[:, n, 0:1]).then_inc(s_far, 1)
                    dve.wait_ge(s_far, n + 1 - HA)
                    first = mx[:, n, 0:1]
                dve.wait_ge(s_mbn, n + 1)
                V.tensor_tensor_reduce(L[:, n % 3, far:KEYS[i]], lg[:, far - lo0:KEYS[i] - lo0], mbn[:, n % 2, 0:near],
                                       1.0, first, ALU.add, ALU.max, mx[:, n, 1:2]).then_inc(s_red, 1)
                dve.wait_ge(s_red, n + 1)
                V.tensor_scalar(nm[:, n:n + 1], mx[:, n, 1:2], -1.0, None, ALU.mult).then_inc(s_nm, 1)

            def copy_even_rounds(n):
                for r, tiles in enumerate(rounds(n // HA)):
                    rr = ROUND0[n] + r
                    if rr % 2 == 0:
                        dve.wait_ge(s_PT, rr + 1)
                        if n >= 2:
                            dve.wait_ge(s_o, n - 1)
                        copy_round(V.tensor_copy, n, rr, tiles).then_inc(s_PTe, 1)

            def gate_block(i):
                dve.wait_ge(s_o, HA * (i + 1))
                dve.wait_ge(s_za[i % 2], 16 * (i // 2 + 1))
                if i:
                    dve.wait_ge(s_oo, 16 * i)
                else:
                    dve.wait_ge(s_cve, 12)
                V.tensor_tensor(oA, ps[:, 5, :], zA[:, i % 2, :], ALU.mult).then_inc(s_on, 1)

            def sums(n):
                dve.wait_ge(s_P, n + 1)
                if n >= 2:
                    dve.wait_ge(s_PT, ROUND0[n - 1])
                V.reciprocal(rinv[:, n % 2:n % 2 + 1], rs[:, n:n + 1]).then_inc(s_ri, 1)
                dve.wait_ge(s_ri, n + 1)
                V.tensor_scalar(diag[:, n % 2, :], ident, rinv[:, n % 2:n % 2 + 1], None, ALU.mult).then_inc(s_dg, 1)

            for m in range(HA * NB + 3):
                if m < COPIES_FIRST:
                    logits(m)
                if 1 <= m <= HA * NB:
                    sums(m - 1)
                if 2 <= m < HA * NB + 2:
                    copy_even_rounds(m - 2)
                if COPIES_FIRST <= m < HA * NB:
                    logits(m)
                if 1 <= m < CONV:
                    conv_tap(11, m)
                if m >= 3 and (m - 3) % HA == HA - 1:
                    gate_block((m - 3) // HA)
                if m == SQ0 + 3 * NT + 1:
                    dve.wait_ge(s_ssq, NT)
                    V.tensor_copy(ssq[0:META, 0, :], ps[0:META, 2, 0:8])
                    glink(V.tensor_copy(ssq[:, 1:, :], ps[:, 2, 8:8 * NT].rearrange("p (t c) -> p t c", c=8)))
                    assert g[0] == G_SSQ, g
                if m == SQ0 + 3 * NT + 4:
                    dve.wait_ge(s_ga, 4)
                    glink(V.scalar_tensor_tensor(rv1, ssq[:, :, 4:8], -0.5, dec, ALU.mult, ALU.add))
                    glink(V.tensor_tensor(rv1, rv1, lnb, ALU.add))
                    V.scalar_tensor_tensor(rv2, ssq[:, :, 0:4], -0.5, dec, ALU.mult, ALU.add)
                    glink(V.scalar_tensor_tensor(cb, ssq[:, :, 4:8], -0.5, dec, ALU.mult, ALU.subtract))
                    glink(V.tensor_scalar(rv2, rv2, -0.5 * math.log(DG), None, ALU.add))
                    glink(V.tensor_tensor(t2[:, :, 0:4], cb, tot, ALU.add))
                    assert g[0] == G_CB, g
                if m == SQ0 + 3 * NT + 8:
                    dve.wait_ge(s_ga, 8)
                    glink(V.tensor_scalar(skbe, skbe, -1.0, None, ALU.mult))
            glink(V.memset(AT[0], 0.0))
            assert g[0] == G_ALL, g

            def bank(b):
                return ps[:, b, :].rearrange("p (h t) -> p h t", h=HG)

            def flat(ap):
                return ap.rearrange("p h t -> p (h t)")

            bd32 = masks[:, 6, :].rearrange("p (b t) -> p b t", b=4).unsqueeze(1).broadcast_to([128, HG, 4, 32])

            def spread(dst, src):
                return V.tensor_tensor(dst.rearrange("p h (b t) -> p h b t", b=4),
                                       src.unsqueeze(2).broadcast_to([128, HG, 4, 32]), bd32, ALU.mult)

            def norm_keys(t):
                n, s_, r_ = ROWS[t], t % 2, t % 4
                dve.wait_ge(g_pe, PE(t, "kn"))
                if t >= 4:
                    dve.wait_ge(g_pe, PE(t - 4, "s"))
                V.tensor_tensor(kbe[s_][0:n], bank(2 * s_)[0:n], per_head(skbe[0:n, t], n), ALU.mult).then_inc(g_dve, 1)
                V.tensor_tensor(kdec[r_][0:n], bank(2 * s_)[0:n], per_head(skd[0:n, t], n), ALU.mult).then_inc(g_dve, 1)
                dve.wait_ge(g_pe, PE(t, "vn"))
                V.tensor_tensor(bv[r_][0:n], bank(2 * s_ + 1)[0:n], per_head(beta[0:n, t], n), ALU.mult).then_inc(g_dve, 1)

            def exponents(t):
                n, s_, r_ = ROWS[t], t % 2, t % 4
                dve.wait_ge(g_pe, PE(t, "rb"))
                if t >= 2:
                    dve.wait_ge(g_pool, PO(t - 2, f"m{levels(t - 2)[-1]}"))
                V.tensor_tensor(AT[s_][0:n, :, 0:n], bank(2 * s_)[0:n, :, 0:n], all_heads(maskS[0:n, 0:n], n, n),
                                ALU.add).then_inc(g_dve, 1)
                V.tensor_tensor(aq[r_][0:n, :, 0:n], bank(2 * s_ + 1)[0:n, :, 0:n], all_heads(maskI[0:n, 0:n], n, n),
                                ALU.add).then_inc(g_dve, 1)

            def products(t):
                n, s_, r_ = ROWS[t], t % 2, t % 4
                kk = pf[0:n, 1024 * s_:1024 * s_ + 1024].rearrange("p (h g t) -> p h g t", h=HG, g=2)
                at, q = AT[s_], aq[r_]
                dve.wait_ge(g_pe, PE(t, "kk"))
                dve.wait_ge(g_act, AC(t, "gq3"))
                V.tensor_tensor(at[0:n, :, 0:n], kk[:, :, 1, 0:n], at[0:n, :, 0:n], ALU.mult).then_inc(g_dve, 1)
                V.tensor_tensor(q[0:n, :, 0:n], kk[:, :, 0, 0:n], q[0:n, :, 0:n], ALU.mult).then_inc(g_dve, 1)
                dve.wait_ge(g_dve, DV(t, "at"))
                for b in range(4):
                    rows = slice(32 * b, 32 * b + 32)
                    V.tensor_tensor(TTc[s_][rows], at[rows, :, 32 * b:32 * b + 32], all_heads(negc1[rows], 32, 32),
                                    ALU.mult).then_inc(g_dve, 1)
                dve.wait_ge(g_dve, DV(t, "t3"))
                V.tensor_tensor(TTc[s_], TTc[s_], all_heads(ic, 128, 32), ALU.add).then_inc(g_dve, 1)
                dve.wait_ge(g_dve, DV(t, "tc1"))
                V.transpose(flat(Tc[s_]), flat(TTc[s_])).then_inc(g_dve, 1)
                spread(TTf[r_], TTc[s_]).then_inc(g_dve, 1)

            def merge(t, l):
                s_, r_ = t % 2, t % 4
                dve.wait_ge(g_pe, PE(t, f"y{l}"))
                if l <= 16:
                    V.tensor_tensor(Tc[s_], Tc[s_], ps[:, 2 * s_ + 1, 0:128].rearrange("p (h t) -> p h t", h=HG),
                                    ALU.subtract).then_inc(g_dve, 1)
                    dve.wait_ge(g_dve, DV(t, f"tc{l}"))
                    if l == 16:
                        spread(Tf[s_], Tc[s_]).then_inc(g_dve, 1)
                    V.transpose(flat(TTc[s_]), flat(Tc[s_])).then_inc(g_dve, 1)
                    dve.wait_ge(g_dve, DV(t, f"ttc{l}"))
                    spread(TTf[r_], TTc[s_]).then_inc(g_dve, 1)
                else:
                    if l == 32:
                        V.tensor_tensor(Tf[s_], Tf[s_], bank(2 * s_ + 1), ALU.subtract).then_inc(g_dve, 1)
                    b = 2 * s_ if l == 32 else 2 * s_ + 1
                    V.tensor_tensor(TTf[r_], TTf[r_], bank(b), ALU.subtract).then_inc(g_dve, 1)

            def state(t):
                dve.wait_ge(g_pe, PE(t, "s"))
                if t == 0:
                    V.tensor_copy(S, bank(4)).then_inc(g_dve, 1)
                    return
                for h in range(HG):
                    V.scalar_tensor_tensor(S[:, h, :], S[:, h, :], cd[:, t, h:h + 1], bank(4)[:, h, :], ALU.mult,
                                           ALU.add).then_inc(g_dve, 1)

            def gate_tile(t):
                u = t - 1
                dve.wait_ge(g_act, AC(t, "ro"))
                dve.wait_ge(g_pool, PO(t, "zg"))
                if u >= 2:
                    dve.wait_ge(g_pe, PE(t - 2, "yt"))
                for h in range(HG):
                    V.scalar_tensor_tensor(ygdn[:, u % 2, 128 * h:128 * h + 128], bank(5)[:, h, :],
                                           ro[:, h:h + 1], zG[:, u % 2, 128 * h:128 * h + 128], ALU.mult,
                                           ALU.mult).then_inc(g_dve, 1)

            for t, stage in ORDER:
                u = t - 1
                if stage == "nat":
                    norm_keys(t)
                elif stage == "rb":
                    exponents(t)
                elif stage == "kk":
                    products(t)
                elif stage == "v":
                    dve.wait_ge(g_pe, PE(t, "v"))
                    V.tensor_copy(vnew[0:ROWS[t]], bank(4)[0:ROWS[t]]).then_inc(g_dve, 1)
                elif stage == "os":
                    state(t)
                elif stage == "yt":
                    gate_tile(t)
                elif stage[0] == "y":
                    merge(t, int(stage[1:]))
                elif stage == "c":
                    dve.wait_ge(g_pe, PE(t, "yt"))
                    V.tensor_copy(yT, bank(7)).then_inc(g_dve, 1)
                elif stage == "fin":
                    dve.wait_ge(g_pe, PE(t, "out"))
                    dve.wait_ge(s_xr[u % 2], 16 * (u // 2 + 1))
                    V.tensor_tensor(xres[:, u % 2, :], pf[:, 3072:4096], xres[:, u % 2, :], ALU.add).then_inc(g_dve, 1)

        @block.tensor
        def _(pe):
            mm, turn = nc.tensor.matmul, nc.tensor.transpose
            pe.wait_ge(s_const, 3)

            def turn_x(t):
                n = ROWS[t]
                pe.wait_ge(s_xn, t + 1)
                for b in range(2):
                    if t >= 2:
                        pe.wait_ge(s_hn, 2 * (t - 2) + b + 1)
                    for k in range(4):
                        ins = turn(ps[:, 2 * (t % 2) + b, 128 * k:128 * k + n],
                                   xin[0:n, t % 2, 128 * (4 * b + k):128 * (4 * b + k + 1)], ident[0:n, 0:n])
                    ins.then_inc(s_xT, 1)

            def proj_a(t):
                n, b = ROWS[t], 4 + t % 2
                pe.wait_ge(s_hn, 2 * (t + 1))
                if t == 0:
                    pe.wait_ge(s_w[0], 16 * 2 * KD)
                if t >= 2:
                    pe.wait_ge(s_c1, t - 1)
                    pe.wait_ge(s_cn, t - 1)
                for k in range(KD):
                    ins = mm(ps[0:n, b, 0:NA], hT[:, k, tok(t)], wslot[:, 0, k, 0:NA], start=k == 0, stop=k == KD - 1)
                ins.then_inc(s_pA, 1)

            def turn_c(t):
                n = ROWS[t]
                pe.wait_ge(s_cn, t + 1)
                pe.wait_ge(s_c1, t + 1)
                if t >= 2:
                    pe.wait_ge(s_ceD, t - 1)
                    pe.wait_ge(s_ceA, t - 1)
                for k in range(4):
                    ins = turn(ps[:, 6 + t % 2, 128 * k:128 * k + n], cn[0:n, t % 2, 128 * k:128 * k + 128],
                               ident[0:n, 0:n])
                ins.then_inc(s_cT, 1)

            for t in range(NT + 2):
                if t < NT:
                    turn_x(t)
                if 1 <= t <= NT:
                    proj_a(t - 1)
                if t >= 2:
                    turn_c(t - 2)
            pe.wait_ge(s_ceD, NT)
            pe.wait_ge(s_ceA, NT)
            pe.wait_ge(s_const, N_CONST)
            pe.wait_ge(s_small, 48)
            for n in range(4):
                m, cc = n // 2, n % 2
                if n >= 2:
                    pe.wait_ge(s_qie, n - 1)
                for k in range(2):
                    ins = mm(ps[:, 6 + n % 2, :], wqi[:, k, 128 * m:128 * m + 128],
                             cT[:, k, META + 512 * cc:META + 512 * cc + 512], start=k == 0, stop=k == 1)
                ins.then_inc(s_qi, 1)
            pe.wait_ge(s_gd, G_GG)
            for cidx, m in ((0, triu), (1, ones)):
                o = ps[:, 5, 36 * cidx:36 * cidx + 36].rearrange("p (t h) -> p t h", h=4)
                mm(o[:, 0, :], m[0:META, :], gg[0:META, 0, :], start=True, stop=True)
                ins = mm(o[:, 1:, :], m, gg[:, 1:, :], start=True, stop=True)
            ins.then_inc(s_gp, 1)
            pe.wait_ge(s_qie, 4)
            pe.wait_ge(s_gd, G_DEC)
            for n in range(HI * (NB - 1)):
                i, h = 1 + n // HI, n % HI
                if n >= 2:
                    pe.wait_ge(s_relu, n - 1)
                r = slice(64 * (h % 2), 64 * (h % 2) + 64)
                for lo, hi in pieces(KEYS[i]):
                    ins = mm(pf[:, 1536 * (n % 2) + lo:1536 * (n % 2) + hi], qiT[r, h // 2, 128 * i:128 * i + 128],
                             kiT[r, lo:hi], start=True, stop=True)
                ins.then_inc(s_iq, 1)
            pe.wait_ge(s_oneh, 16)
            pe.wait_ge(s_par, N_PAR)
            for h in range(HA):
                if h >= 2:
                    pe.wait_ge(s_rbe, h - 1)
                mm(ps[:, 6 + h % 2, 0:SKEW], relt[:, h:h + 1].broadcast_to([N_REL, 128]), oneh[0:N_REL],
                   start=True, stop=True).then_inc(s_rb, 1)
            pe.wait_ge(s_relu, HI * (NB - 1))
            pe.wait_ge(s_rbe, HA)

            def up(t):
                n = ROWS[t]
                if t:
                    pe.wait_ge(s_kqn, t)
                    pe.wait_ge(s_v, t)
                mm(ps[0:n, 0, :], cT[:, 2, tok(t)], wukv[:, 0:512], start=True, stop=True)
                for k in range(2):
                    mm(ps[0:n, 1, :], cT[:, k, tok(t)], wuq[:, k, :], start=k == 0, stop=k == 1)
                mm(ps[0:n, 4, :], cT[:, 2, tok(t)], wukv[:, 512:1024], start=True, stop=True).then_inc(s_kq, 1)

            def turn_kq(t):
                n = ROWS[t]
                pe.wait_ge(s_kqn, t + 1)
                if t >= 1:
                    pe.wait_ge(s_kTe, t)
                if t >= 2:
                    pe.wait_ge(s_qTe, t - 1)
                for j in range(8 if t else 4):
                    ins = turn(ps[:, 6 + j // 4, 128 * (j % 4):128 * (j % 4) + n],
                               qkn[0:n, t % 2, 128 * j:128 * j + 128], ident[0:n, 0:n])
                ins.then_inc(s_kqT, 1)

            def gate(n):
                g, u = 1 + n // NB, n % NB
                if u == 0:
                    pe.wait_ge(s_w[g % 2], 16 if g == 1 else 16 * (2 * KD + 1))
                if n >= 2:
                    pe.wait_ge(s_ze, n - 1)
                for k in range(KD):
                    m, cc = u // 2, u % 2
                    w, hh = ((wslot[:, 1, k, 128 * m:128 * m + 128], hT[:, k, META + 512 * cc:META + 512 * cc + 512])
                             if g == 1 else (hT[:, k, tok(u + 1)], wslot[:, 0, k, :]))
                    ins = mm(ps[:, 2 + n % 2, :], w, hh, start=k == 0, stop=k == KD - 1)
                ins.then_inc(s_z, 1)

            for t in range(NT + 1):
                if t < NT:
                    up(t)
                gate(GATES[t][0])
                if t:
                    turn_kq(t - 1)
                for n in GATES[t][1:]:
                    gate(n)
            pe.wait_ge(s_ze, 2 * NB)
            pe.wait_ge(s_kTe, NT)
            pe.wait_ge(s_qTe, NB)
            for n in range(36):
                g, m, (lo, hi) = 3 + n // 12, n // 3 % 4, CHUNKS[n % 3]
                if n % 12 == 0:
                    pe.wait_ge(s_w[g % 2], {3: 32, 4: 16 * (2 * KD + 2), 5: 48}[g])
                if n >= 4:
                    pe.wait_ge(s_che, n - 3)
                for k in range(KD):
                    ins = mm(ps[:, n % 4, 0:hi - lo], wslot[:, g % 2, k, 128 * m:128 * m + 128], hT[:, k, lo:hi],
                             start=k == 0, stop=k == KD - 1)
                ins.then_inc(s_ch, 1)
            pe.wait_ge(s_che, 36)

            def dots(n):
                i, h = n // HA, n % HA
                if n >= 2:
                    pe.wait_ge(s_red, n - 1)
                if n == HA * (NB - 1):
                    pe.wait_ge(s_gd, G_SSQ)
                r = slice(64 * (h % 2), 64 * (h % 2) + 64)
                lo0 = split(i)
                for lo, hi in pieces(KEYS[i] - lo0):
                    ins = mm(pf[:, 1536 * (n % 2) + lo:1536 * (n % 2) + hi], qT[r, h // 2, 128 * i:128 * i + 128],
                             kT[r, h // 2, lo0 + lo:lo0 + hi], start=True, stop=True)
                if lo0:
                    if h:
                        pe.wait_ge(s_meta, h)
                    ins = mm(ps[:, 2, 0:META], qT[r, h // 2, 128 * i:128 * i + 128], kT[r, h // 2, 0:META],
                             start=True, stop=True)
                ins.then_inc(s_S, 1)

            def turn_p(n):
                i = n // HA
                pe.wait_ge(s_dg, n + 1)
                for r, tiles in enumerate(rounds(i)):
                    rr = ROUND0[n] + r
                    if rr >= 2:
                        pe.wait_ge(*turned(rr - 2))
                    for j, kt in enumerate(tiles):
                        ins = mm(ps[0:ROWS[kt], 6 + rr % 2, 128 * j:128 * j + 128], L[:, n % 3, tok(kt)],
                                 diag[:, n % 2, :], start=True, stop=True)
                    ins.then_inc(s_PT, 1)

            def weigh(n):
                i, h = n // HA, n % HA
                if h == 0 and i:
                    pe.wait_ge(s_on, i)
                for r, tiles in enumerate(rounds(i)):
                    pe.wait_ge(*turned(ROUND0[n] + r))
                    for kt in tiles:
                        o = ps[DA * (h % 2):DA * (h % 2) + DA, 5, 128 * (h // 2):128 * (h // 2) + 128]
                        ins = mm(o, vN[0:ROWS[kt], kt, DA * h:DA * h + DA], pT[0:ROWS[kt], n % 2, kt, :],
                                 start=kt == 0, stop=kt == i + 1)
                ins.then_inc(s_o, 1)

            for n in range(HA * NB + 3):
                if n < HA * NB:
                    dots(n)
                if 2 <= n < HA * NB + 2:
                    turn_p(n - 2)
                if n >= 3:
                    weigh(n - 3)
                t = (n - SQ0 - 2) // 3
                if n >= SQ0 + 2 and (n - SQ0 - 2) % 3 == 0 and t < NT:
                    pe.wait_ge(s_sqk, t + 1)
                    for j in range(8):
                        ins = mm(ps[0:ROWS[t], 2, 8 * t + j:8 * t + j + 1], sqk[:, 128 * j:128 * j + ROWS[t]],
                                 ones[:, 0:1], start=True, stop=True)
                    ins.then_inc(s_ssq, 1)

            pe.wait_ge(s_on, NB)
            pe.wait_ge(s_gd, G_ALL)

            def col(b, h, w=128):
                return ps[:, b, 128 * h:128 * h + w]

            for t, stage in ORDER:
                n, s_, r_, u = ROWS[t], t % 2, t % 4, t - 1
                cols = slice(3 + OFF[t], 3 + OFF[t] + n)
                b0, b1 = 2 * s_, 2 * s_ + 1
                if stage == "nat":
                    if t >= 2:
                        pe.wait_ge(g_act, AC(t - 2, "w"))
                    for b, g in ((b0, 1), (b1, 2)):
                        for h in range(HG):
                            ins = turn(ps[0:n, b, 128 * h:128 * h + 128], conv4[:, g, h, cols], ident)
                        ins.then_inc(g_pe, 1)
                elif stage == "rb":
                    for b, rv, name in ((b0, rv1, "kdec"), (b1, rv2, "bv")):
                        pe.wait_ge(g_dve, DV(t, name))
                        for h in range(HG):
                            ins = mm(col(b, h, n), rv[0:n, t, h:h + 1].broadcast_to([n, 128]), ident[0:n, 0:n],
                                     start=True, stop=True)
                    ins.then_inc(g_pe, 1)
                elif stage == "kk":
                    pe.wait_ge(g_dve, DV(t, "gq"))
                    if t:
                        pe.wait_ge(g_act, AC(t, "eq"))
                    for h in range(HG):
                        o = pf[0:n, 512 * b0 + 256 * h:512 * b0 + 256 * h + 256]
                        ins = mm(o.rearrange("p (g t) -> p g t", g=2)[:, :, 0:n], conv4[:, 1, h, cols],
                                 conv4[:, 0:2, h, cols], start=True, stop=True)
                    ins.then_inc(g_pe, 1)
                elif stage[0] == "x":
                    l = int(stage[1:])
                    k = levels(t).index(l)
                    pe.wait_ge(g_pool, PO(t, f"m{l}"))
                    pe.wait_ge(g_dve, DV(t, {2: "ttc1", 32: "tf16", 64: "ttf32"}.get(l, f"tc{l // 2}")))
                    for h in range(HG):
                        if l <= 16:
                            ins = mm(ps[:, b0, 32 * h:32 * h + 32], ATm[k % 2][s_][:, h, :], Tc[s_][:, h, :],
                                     start=True, stop=True)
                        else:
                            ins = mm(col(b0, h), ATm[k % 2][s_][:, h, :], Tf[s_][:, h, :], start=True, stop=True)
                    ins.then_inc(g_pe, 1)
                elif stage[0] == "y" and stage != "yt":
                    l = int(stage[1:])
                    pe.wait_ge(g_act, AC(t, f"x{l}"))
                    pe.wait_ge(g_dve, DV(t, f"ttf{l // 2}"))
                    for h in range(HG):
                        if l <= 16:
                            ins = mm(ps[:, b1, 32 * h:32 * h + 32], TTf[r_][:, h, :], Xc[s_][:, h, :],
                                     start=True, stop=True)
                        else:
                            if l == 32:
                                mm(col(b1, h), TTf[r_][:, h, :], Xf[s_][:, h, :], start=True, stop=True)
                            ins = mm(col(b0 if l == 32 else b1, h), Xf[s_][:, h, :], TTf[r_][:, h, :],
                                     start=True, stop=True)
                    ins.then_inc(g_pe, 1)
                elif stage == "w":
                    pe.wait_ge(g_dve, DV(t, f"ttf{levels(t)[-1]}"))
                    for h in range(HG):
                        ins = mm(col(b0, h, n), kbe[s_][0:n, h, :], TTf[r_][0:n, h, 0:n], start=True, stop=True)
                    ins.then_inc(g_pe, 1)
                elif stage == "v":
                    pe.wait_ge(g_act, AC(t, "w"))
                    if t:
                        pe.wait_ge(g_dve, DV(t - 1, "s"))
                    for h in range(HG):
                        o = ps[0:n, 4, 128 * h:128 * h + 128]
                        ins = mm(o, TTf[r_][0:n, h, 0:n], bv[r_][0:n, h, :], start=True, stop=t == 0)
                        if t:
                            ins = mm(o, wT[r_][:, h, :], S[:, h, :], start=False, stop=True)
                    ins.then_inc(g_pe, 1)
                elif stage == "os":
                    pe.wait_ge(g_dve, DV(t, "vnew"))
                    if t:
                        pe.wait_ge(g_pool, PO(t, "qd"))
                        if t > 1:
                            pe.wait_ge(g_dve, DV(t - 1, "y"))
                        for h in range(HG):
                            mm(col(5, h), qd[r_][:, h, :], S[:, h, :], start=True, stop=False)
                            ins = mm(col(5, h), aq[r_][:, h, :], vnew[:, h, :], start=False, stop=True)
                        ins.then_inc(g_pe, 1)
                    for h in range(HG):
                        ins = mm(col(4, h), kdec[r_][0:n, h, :], vnew[0:n, h, :], start=True, stop=True)
                    ins.then_inc(g_pe, 1)
                elif stage == "yt":
                    pe.wait_ge(g_dve, DV(t, "y"))
                    if t > 1:
                        pe.wait_ge(g_dve, DV(t - 1, "out"))
                    for j in range(4):
                        ins = turn(ps[:, 7, 128 * j:128 * j + 128], ygdn[:, u % 2, 128 * j:128 * j + 128], ident)
                    ins.then_inc(g_pe, 1)
                elif stage[0] == "o":
                    if stage == "o0":
                        if t == 1:
                            pe.wait_ge(s_w[0], 16 * (2 * KD + 3))
                            pe.wait_ge(s_w[1], 16 * 4)
                        pe.wait_ge(s_yc[u % 2], 16 * (u // 2 + 1))
                        if t > 1:
                            pe.wait_ge(g_dve, DV(t - 1, "out"))
                    if stage == "o1":
                        pe.wait_ge(g_dve, DV(t, "yt"))
                    q = int(stage[1])
                    for k in range(4 * (q % 2), 4 * (q % 2) + 4):
                        y = yA[:, u % 2, k, :] if k < 4 else yT[:, k - 4, :]
                        ins = mm(ps[:, 6 + q // 2, :], y, wslot[:, q // 2, k, :], start=k == 0, stop=k == 7)
                    if q == 3:
                        ins.then_inc(g_pe, 1)


_INS = ["x", "meta_tokens", "rel_bias_table", "norm_gain", "w_in", "cq_norm_gain", "ckv_norm_gain", "w_uq", "w_ukv",
        "w_q_idx", "q_norm_gain", "k_norm_gain", "conv_w", "a_log", "dt_bias", "gdn_norm_gain", "w_out", "onehot"]


def kernel(**inputs):
    import concourse.bacc as bacc
    from concourse.bass_utils import run_bass_kernel_spmd

    inputs = dict(inputs, onehot=rel_onehot())
    nc = bacc.Bacc("TRN2", target_bir_lowering=False, num_devices=1)
    arrays, args = {}, []
    for name in _INS:
        arr = np.ascontiguousarray(inputs[name])
        arrays[f"in_{name}"] = arr
        args.append(nc.dram_tensor(f"in_{name}", arr.shape, mybir.dt.from_np(arr.dtype), kind="ExternalInput").ap())
    y = nc.dram_tensor("y", (1, SEQ, D), F32, kind="ExternalOutput").ap()
    hybrid(nc, *args, y)
    r = run_bass_kernel_spmd(nc, [arrays], core_ids=[0])
    return r.results[0]["y"]
```
